# Optimizing a Trainium2 kernel written in Bass

```python
import math
import jax, jax.numpy as jnp
from jax import lax
import numpy as np
import jax
import jax.numpy as jnp

D_MODEL = 1024
BATCH = 1
SEQ = 256
DEPTH = 2

CHUNK = 64
Q_BLOCK = 128
HEAD_DIM = 64
N_HEADS_TOTAL = D_MODEL // HEAD_DIM
N_HEADS_B = N_HEADS_TOTAL // 4
N_HEADS_A = (N_HEADS_TOTAL - N_HEADS_B) // 2
N_HEADS_C = N_HEADS_TOTAL - N_HEADS_A - N_HEADS_B
DIFF_QK_DIM = HEAD_DIM // 2
DIFF_V_DIM = HEAD_DIM
WIDTH_A = N_HEADS_A * HEAD_DIM
WIDTH_B = N_HEADS_B * DIFF_V_DIM
WIDTH_C = N_HEADS_C * HEAD_DIM
B_QK_WIDTH = N_HEADS_B * 2 * DIFF_QK_DIM
D_MIX = WIDTH_A + WIDTH_B + WIDTH_C
IN_COLS = 3 * WIDTH_A + 2 * B_QK_WIDTH + WIDTH_B + 3 * WIDTH_C
LEFT_CHUNKS = 8
BAND = (LEFT_CHUNKS + 1) * CHUNK
REL_CLIP = 128
D_FF = 2816
NORM_EPS = 1e-6
NEG_INF = -1e30
FFN_RESIDUAL_WEIGHT = 0.5


def rmsnorm(x, g):
    xf = x.astype(jnp.float32)
    y = xf * lax.rsqrt(jnp.mean(xf * xf, axis=-1, keepdims=True) + NORM_EPS)
    return (y * g.astype(jnp.float32)).astype(x.dtype)

def swiglu(x, w_gate, w_up, w_down):
    return (jax.nn.silu(x @ w_gate) * (x @ w_up)) @ w_down

def chunk_band_attention(q, k, v, rel_bias):
    b, s, h, d = q.shape
    nc = s // CHUNK
    qc = q.reshape(b, nc, CHUNK, h, d)
    pad = ((0, 0), (LEFT_CHUNKS, 0), (0, 0), (0, 0), (0, 0))
    kp = jnp.pad(k.reshape(b, nc, CHUNK, h, d), pad)
    vp = jnp.pad(v.reshape(b, nc, CHUNK, h, d), pad)
    kband = jnp.concatenate([kp[:, w:w + nc] for w in range(LEFT_CHUNKS + 1)], axis=2)
    vband = jnp.concatenate([vp[:, w:w + nc] for w in range(LEFT_CHUNKS + 1)], axis=2)
    qi = jnp.arange(CHUNK)
    kk = jnp.arange(BAND)
    rel = jnp.clip(qi[:, None] + LEFT_CHUNKS * CHUNK - kk[None, :], -REL_CLIP, REL_CLIP) + REL_CLIP
    bias = rel_bias[:, rel].astype(jnp.float32)
    valid = (jnp.arange(nc)[:, None] - LEFT_CHUNKS + kk[None, :] // CHUNK) >= 0
    scores = jnp.einsum('bnqhd,bnkhd->bnhqk', qc, kband).astype(jnp.float32) * (d ** -0.5)
    scores = scores + bias[None, None]
    scores = jnp.where(valid[None, :, None, None, :], scores, NEG_INF)
    p = jax.nn.softmax(scores, axis=-1).astype(v.dtype)
    o = jnp.einsum('bnhqk,bnkhd->bnqhd', p, vband)
    return o.reshape(b, s, h, d)

def diff_attention(q, k, v, lam, subln_g, lambda_init):
    b, s, h, _, dq = q.shape
    scale = dq ** -0.5
    slopes = jnp.exp2(-8.0 * jnp.arange(1, h + 1, dtype=jnp.float32) / h)
    outs = []
    for blk in range(s // Q_BLOCK):
        q0 = blk * Q_BLOCK
        kend = q0 + Q_BLOCK
        tpos = q0 + jnp.arange(Q_BLOCK)
        spos = jnp.arange(kend)
        allowed = (spos[None, :] // CHUNK) <= (tpos[:, None] // CHUNK)
        dist = jnp.abs(tpos[:, None] - spos[None, :]).astype(jnp.float32)
        alibi = -slopes[:, None, None] * dist[None]
        sc = jnp.einsum('bqhmd,bkhmd->bhmqk', q[:, q0:kend], k[:, :kend]).astype(jnp.float32) * scale
        sc = sc + alibi[None, :, None]
        sc = jnp.where(allowed[None, None, None], sc, NEG_INF)
        p = jax.nn.softmax(sc, axis=-1)
        w = p[:, :, 0] - lam * p[:, :, 1]
        outs.append(jnp.einsum('bhqk,bkhd->bqhd', w.astype(v.dtype), v[:, :kend]))
    o = jnp.concatenate(outs, axis=1)
    return rmsnorm(o, subln_g) * (1.0 - lambda_init)

def stick_breaking_attention(q, k, v):
    b, s, h, d = q.shape
    scale = d ** -0.5
    outs = []
    for blk in range(s // Q_BLOCK):
        q0 = blk * Q_BLOCK
        kend = q0 + Q_BLOCK
        tpos = q0 + jnp.arange(Q_BLOCK)
        spos = jnp.arange(kend)
        strict = spos[None, :] < tpos[:, None]
        z = jnp.einsum('bqhd,bkhd->bhqk', q[:, q0:kend], k[:, :kend]).astype(jnp.float32) * scale
        log_beta = jax.nn.log_sigmoid(z)
        log_one_minus = jnp.where(strict, jax.nn.log_sigmoid(-z), 0.0)
        suffix = lax.cumsum(log_one_minus, axis=3, reverse=True) - log_one_minus
        a = jnp.where(strict, jnp.exp(log_beta + suffix), 0.0)
        outs.append(jnp.einsum('bhqk,bkhd->bqhd', a.astype(v.dtype), v[:, :kend]))
    return jnp.concatenate(outs, axis=1)

def token_mixing(h, w_in, rel_bias, lq1, lk1, lq2, lk2, subln_g, w_out, lambda_init):
    b, s, _ = h.shape
    proj = h @ w_in
    sizes = [WIDTH_A, WIDTH_A, WIDTH_A, B_QK_WIDTH, B_QK_WIDTH, WIDTH_B, WIDTH_C, WIDTH_C, WIDTH_C]
    qa, ka, va, qb, kb, vb, qc, kc, vc = jnp.split(proj, [int(c) for c in np.cumsum(sizes)[:-1]], axis=-1)
    hd_a = (b, s, N_HEADS_A, HEAD_DIM)
    o_a = chunk_band_attention(qa.reshape(hd_a), ka.reshape(hd_a), va.reshape(hd_a), rel_bias)
    lam = (jnp.exp(jnp.sum(lq1.astype(jnp.float32) * lk1.astype(jnp.float32)))
           - jnp.exp(jnp.sum(lq2.astype(jnp.float32) * lk2.astype(jnp.float32))) + lambda_init)
    hd_bqk = (b, s, N_HEADS_B, 2, DIFF_QK_DIM)
    o_b = diff_attention(qb.reshape(hd_bqk), kb.reshape(hd_bqk), vb.reshape(b, s, N_HEADS_B, DIFF_V_DIM),
                         lam, subln_g, lambda_init)
    hd_c = (b, s, N_HEADS_C, HEAD_DIM)
    o_c = stick_breaking_attention(qc.reshape(hd_c), kc.reshape(hd_c), vc.reshape(hd_c))
    y = jnp.concatenate([o_a.reshape(b, s, WIDTH_A), o_b.reshape(b, s, WIDTH_B),
                         o_c.reshape(b, s, WIDTH_C)], axis=-1)
    return y @ w_out

def first_inputs(seed: int = 0) -> dict:
    key = jax.random.key(seed)
    ks = jax.random.split(key, 32)
    f32 = jnp.float32

    def nrm(k, shape, scale):
        return jax.random.normal(k, shape, f32) * scale

    def gain(k, shape):
        return 1.0 + 0.05 * jax.random.normal(k, shape, f32)

    L = DEPTH
    return {
        "x": jax.random.normal(ks[0], (BATCH, SEQ, D_MODEL), f32),
        "ffn1_pre_g": gain(ks[1], (L, D_MODEL)),
        "ffn1_w_gate": nrm(ks[2], (L, D_MODEL, D_FF), D_MODEL ** -0.5),
        "ffn1_w_up": nrm(ks[3], (L, D_MODEL, D_FF), D_MODEL ** -0.5),
        "ffn1_w_down": nrm(ks[4], (L, D_FF, D_MODEL), D_FF ** -0.5),
        "ffn1_post_g": gain(ks[5], (L, D_MODEL)),
        "mix_pre_g": gain(ks[6], (L, D_MODEL)),
        "w_in": nrm(ks[7], (L, D_MODEL, IN_COLS), D_MODEL ** -0.5),
        "rel_bias": nrm(ks[8], (L, N_HEADS_A, 2 * REL_CLIP + 1), 0.2),
        "diff_lambda_q1": nrm(ks[9], (L, DIFF_QK_DIM), 0.1),
        "diff_lambda_k1": nrm(ks[10], (L, DIFF_QK_DIM), 0.1),
        "diff_lambda_q2": nrm(ks[11], (L, DIFF_QK_DIM), 0.1),
        "diff_lambda_k2": nrm(ks[12], (L, DIFF_QK_DIM), 0.1),
        "diff_subln_g": gain(ks[13], (L, DIFF_V_DIM)),
        "w_out": nrm(ks[14], (L, D_MIX, D_MODEL), D_MIX ** -0.5),
        "mix_post_g": gain(ks[15], (L, D_MODEL)),
        "ffn2_pre_g": gain(ks[16], (L, D_MODEL)),
        "ffn2_w_gate": nrm(ks[17], (L, D_MODEL, D_FF), D_MODEL ** -0.5),
        "ffn2_w_up": nrm(ks[18], (L, D_MODEL, D_FF), D_MODEL ** -0.5),
        "ffn2_w_down": nrm(ks[19], (L, D_FF, D_MODEL), D_FF ** -0.5),
        "ffn2_post_g": gain(ks[20], (L, D_MODEL)),
    }

def first_block(x, ffn1_pre_g, ffn1_w_gate, ffn1_w_up, ffn1_w_down, ffn1_post_g,
              mix_pre_g, w_in, rel_bias, diff_lambda_q1, diff_lambda_k1, diff_lambda_q2,
              diff_lambda_k2, diff_subln_g, w_out, mix_post_g,
              ffn2_pre_g, ffn2_w_gate, ffn2_w_up, ffn2_w_down, ffn2_post_g):
    for l in range(DEPTH):
        lambda_init = 0.8 - 0.6 * math.exp(-0.3 * l)
        f = swiglu(rmsnorm(x, ffn1_pre_g[l]), ffn1_w_gate[l], ffn1_w_up[l], ffn1_w_down[l])
        x = x + FFN_RESIDUAL_WEIGHT * rmsnorm(f, ffn1_post_g[l])
        m = token_mixing(rmsnorm(x, mix_pre_g[l]), w_in[l], rel_bias[l],
                         diff_lambda_q1[l], diff_lambda_k1[l], diff_lambda_q2[l], diff_lambda_k2[l],
                         diff_subln_g[l], w_out[l], lambda_init)
        x = x + rmsnorm(m, mix_post_g[l])
        f = swiglu(rmsnorm(x, ffn2_pre_g[l]), ffn2_w_gate[l], ffn2_w_up[l], ffn2_w_down[l])
        x = x + FFN_RESIDUAL_WEIGHT * rmsnorm(f, ffn2_post_g[l])
    return x


MEM_LEN = 256

NSA_HEADS = 8
NSA_GROUPS = 2
NSA_HEAD_DIM = 64
CMP_BLOCK = 32
CMP_STRIDE = 16
CMP_HIDDEN = 4 * NSA_HEAD_DIM
SEL_BLOCK = 64
N_SEL = 16
WINDOW = 512
NSA_QBLOCK = 64
FORCE_SCORE = 1e4

GLA_HEADS = 4
GLA_HEAD_DK = 64
GLA_HEAD_DV = 128
GLA_RANK = 16
GLA_TAU = 16.0
GLA_CHUNK = 64

MEM_HEADS = 4
MEM_HEAD_DIM = 128

N_BRANCH = 3
BRANCH_WIDTH = NSA_HEADS * NSA_HEAD_DIM
MLP_HIDDEN = 4 * D_MODEL
ROPE_THETA = 500000.0
ROPE_FRACTION = 4

IN_SIZES = (
    NSA_HEADS * NSA_HEAD_DIM,
    NSA_GROUPS * NSA_HEAD_DIM,
    NSA_GROUPS * NSA_HEAD_DIM,
    NSA_GROUPS * NSA_HEAD_DIM,
    NSA_GROUPS * NSA_HEAD_DIM,
    NSA_GROUPS * NSA_HEAD_DIM,
    NSA_GROUPS * NSA_HEAD_DIM,
    NSA_HEADS * 3,
    GLA_HEADS * GLA_HEAD_DK,
    GLA_HEADS * GLA_HEAD_DK,
    GLA_HEADS * GLA_HEAD_DV,
    GLA_HEADS * GLA_HEAD_DV,
    GLA_RANK,
    MEM_HEADS * MEM_HEAD_DIM,
    N_BRANCH * D_MODEL,
)
D_IN = sum(IN_SIZES)


def rms_norm(x, g):
    xf = x.astype(jnp.float32)
    y = xf * lax.rsqrt(jnp.mean(xf * xf, axis=-1, keepdims=True) + NORM_EPS)
    return (y * g.astype(jnp.float32)).astype(x.dtype)

def split_heads(t, n):
    B, S, _ = t.shape
    return t.reshape(B, S, n, -1).transpose(0, 2, 1, 3)

def partial_rope(x, pos):
    rot = x.shape[-1] // ROPE_FRACTION
    half = rot // 2
    inv_freq = jnp.power(ROPE_THETA, -jnp.arange(half, dtype=jnp.float32) / half)
    ang = pos.astype(jnp.float32)[:, None, :, None] * inv_freq
    cos, sin = jnp.cos(ang), jnp.sin(ang)
    xf = x.astype(jnp.float32)
    x1, x2, rest = xf[..., :half], xf[..., half:rot], xf[..., rot:]
    out = jnp.concatenate([x1 * cos - x2 * sin, x2 * cos + x1 * sin, rest], axis=-1)
    return out.astype(x.dtype)

def masked_softmax(s, mask):
    s = jnp.where(mask, s.astype(jnp.float32), -jnp.inf)
    m = jnp.max(s, axis=-1, keepdims=True)
    m = jnp.where(jnp.isfinite(m), m, 0.0)
    p = jnp.exp(s - m)
    d = jnp.sum(p, axis=-1, keepdims=True)
    return p / jnp.where(d > 0, d, 1.0)

def nsa_attention(q, k_c, v_c, k_s, v_s, k_w, v_w, gate_logits, positions,
                  q_norm, k_norm, cmp_pe, cmp_w1, cmp_w2):
    B, S, _ = q.shape
    H, G, dh, QB = NSA_HEADS, NSA_GROUPS, NSA_HEAD_DIM, NSA_QBLOCK
    R = H // G
    q = partial_rope(rms_norm(split_heads(q, H), q_norm), positions) * (dh ** -0.5)
    k_s = partial_rope(rms_norm(split_heads(k_s, G), k_norm[1]), positions)
    k_w = partial_rope(rms_norm(split_heads(k_w, G), k_norm[2]), positions)
    v_s = split_heads(v_s, G)
    v_w = split_heads(v_w, G)

    n_cmp = (S - CMP_BLOCK) // CMP_STRIDE + 1
    cmp_idx = np.arange(n_cmp)[:, None] * CMP_STRIDE + np.arange(CMP_BLOCK)[None, :]
    cmp_end_np = cmp_idx[:, -1]
    raw = jnp.stack([split_heads(k_c, G), split_heads(v_c, G)])[:, :, :, cmp_idx]
    raw = (raw + cmp_pe[:, None, None, None]).reshape(2, B, G, n_cmp, CMP_BLOCK * dh)
    hid = jax.nn.gelu(jnp.einsum('kbgnf,kfe->kbgne', raw, cmp_w1))
    comp = jnp.einsum('kbgne,ked->kbgnd', hid, cmp_w2)
    k_cmp = partial_rope(rms_norm(comp[0], k_norm[0]), positions[:, cmp_end_np])
    v_cmp = comp[1]
    cmp_end = jnp.asarray(cmp_end_np, jnp.int32)

    n_blk = S // SEL_BLOCK
    c_start = np.arange(n_cmp) * CMP_STRIDE
    b_start = np.arange(n_blk) * SEL_BLOCK
    overlap = jnp.asarray(((c_start[:, None] < b_start[None, :] + SEL_BLOCK)
                           & (b_start[None, :] < c_start[:, None] + CMP_BLOCK)).astype(np.float32))
    n_sel = min(N_SEL, n_blk)
    ks_blk = k_s.reshape(B, G, n_blk, SEL_BLOCK, dh)
    vs_blk = v_s.reshape(B, G, n_blk, SEL_BLOCK, dh)
    kw_pad = jnp.pad(k_w, ((0, 0), (0, 0), (WINDOW, 0), (0, 0)))
    vw_pad = jnp.pad(v_w, ((0, 0), (0, 0), (WINDOW, 0), (0, 0)))

    n_qb = S // QB
    q_blocks = q.reshape(B, H, n_qb, QB, dh).transpose(2, 0, 1, 3, 4).reshape(n_qb, B, G, R, QB, dh)
    gates = jax.nn.sigmoid(gate_logits.astype(jnp.float32)).astype(q.dtype)
    g_blocks = (gates.reshape(B, S, H, 3).transpose(0, 2, 1, 3)
                .reshape(B, H, n_qb, QB, 3).transpose(2, 0, 1, 3, 4).reshape(n_qb, B, G, R, QB, 3))
    gather_blocks = jax.vmap(jax.vmap(lambda blk, ix: blk[ix]))
    blk_ids = jnp.arange(n_blk)

    def query_block(args):
        qi, qb, gb = args
        t = qi * QB + jnp.arange(QB)
        s_c = jnp.einsum('bgrqd,bgnd->bgrqn', qb, k_cmp)
        p_c = masked_softmax(s_c, cmp_end[None, :] <= t[:, None])
        o_c = jnp.einsum('bgrqn,bgnd->bgrqd', p_c.astype(v_cmp.dtype), v_cmp)
        imp = jnp.einsum('bgqn,nj->bgqj', jnp.sum(p_c, axis=2), overlap)
        causal = (blk_ids * SEL_BLOCK)[None, :] <= t[:, None]
        cur = (t // SEL_BLOCK)[:, None]
        forced = causal & ((blk_ids[None, :] == 0) | (blk_ids[None, :] == cur)
                           | (blk_ids[None, :] == cur - 1))
        score = jnp.where(forced, FORCE_SCORE, jnp.where(causal, imp, -FORCE_SCORE))
        _, idx = lax.top_k(score, n_sel)
        k_g = gather_blocks(ks_blk, idx)
        v_g = gather_blocks(vs_blk, idx)
        kpos = idx[..., None] * SEL_BLOCK + jnp.arange(SEL_BLOCK)
        mask_s = (kpos <= t[:, None, None])[:, :, None].reshape(B, G, 1, QB, n_sel * SEL_BLOCK)
        s_s = jnp.einsum('bgrqd,bgqnld->bgrqnl', qb, k_g).reshape(B, G, R, QB, n_sel * SEL_BLOCK)
        p_s = masked_softmax(s_s, mask_s).reshape(B, G, R, QB, n_sel, SEL_BLOCK)
        o_s = jnp.einsum('bgrqnl,bgqnld->bgrqd', p_s.astype(v_g.dtype), v_g)
        kwb = lax.dynamic_slice_in_dim(kw_pad, qi * QB, WINDOW + QB, axis=2)
        vwb = lax.dynamic_slice_in_dim(vw_pad, qi * QB, WINDOW + QB, axis=2)
        kp = qi * QB - WINDOW + jnp.arange(WINDOW + QB)
        mask_w = ((kp[None, :] <= t[:, None]) & (kp[None, :] > t[:, None] - WINDOW)
                  & (kp[None, :] >= 0))
        p_w = masked_softmax(jnp.einsum('bgrqd,bgkd->bgrqk', qb, kwb), mask_w)
        o_w = jnp.einsum('bgrqk,bgkd->bgrqd', p_w.astype(vwb.dtype), vwb)
        return gb[..., 0:1] * o_c + gb[..., 1:2] * o_s + gb[..., 2:3] * o_w

    out = lax.map(query_block, (jnp.arange(n_qb), q_blocks, g_blocks))
    return out.reshape(n_qb, B, H, QB, dh).transpose(1, 0, 3, 2, 4).reshape(B, S, H * dh)

def gated_linear_attention(q, k, v, r, g_low, w_gate, b_gate, norm_g):
    B, S, _ = q.shape
    H, C = GLA_HEADS, GLA_CHUNK
    n_c = S // C
    log_a = jax.nn.log_sigmoid((g_low @ w_gate + b_gate).astype(jnp.float32)) / GLA_TAU

    def chunks(t):
        return t.astype(jnp.float32).reshape(B, n_c, C, H, -1).transpose(1, 0, 3, 2, 4)

    qc = chunks(q) * (GLA_HEAD_DK ** -0.5)
    kc, vc, ac = chunks(k), chunks(v), chunks(log_a)
    tril = jnp.tril(jnp.ones((C, C), dtype=bool))

    def step(state, xs):
        qb, kb, vb, ab = xs
        b = jnp.cumsum(ab, axis=2)
        decay = jnp.exp(jnp.where(tril[:, :, None], b[:, :, :, None, :] - b[:, :, None, :, :], -jnp.inf))
        attn = jnp.einsum('bhid,bhjd,bhijd->bhij', qb, kb, decay)
        o = attn @ vb + jnp.einsum('bhid,bhdv->bhiv', qb * jnp.exp(b), state)
        b_last = b[:, :, -1:, :]
        state = (jnp.exp(b_last)[:, :, 0, :, None] * state
                 + jnp.einsum('bhjd,bhjv->bhdv', kb * jnp.exp(b_last - b), vb))
        return state, o

    state0 = jnp.zeros((B, H, GLA_HEAD_DK, GLA_HEAD_DV), jnp.float32)
    _, o = lax.scan(step, state0, (qc, kc, vc, ac))
    o = o.transpose(1, 0, 3, 2, 4).reshape(B, S, H, GLA_HEAD_DV)
    o = rms_norm(o, norm_g).reshape(B, S, H * GLA_HEAD_DV)
    return (o * jax.nn.silu(r.astype(jnp.float32))).astype(q.dtype)

def memory_attention(q, mem, mem_norm, w_kv, q_norm, k_norm):
    B, S, _ = q.shape
    H, dh = MEM_HEADS, MEM_HEAD_DIM
    k, v = jnp.split(rms_norm(mem, mem_norm) @ w_kv, 2, axis=-1)
    q = rms_norm(split_heads(q, H), q_norm) * (dh ** -0.5)
    k = rms_norm(split_heads(k, H), k_norm)
    v = split_heads(v, H)
    p = jax.nn.softmax(jnp.einsum('bhsd,bhmd->bhsm', q, k).astype(jnp.float32), axis=-1)
    o = jnp.einsum('bhsm,bhmd->bhsd', p.astype(v.dtype), v)
    return o.transpose(0, 2, 1, 3).reshape(B, S, H * dh)

def hybrid_layer(x, mem, positions, ln_mix, w_in, b_merge, nsa_q_norm, nsa_k_norm,
                 cmp_pe, cmp_w1, cmp_w2, gla_w_gate, gla_b_gate, gla_norm,
                 mem_norm, mem_w_kv, mem_q_norm, mem_k_norm, w_branch, w_out,
                 ln_mlp, w_up, w_down):
    B, S, D = x.shape
    h = rms_norm(x, ln_mix)
    z = h @ w_in
    offsets = np.cumsum(IN_SIZES)[:-1].tolist()
    (n_q, n_kc, n_vc, n_ks, n_vs, n_kw, n_vw, n_g,
     g_q, g_k, g_v, g_r, g_low, m_q, merge) = jnp.split(z, offsets, axis=-1)
    o_nsa = nsa_attention(n_q, n_kc, n_vc, n_ks, n_vs, n_kw, n_vw, n_g, positions,
                          nsa_q_norm, nsa_k_norm, cmp_pe, cmp_w1, cmp_w2)
    o_gla = gated_linear_attention(g_q, g_k, g_v, g_r, g_low, gla_w_gate, gla_b_gate, gla_norm)
    o_mem = memory_attention(m_q, mem, mem_norm, mem_w_kv, mem_q_norm, mem_k_norm)
    gates = jax.nn.sigmoid((merge.reshape(B, S, N_BRANCH, D) + b_merge).astype(jnp.float32)).astype(x.dtype)
    merged = (gates[:, :, 0] * (o_nsa @ w_branch[0])
              + gates[:, :, 1] * (o_gla @ w_branch[1])
              + gates[:, :, 2] * (o_mem @ w_branch[2]))
    x = x + merged @ w_out
    h = rms_norm(x, ln_mlp)
    return x + jnp.square(jax.nn.relu(h @ w_up)) @ w_down

def second_inputs(seed: int = 0) -> dict:
    key = jax.random.key(seed)
    ks = jax.random.split(key, 24)
    f32 = jnp.float32
    dh = NSA_HEAD_DIM
    resid = (2 * DEPTH) ** -0.5

    def nrm(k, shape, scale):
        return jax.random.normal(k, shape, f32) * scale

    def gain(k, shape):
        return 1.0 + 0.02 * jax.random.normal(k, shape, f32)

    positions = (jnp.arange(SEQ, dtype=jnp.int32)[None, :]
                 + jax.random.randint(ks[2], (BATCH, 1), 0, SEQ, dtype=jnp.int32))
    return {
        'x': nrm(ks[0], (BATCH, SEQ, D_MODEL), 1.0),
        'mem': nrm(ks[1], (BATCH, MEM_LEN, D_MODEL), 1.0),
        'positions': positions,
        'ln_mix': gain(ks[3], (DEPTH, D_MODEL)),
        'w_in': nrm(ks[4], (DEPTH, D_MODEL, D_IN), D_MODEL ** -0.5),
        'b_merge': nrm(ks[5], (DEPTH, N_BRANCH, D_MODEL), 0.02),
        'nsa_q_norm': gain(ks[6], (DEPTH, dh)),
        'nsa_k_norm': gain(ks[7], (DEPTH, 3, dh)),
        'cmp_pe': nrm(ks[8], (DEPTH, 2, CMP_BLOCK, dh), 0.02),
        'cmp_w1': nrm(ks[9], (DEPTH, 2, CMP_BLOCK * dh, CMP_HIDDEN), (CMP_BLOCK * dh) ** -0.5),
        'cmp_w2': nrm(ks[10], (DEPTH, 2, CMP_HIDDEN, dh), CMP_HIDDEN ** -0.5),
        'gla_w_gate': nrm(ks[11], (DEPTH, GLA_RANK, GLA_HEADS * GLA_HEAD_DK), GLA_RANK ** -0.5),
        'gla_b_gate': nrm(ks[12], (DEPTH, GLA_HEADS * GLA_HEAD_DK), 0.02),
        'gla_norm': gain(ks[13], (DEPTH, GLA_HEAD_DV)),
        'mem_norm': gain(ks[14], (DEPTH, D_MODEL)),
        'mem_w_kv': nrm(ks[15], (DEPTH, D_MODEL, 2 * MEM_HEADS * MEM_HEAD_DIM), D_MODEL ** -0.5),
        'mem_q_norm': gain(ks[16], (DEPTH, MEM_HEAD_DIM)),
        'mem_k_norm': gain(ks[17], (DEPTH, MEM_HEAD_DIM)),
        'w_branch': nrm(ks[18], (DEPTH, N_BRANCH, BRANCH_WIDTH, D_MODEL), BRANCH_WIDTH ** -0.5),
        'w_out': nrm(ks[19], (DEPTH, D_MODEL, D_MODEL), D_MODEL ** -0.5 * resid),
        'ln_mlp': gain(ks[20], (DEPTH, D_MODEL)),
        'w_up': nrm(ks[21], (DEPTH, D_MODEL, MLP_HIDDEN), D_MODEL ** -0.5),
        'w_down': nrm(ks[22], (DEPTH, MLP_HIDDEN, D_MODEL), MLP_HIDDEN ** -0.5 * resid),
    }

def second_block(x, mem, positions, ln_mix, w_in, b_merge, nsa_q_norm, nsa_k_norm,
              cmp_pe, cmp_w1, cmp_w2, gla_w_gate, gla_b_gate, gla_norm,
              mem_norm, mem_w_kv, mem_q_norm, mem_k_norm, w_branch, w_out,
              ln_mlp, w_up, w_down):
    for l in range(DEPTH):
        x = hybrid_layer(x, mem, positions, ln_mix[l], w_in[l], b_merge[l],
                         nsa_q_norm[l], nsa_k_norm[l], cmp_pe[l], cmp_w1[l], cmp_w2[l],
                         gla_w_gate[l], gla_b_gate[l], gla_norm[l],
                         mem_norm[l], mem_w_kv[l], mem_q_norm[l], mem_k_norm[l],
                         w_branch[l], w_out[l], ln_mlp[l], w_up[l], w_down[l])
    return x


def setup_inputs(seed=0):
    out = dict(first_inputs(seed))
    for name, value in second_inputs(seed + 1).items():
        if name != "x":
            out[name + "_2"] = value
    return out


def reference(
    x, ffn1_pre_g, ffn1_w_gate, ffn1_w_up, ffn1_w_down, ffn1_post_g, mix_pre_g, w_in, rel_bias,
    diff_lambda_q1, diff_lambda_k1, diff_lambda_q2, diff_lambda_k2, diff_subln_g, w_out,
    mix_post_g, ffn2_pre_g, ffn2_w_gate, ffn2_w_up, ffn2_w_down, ffn2_post_g, mem_2,
    positions_2, ln_mix_2, w_in_2, b_merge_2, nsa_q_norm_2, nsa_k_norm_2, cmp_pe_2, cmp_w1_2,
    cmp_w2_2, gla_w_gate_2, gla_b_gate_2, gla_norm_2, mem_norm_2, mem_w_kv_2, mem_q_norm_2,
    mem_k_norm_2, w_branch_2, w_out_2, ln_mlp_2, w_up_2, w_down_2,
):
    x = first_block(
        x, ffn1_pre_g, ffn1_w_gate, ffn1_w_up, ffn1_w_down, ffn1_post_g, mix_pre_g, w_in,
        rel_bias, diff_lambda_q1, diff_lambda_k1, diff_lambda_q2, diff_lambda_k2, diff_subln_g,
        w_out, mix_post_g, ffn2_pre_g, ffn2_w_gate, ffn2_w_up, ffn2_w_down, ffn2_post_g,
    )
    return second_block(
        x, mem_2, positions_2, ln_mix_2, w_in_2, b_merge_2, nsa_q_norm_2, nsa_k_norm_2,
        cmp_pe_2, cmp_w1_2, cmp_w2_2, gla_w_gate_2, gla_b_gate_2, gla_norm_2, mem_norm_2,
        mem_w_kv_2, mem_q_norm_2, mem_k_norm_2, w_branch_2, w_out_2, ln_mlp_2, w_up_2, w_down_2,
    )


_drawn_inputs = setup_inputs


def setup_inputs(seed=0):
    import zlib

    import numpy as np

    out = dict(_drawn_inputs(seed))
    spreads = {}
    factors = {'diff_lambda_q1': 3.687,
     'diff_lambda_k1': 8.0,
     'mem_2': 2.956,
     'ln_mix_2': 8.0,
     'b_merge_2': 8.0,
     'nsa_q_norm_2': 8.0,
     'nsa_k_norm_2': 8.0,
     'cmp_pe_2': 30.772,
     'gla_b_gate_2': 8.0,
     'gla_norm_2': 8.0,
     'mem_norm_2': 8.0,
     'mem_w_kv_2': 2.824,
     'mem_q_norm_2': 8.0,
     'mem_k_norm_2': 8.0,
     'ln_mlp_2': 5.934}
    for name, (base, spread) in spreads.items():
        noise = np.random.default_rng([zlib.crc32(name.encode()), seed]).standard_normal(out[name].shape)
        drawn = base * np.exp(spread * noise) if base else spread * noise
        out[name] = jnp.asarray(drawn.astype(out[name].dtype))
    for name, factor in factors.items():
        out[name] = (out[name] * factor).astype(out[name].dtype)
    return out
```

```python
import math
from contextlib import ExitStack

import numpy as np

import concourse.bass as bass
from concourse import mybir

F32 = mybir.dt.float32
F32R = mybir.dt.float32r
I32 = mybir.dt.int32
ALU = mybir.AluOpType
ACT = mybir.ActivationFunctionType
AX = mybir.AxisListType

P = 128
S = 256
MT = S // P
D = 1024
KD = D // P
L = 2
EPS = 1e-6
BIG = 1e30
HUGE = 3e38

PIECE = 1024
RING = 4
AHEAD = 3

D_FF = 2816
FFN_STRIPS = D_FF // 256
NA, NB, NC_ = 6, 4, 6
COLS1 = 3072
QKV_A, QKV_B, QKV_C = 768, 0, 768 + 1152
FFN_PIECES = FFN_STRIPS * 6
PIECES1 = 2 * FFN_PIECES + COLS1 // 512 * 4 + KD

MLP_STRIPS = 4096 // 512
N_CMP = 15
PIECES2 = 2 * 4 + 13 * 4 + 8 + 12 + KD + MLP_STRIPS * 8
PIECES = L * (PIECES1 + PIECES2)
STREAM = PIECES + RING
assert PIECES1 % RING == 0 and PIECES2 % RING == 0

LEVELS = (128, 64, 32, 16, 8, 4, 2, 1)


class At:

    def __init__(self, sem, value):
        self.sem, self.value = sem, value


class Queue:

    def __init__(self, engine, sem):
        self.engine, self.sem = engine, sem
        self.n, self.seen = 0, {}

    def after(self, *steps):
        for step in steps:
            if isinstance(step, At):
                self.engine.wait_ge(step.sem, step.value)
                continue
            queue, n = step
            if self.seen.get(id(queue), 0) < n:
                self.engine.wait_ge(queue.sem, n)
                self.seen[id(queue)] = n
        return self.engine

    def step(self, instruction):
        instruction.then_inc(self.sem, 1)
        self.n += 1
        return (self, self.n)

    def restart(self):
        self.n, self.seen = 0, {}


def build(nc, T):
    with ExitStack() as stack:
        build_in(nc, T, stack)


def build_in(nc, T, stack):
    def sb(name, shape, dtype=F32):
        return stack.enter_context(nc.sbuf_tensor(name, list(shape), dtype))

    def sem(name):
        return stack.enter_context(nc.semaphore(name))

    pe, dve, act, pool, sp = nc.tensor, nc.vector, nc.scalar, nc.gpsimd, nc.sync
    three = [pe.engine, act.engine, dve.engine]

    raw = sb("raw", [P, RING, PIECE])
    hi = sb("hi", [P, RING, PIECE], F32R)
    lo = sb("lo", [P, RING, PIECE], F32R)
    x = sb("x", [P, MT, D])
    h_hi = sb("h_hi", [P, KD, S], F32R)
    h_lo = sb("h_lo", [P, KD, S], F32R)
    y_hi = sb("y_hi", [P, 12, S], F32R)
    y_lo = sb("y_lo", [P, 12, S], F32R)
    big = sb("big", [P, 12904])
    memkv = sb("memkv", [P, MT, 1024])
    soft = sb("soft", [P, 2, 2, 512])
    qT = sb("qT", [P, 4, S])
    kT = sb("kT", [P, 4, S])
    consts = sb("consts", [P, 1024])
    special = sb("special", [P, 5888])
    extra = sb("extra", [P, 2048])
    small = sb("small", [P, 512])
    psum = stack.enter_context(nc.psum_tensor("psum", [P, 8, 512], F32))

    ident = consts[:, 0:128]
    tri = consts[:, 128:256]
    ones = consts[:, 256:384]
    strict = consts[:, 512:640]
    causal = consts[:, 640:896]
    cmp_table = consts[:, 896:928].rearrange("p (m n) -> p m n", m=MT)
    cmp_valid = consts[:, 928:960].rearrange("p (m n) -> p m n", m=MT)
    own_values = consts[:, 960:968]
    own_keys = consts[0:32, 968:970]
    inv_freq = consts[:, 976:984]
    f32 = lambda a: a.bitcast(F32)

    s_landed = [sem(f"s_landed{i}") for i in range(RING)]
    s_hi = sem("s_hi")
    s_lo = sem("s_lo")
    s_used = sem("s_used")
    PE, AC, VE = (Queue(e, sem(n)) for e, n in ((pe, "s_pe"), (act, "s_act"), (dve, "s_dve")))
    s_par = sem("s_par")
    s_gu = sem("s_gu")
    s_silu = sem("s_silu")
    s_prod = sem("s_prod")
    s_turn = sem("s_turn")
    s_ahi = sem("s_ahi")
    s_alo = sem("s_alo")
    s_down = sem("s_down")
    s_out = sem("s_out")
    ffn_sems = [s_gu, s_silu, s_prod, s_turn, s_ahi, s_alo, s_down]
    layer_sems = [PE.sem, AC.sem, VE.sem, s_par] + ffn_sems

    for slot in range(RING):
        sp.dma_start(raw[:, slot, :], T["stream"][slot]).then_inc(s_landed[slot], 16)
    with sp.Fori(0, STREAM // RING - 1) as turn:
        for slot in range(RING):
            sp.wait_ge(s_lo, turn * RING + slot + 1)
            sp.dma_start(raw[:, slot, :], T["stream"][(turn + 1) * RING + slot]).then_inc(s_landed[slot], 16)
    with pool.Fori(0, STREAM // RING) as turn:
        for slot in range(RING):
            pool.wait_ge(s_hi, turn * RING + slot + 1)
            pool.tensor_tensor(lo[:, slot, :], raw[:, slot, :], f32(hi[:, slot, :]),
                               ALU.subtract).then_inc(s_lo, 1)

    def round_piece(first, c):
        slot = c % RING
        act.wait_ge(s_landed[slot], first * (16 // RING) + 16 * (c // RING + 1))
        act.activation(hi[:, slot, :], raw[:, slot, :], ACT.Copy).then_inc(s_hi, 1)

    def next_piece(first, c):
        act.wait_ge(s_used, first + c + 1)
        round_piece(first, c + AHEAD)
        pe.wait_ge(s_lo, first + c + 1)
        return c % RING

    def product(out, lhs_hi, lhs_lo, rhs_hi, rhs_lo, start, stop):
        pe.matmul(out, lhs_hi, rhs_hi, start=start, stop=False)
        pe.matmul(out, lhs_hi, rhs_lo, start=False, stop=False)
        return pe.matmul(out, lhs_lo, rhs_hi, start=False, stop=stop)

    def strip(first, c, a_hi, a_lo, bank, between=None):
        for j in range(4):
            slot = next_piece(first, c + j)
            for i in range(2):
                k = 2 * j + i
                for m in range(MT):
                    w = slice(i * 512, i * 512 + 512)
                    last = product(psum[:, bank + m, :], a_hi[:, k, m * P:m * P + P], a_lo[:, k, m * P:m * P + P],
                                   hi[:, slot, w], lo[:, slot, w], k == 0, k == KD - 1)
            last.then_inc(s_used, 1)
            if between and j < 3:
                between()
        return At(s_used, first + (c + 4 + 1))

    def rows(first, c, kt, a_hi, a_lo, bank, start, stop):
        slot = next_piece(first, c)
        for m in range(MT):
            for n in range(2):
                w = slice(n * 512, n * 512 + 512)
                last = product(psum[:, bank + 2 * m + n, :], a_hi[:, kt, m * P:m * P + P],
                               a_lo[:, kt, m * P:m * P + P], hi[:, slot, w], lo[:, slot, w], start, stop)
        last.then_inc(s_used, 1)
        return At(s_used, first + (c + 1 + 1))

    def exp_and_ln():
        act.preload_act_table_set("natural_log_exp_and_others")

    def rsqrt(v, t, y, *ready):
        s = AC.step(AC.after(*ready).activation(t, v, ACT.Ln))
        s = AC.step(AC.after(s).activation(y, t, ACT.Exp, scale=-0.5))
        s = VE.step(VE.after(s, *ready).tensor_tensor(t, y, y, ALU.mult))
        s = VE.step(VE.after(s).tensor_tensor(t, t, v, ALU.mult))
        s = VE.step(VE.after(s).tensor_scalar(t, t, -0.5, 1.5, ALU.mult, ALU.add))
        return VE.step(VE.after(s).tensor_tensor(y, y, t, ALU.mult))

    small_at = [0]

    def cell(n):
        small_at[0] += n
        assert small_at[0] <= 512, small_at
        return small[:, small_at[0] - n:small_at[0]]

    def row_norms(src, scratch, *ready):
        exp_and_ln()
        ss, t, y = n_ss, n_t, n_y
        for m in range(MT):
            s = AC.step(AC.after(*ready).activation(scratch[:, m, :], src[:, m, :], ACT.Square,
                                                    accum_out=ss[:, m:m + 1]))
        s = VE.step(VE.after(s).tensor_scalar(ss, ss, 1.0 / D, EPS, ALU.mult, ALU.add))
        return y, rsqrt(ss, t, y, s)

    def to_features(src, scratch, gain, out_hi, out_lo, banks, free, *ready):
        y, s = row_norms(src, work_sq, *ready)
        done = []
        for m in range(MT):
            done.append(VE.step(VE.after(s).tensor_scalar(scratch[:, m, :], src[:, m, :], y[:, m:m + 1], None,
                                                          ALU.mult)))
        read = {}
        for pair in range(KD // 2):
            bank = banks[pair % len(banks)]
            pe_ = PE.after(*done, *free, *read.get(bank, ()))
            for i in range(2):
                for m in range(MT):
                    k = 2 * pair + i
                    t = pe_.transpose(psum[:, bank, i * S + m * P:i * S + m * P + P],
                                      scratch[:, m, k * P:k * P + P], ident)
            t = PE.step(t)
            kts = [(2 * pair + i, psum[:, bank, i * S:i * S + S]) for i in range(2)]
            for k, part in kts:
                a = AC.step(AC.after(t, *free).activation(out_hi[:, k, :], part, ACT.Copy, scale=gain[:, k:k + 1]))
            for k, part in kts:
                b = VE.step(VE.after(a).scalar_tensor_tensor(out_lo[:, k, :], part, gain[:, k:k + 1],
                                                             f32(out_hi[:, k, :]), ALU.mult, ALU.subtract))
            read[bank] = (a, b)
        return b

    def add_norm(weight, post_gain, bank, *ready):
        ss, t, y = n_ss, n_t, n_y
        exp_and_ln()
        for m in range(MT):
            f = psum[:, bank + 2 * m:bank + 2 * m + 2, :]
            s = AC.step(AC.after(*ready).activation(work_post[:, m, :], f, ACT.Square, accum_out=ss[:, m:m + 1]))
        s = VE.step(VE.after(s, *ready).tensor_scalar(ss, ss, 1.0 / D, EPS, ALU.mult, ALU.add))
        s = rsqrt(ss, t, y, s)
        if weight != 1.0:
            s = VE.step(VE.after(s).tensor_scalar(y, y, weight, None, ALU.mult))
        for m in range(MT):
            f = psum[:, bank + 2 * m:bank + 2 * m + 2, :].rearrange("p a b -> p (a b)")
            s2 = VE.step(VE.after(s).scalar_tensor_tensor(work_post[:, m, :], f, y[:, m:m + 1], post_gain,
                                                          ALU.mult, ALU.mult))
            s3 = VE.step(VE.after(s2).tensor_tensor(x[:, m, :], x[:, m, :], work_post[:, m, :], ALU.add))
        return s3

    def feed_forward(first, c, strips, gated, strips_before):
        kts = 2 if gated else 4
        width = kts * P
        pieces = 4 + kts
        per_turn = 2 if gated else 1
        act_s, prod_s = work_act[:, :, 0:width], work_prod[:, :, 0:width]

        def project(base, c, n):
            pe.wait_ge(s_prod, n + 1)
            done = strip(base, c, h_hi, h_lo, 0)
            for q in (act, dve):
                q.wait_ge(done.sem, done.value)
            if gated:
                act.wait_ge(s_prod, n + 1)
                act.activation(act_s, psum[:, 0:2, 0:width], ACT.Silu).then_inc(s_silu, 1)
                dve.wait_ge(s_silu, n + 1)
                dve.wait_ge(s_turn, n + 1)
                dve.tensor_tensor(prod_s, act_s, psum[:, 0:2, width:2 * width], ALU.mult).then_inc(s_prod, 1)
            else:
                act.wait_ge(s_prod, n + 1)
                act.activation(act_s, psum[:, 0:2, :], ACT.Relu).then_inc(s_silu, 1)
                dve.wait_ge(s_silu, n + 1)
                dve.wait_ge(s_turn, n + 1)
                dve.tensor_tensor(prod_s, act_s, act_s, ALU.mult).then_inc(s_prod, 1)

        def down(base, c, n, start, stop):
            pe.wait_ge(s_alo, n)
            for i in range(kts):
                end = rows(base, c + i, i, y_hi, y_lo, 4, start and i == 0, stop and i == kts - 1)
            return end

        def turn(base, c, n):
            pe.wait_ge(s_prod, n + 2)
            for i in range(kts):
                for m in range(MT):
                    t = pe.transpose(psum[:, 2 + i // 2, (i % 2) * S + m * P:(i % 2) * S + m * P + P],
                                     prod_s[:, m, i * P:i * P + P], ident)
            t.then_inc(s_turn, 1)
            src = psum[:, 2:2 + kts // 2, :].rearrange("p a b -> p (a b)")
            high = y_hi[:, 0:kts, :].rearrange("p a b -> p (a b)")
            low = y_lo[:, 0:kts, :].rearrange("p a b -> p (a b)")
            for q in (act, dve):
                q.wait_ge(s_turn, n + 2)
                q.wait_ge(s_used, base + (c + 1))
            act.activation(high, src, ACT.Copy).then_inc(s_ahi, 1)
            dve.wait_ge(s_ahi, n + 1)
            dve.tensor_tensor(low, src, f32(high), ALU.subtract).then_inc(s_alo, 1)

        n0 = strips_before
        project(first, c, n0)
        turn(first, c + 4, n0)
        project(first, c + 4, n0 + 1)
        down(first, c + 8, n0 + 1, True, False)
        turn(first, c + 8 + kts, n0 + 1)
        left = strips - 2
        c += 8 + kts
        whole = left // per_turn
        if whole:
            with nc.Fori(0, whole, engines=three) as i:
                base = first + i * (pieces * per_turn)
                for j in range(per_turn):
                    n = i * per_turn + (n0 + 2 + j)
                    cj = c + j * pieces
                    project(base, cj, n)
                    down(base, cj + 4, n, False, False)
                    turn(base, cj + pieces, n)
        c += whole * per_turn * pieces
        for j in range(left - whole * per_turn):
            n = n0 + 2 + whole * per_turn + j
            project(first, c, n)
            down(first, c + 4, n, False, False)
            turn(first, c + pieces, n)
            c += pieces
        end = down(first, c, n0 + strips, False, True)
        return end

    SCORE, TURNED, OUT = (4, 5), 6, 7
    score_read, prob_read, pt_read = {}, {}, {}
    bank_read = {TURNED: (), OUT: ()}

    def pipeline(units):
        states = [None] * len(units)
        for i in range(len(units) + 2):
            if 0 <= i - 2:
                units[i - 2][2]((i - 2) % 2, states[i - 2])
            if 0 <= i - 1 < len(units):
                states[i - 1] = units[i - 1][1]((i - 1) % 2, states[i - 1])
            if i < len(units):
                states[i] = units[i][0](i % 2)
            yield

    stat = [[cell(8) for _ in range(6)] for _ in range(2)]

    def softmax_parts(slot, products, ready, tables, segments, row_tiles=False):
        bank, prob = SCORE[slot], soft[:, slot, 0, :]
        mn, total, inverse = stat[slot][0:3]
        pe_ = PE.after(*ready, *score_read.get(slot, ()))
        t = None
        for lhsT, rhs, col, width in products:
            if t and row_tiles:
                PE.after(t)
            t = PE.step(pe_.matmul(psum[:, bank, col:col + width], lhsT, rhs, start=True, stop=True))
        for i, ((col, width), table) in enumerate(zip(segments, tables)):
            w = slice(col, col + width)
            a = VE.step(VE.after(t, *prob_read.get(slot, ())).tensor_tensor_reduce(
                prob[:, w], psum[:, bank, w], table, 1.0, HUGE, ALU.add, ALU.min, mn[:, i:i + 1])) \
                if table is not None else VE.step(VE.after(t, *prob_read.get(slot, ())).tensor_scalar(
                    prob[:, w], psum[:, bank, w], 0.0, HUGE, ALU.add, ALU.min, accum_out=mn[:, i:i + 1]))
            s = AC.step(AC.after(a).activation(prob[:, w], prob[:, w], ACT.Exp, scale=-1.0, bias=mn[:, i:i + 1],
                                               accum_out=total[:, i:i + 1]))
        score_read[slot] = (a,)
        return s

    def normalised(slot, s, segments, gates):
        prob = soft[:, slot, 0, :]
        total, inverse = stat[slot][1:3]
        n = len(segments)
        r = VE.step(VE.after(s).reciprocal(inverse[:, 0:n], total[:, 0:n]))
        for i, (col, width) in enumerate(segments):
            w = slice(col, col + width)
            r2 = VE.step(VE.after(r).tensor_scalar(prob[:, w], prob[:, w], inverse[:, i:i + 1],
                                                   gates[i] if gates else None, ALU.mult,
                                                   ALU.mult if gates else ALU.bypass))
        return r2

    def turn_blocks(slot, ready, cols):
        pe_ = PE.after(ready, *bank_read[TURNED])
        for i, col in enumerate(cols):
            t = pe_.transpose(psum[:, TURNED, i * P:i * P + P], soft[:, slot, 0, col:col + P], ident)
        t = PE.step(t)
        prob_read[slot] = (t,)
        n = len(cols) * P
        a = VE.step(VE.after(t, *pt_read.get(slot, ())).tensor_copy(soft[:, slot, 1, 0:n], psum[:, TURNED, 0:n]))
        bank_read[TURNED] = (a,)
        return a

    def split_out(src, high, low, t):
        a = AC.step(AC.after(t).activation(high, src, ACT.Copy))
        b = VE.step(VE.after(t, a).tensor_tensor(low, src, f32(high), ALU.subtract))
        return b

    def causal_out(slot, pt, base, v, col, start=True, stop=True):
        probs = soft[:, slot, 1, :]
        out = psum[base:base + 64, OUT, col:col + S]
        pe.matmul(out[:, 0:P], v[:, 0, :], probs[:, 0:P], start=start, stop=stop, skip_group_check=True)
        pe.matmul(out[:, P:S], v[:, 0, :], probs[:, P:2 * P], start=start, stop=False, skip_group_check=True)
        return pe.matmul(out[:, P:S], v[:, 1, :], probs[:, 2 * P:3 * P], start=False, stop=stop,
                         skip_group_check=True)

    SEG = [(0, P), (P, S)]
    BLOCKS = [0, P, 2 * P]

    def turn_qk(z, jobs, ready):
        for n, (col, target, scale) in enumerate(jobs):
            bank = SCORE[n % 2]
            pe_ = PE.after(*ready, *score_read.get(n % 2, ()))
            for m in range(MT):
                t = pe_.transpose(psum[:, bank, m * P:m * P + P], z[:, m, col:col + P], ident)
            t = PE.step(t)
            a = AC.step(AC.after(t).activation(target, psum[:, bank, 0:S], ACT.Copy, scale=scale))
            score_read[n % 2] = (a,)
        return a

    def load(target, source, s=None, **how):
        act.dma_start(target, source, **how).then_inc(s or s_par, 16)
        loads[0] += 1

    loads = [0]
    n_ss, n_t, n_y = cell(2), cell(2), cell(2)
    work_sq = big[:, 2048:4096].rearrange("p (m d) -> p m d", m=MT)
    hn = big[:, 0:2048].rearrange("p (m d) -> p m d", m=MT)
    work_act = big[:, 0:1024].rearrange("p (m d) -> p m d", m=MT)
    work_prod = big[:, 1024:2048].rearrange("p (m d) -> p m d", m=MT)
    work_post = big[:, 4096:6144].rearrange("p (m d) -> p m d", m=MT)

    s_const = sem("s_const")
    load(consts[:, :], T["consts"], s_const)
    load(x[:, :, :], T["x"].rearrange("b (m p) d -> p (b m) d", p=P), s_const)
    load(special[:, 0:1024], T["special1"], s_const)
    for c in range(AHEAD):
        round_piece(0, c)
    for queue in (PE, AC, VE):
        queue.engine.wait_ge(s_const, 48)

    def start_counts():
        act.sem_inc(s_prod, 1)
        act.sem_inc(s_turn, 1)

    def end_layer(last):
        nc.multi_engine_barrier(three)
        for one in layer_sems:
            act.sem_clear(one)
        start_counts()
        nc.multi_engine_barrier(three)
        for queue in (PE, AC, VE):
            queue.restart()
        for reads in (score_read, prob_read, pt_read):
            reads.clear()
        bank_read[TURNED] = bank_read[OUT] = ()
        loads[0] = 0

    loads[0] = 0
    act.sem_inc(s_used, 1)
    start_counts()
    nc.multi_engine_barrier(three)

    z1 = big[:, 0:6144].rearrange("p (m c) -> p m c", m=MT)
    post = [big[:, 6144 + 1024 * i:7168 + 1024 * i] for i in range(3)]
    band = big[:, 9216:10752].rearrange("p (h k) -> p h k", h=NA)
    alibi = special[:, 0:1024].rearrange("p (h k) -> p h k", h=NB)
    pre1 = special[:, 1024:1048].rearrange("p (i k) -> p i k", i=3)
    lam_in = special[:, 1056:1056 + 128].rearrange("p (i k) -> p i k", i=4)
    lam_c = special[:, 1184:1186]
    subln = special[:, 1216:1280]
    lam_t = special[:, 1280:1312]
    ob = special[:, 1536:2048]
    ob2 = special[:, 2048:2560]
    lb = [special[:, 2560 + 384 * i:2944 + 384 * i] for i in range(2)]
    lams = cell(8)
    c_ratio = [cell(2), cell(2)]
    r0 = cell(8)
    ob_s, ob_t, ob_y = cell(8), cell(8), cell(8)

    with nc.Fori(0, L, engines=three) as layer:
        first = layer * PIECES1
        load(pre1, T["pre1"][layer])
        load(lam_in, T["lams"][layer].partition_broadcast(P))
        load(lam_c, T["lam_const"][layer].partition_broadcast(P))
        load(subln, T["subln"][layer].partition_broadcast(P))
        for i in range(3):
            load(post[i], T["post1"][layer, i].partition_broadcast(P))
        load(band, T["band"][layer])
        for queue in (PE, AC, VE):
            queue.engine.wait_ge(s_par, 16 * loads[0])

        t = to_features(x, hn, pre1[:, 0, :], h_hi, h_lo, (0, 1, 2, 3), ())
        PE.after(t)
        end = feed_forward(first, 0, FFN_STRIPS, True, 0)
        t = add_norm(0.5, post[0], 4, end)

        t = to_features(x, hn, pre1[:, 1, :], h_hi, h_lo, (0, 1, 2, 3), (), t)
        PE.after(t)
        s = VE.step(dve.tensor_scalar(band, band, -1.0, None, ALU.mult))
        band_ready = VE.step(VE.after(s).memset(band[0:64, :, 192:256], BIG))
        for i in range(2):
            s = VE.step(VE.after(s).tensor_tensor_reduce(lam_t, lam_in[:, 2 * i, :], lam_in[:, 2 * i + 1, :], 1.0,
                                                 0.0, ALU.mult, ALU.add, lams[:, i:i + 1]))
        s = AC.step(AC.after(s).activation(lams[:, 2:4], lams[:, 0:2], ACT.Exp))
        s = VE.step(VE.after(s).tensor_tensor(lams[:, 4:5], lams[:, 3:4], lams[:, 2:3], ALU.subtract))
        lam_ready = VE.step(VE.after(s).tensor_tensor(lams[:, 5:6], lams[:, 4:5], lam_c[:, 0:1], ALU.subtract))
        minus_lam = lams[:, 5:6]
        gain_ready = VE.step(dve.tensor_scalar(subln, subln, lam_c[:, 1:2], None, ALU.mult))

        done = {}

        def evacuate(end, i, z=z1):
            dst = z[:, :, i * 512:i * 512 + 512]
            if i % 2:
                s = AC.step(AC.after(end).activation(dst, psum[:, 2:4, :], ACT.Copy))
            else:
                s = VE.step(VE.after(end).tensor_copy(dst, psum[:, 0:2, :]))
            done[i] = s

        def diff_units():
            units = []
            for h in range(NB):
                for m in range(MT):
                    def score(slot, h=h, m=m):
                        keys = (m + 1) * P
                        prods, segs = [], []
                        for j in range(2):
                            rows_ = slice(32 * (2 * (h % 2) + j), 32 * (2 * (h % 2) + j) + 32)
                            prods.append((qT[rows_, h // 2, m * P:m * P + P], kT[rows_, h // 2, 0:keys],
                                          j * S, keys))
                            segs.append((j * S, keys))
                        table = alibi[:, h, (1 - m) * P:(1 - m) * P + keys]
                        s = softmax_parts(slot, prods, (diff_qk[0],), [table] * 2, segs, True)
                        total, inverse = stat[slot][1:3]
                        r = VE.step(VE.after(s).reciprocal(inverse[:, 0:2], total[:, 0:2]))
                        c1 = VE.step(VE.after(r, lam_ready).scalar_tensor_tensor(
                            c_ratio[slot][:, 0:1], total[:, 0:1], inverse[:, 1:2], minus_lam, ALU.mult, ALU.mult))
                        VE.step(VE.after(r).tensor_copy(r0[:, 4 * m + h:4 * m + h + 1], inverse[:, 0:1]))
                        prob = soft[:, slot, 0, :]
                        return VE.step(VE.after(c1).scalar_tensor_tensor(
                            prob[:, 0:keys], prob[:, S:S + keys], c_ratio[slot][:, 0:1], prob[:, 0:keys],
                            ALU.mult, ALU.add))

                    def turn(slot, s, m=m):
                        return turn_blocks(slot, s, [P * i for i in range(m + 1)])

                    def out(slot, s, h=h, m=m):
                        pe_ = PE.after(s, *bank_read[OUT])
                        for i in range(m + 1):
                            t = pe_.matmul(psum[:, OUT, (4 * m + h) * 64:(4 * m + h) * 64 + 64],
                                           soft[:, slot, 1, i * P:i * P + P],
                                           z1[:, i, QKV_B + 512 + 64 * h:QKV_B + 576 + 64 * h],
                                           start=i == 0, stop=i == m, skip_group_check=True)
                        t = PE.step(t)
                        pt_read[slot] = (t,)
                        last_out[0] = t

                    units.append((score, turn, out))
            return units

        last_out, diff_qk, y_done = [None], [None], []

        def diff():
            diff_qk[0] = turn_qk(z1, [(QKV_B + 128 * i, qT[:, i, :], -32.0 ** -0.5) for i in range(2)]
                                 + [(QKV_B + 256 + 128 * i, kT[:, i, :], 1.0) for i in range(2)],
                                 (done[0], done[1]))
            yield
            yield from pipeline(diff_units())
            o3 = ob.rearrange("p (g d) -> p g d", d=64)
            q3 = ob2.rearrange("p (g d) -> p g d", d=64)
            s = VE.step(VE.after(last_out[0]).tensor_tensor(
                o3, psum[:, OUT, :].rearrange("p (g d) -> p g d", d=64), r0.unsqueeze(2).broadcast_to((P, 8, 64)),
                ALU.mult))
            bank_read[OUT] = (s,)
            s = VE.step(VE.after(s).tensor_tensor(q3, o3, o3, ALU.mult))
            s = VE.step(VE.after(s).tensor_reduce(ob_s, q3, AX.X, ALU.add))
            s = VE.step(VE.after(s).tensor_scalar(ob_s, ob_s, 1.0 / 64, EPS, ALU.mult, ALU.add))
            s = rsqrt(ob_s, ob_t, ob_y, s)
            yield
            s = VE.step(VE.after(s).tensor_tensor(o3, o3, ob_y.unsqueeze(2).broadcast_to((P, 8, 64)), ALU.mult))
            s = VE.step(VE.after(s, gain_ready).tensor_tensor(o3, o3, subln.unsqueeze(1).broadcast_to((P, 8, 64)),
                                                              ALU.mult))
            yield
            pe_ = PE.after(s, *bank_read[TURNED])
            for i in range(2):
                for m in range(MT):
                    t = pe_.transpose(psum[:, TURNED, i * S + m * P:i * S + m * P + P],
                                      ob[:, m * S + i * P:m * S + i * P + P], ident)
            t = PE.step(t)
            s = split_out(psum[:, TURNED, :], y_hi[:, 3:5, :].rearrange("p a b -> p (a b)"),
                          y_lo[:, 3:5, :].rearrange("p a b -> p (a b)"), t)
            bank_read[TURNED] = (s,)
            y_done.append(s)
            yield

        def head_units(col, kind, ready):
            units = []
            for h in range(6):
                half = slice(64 * (h % 2), 64 * (h % 2) + 64)
                q, k = qT[half, h // 2, :], kT[half, h // 2, :]
                v = z1[:, :, col + 768 + 64 * h:col + 832 + 64 * h]

                def band_score(slot, h=h, q=q, k=k):
                    prods = [(q[:, 0:P], k[:, 0:P], 0, P), (q[:, P:S], k, P, S)]
                    s = softmax_parts(slot, prods, ready, [band[:, h, P:S], band[:, h, :]], SEG)
                    return normalised(slot, s, SEG, None)

                def stick_score(slot, q=q, k=k):
                    bank = SCORE[slot]
                    zt = psum[:, bank, 0:384]
                    a_ = soft[:, slot, 0, 0:384]
                    pe_ = PE.after(*ready, *score_read.get(slot, ()))
                    pe_.matmul(psum[:, bank, 0:S], k[:, 0:P], q, start=True, stop=True)
                    t = PE.step(pe_.matmul(psum[:, bank, S:384], k[:, P:S], q[:, P:S], start=True, stop=True))
                    s = AC.step(AC.after(t, *prob_read.get(slot, ())).activation(a_, zt, ACT.Abs))
                    s = AC.step(AC.after(s).activation(a_, a_, ACT.Exp, scale=-1.0))
                    s = AC.step(AC.after(s).activation(a_, a_, ACT.Ln, bias=1.0))
                    s = VE.step(VE.after(s, *pt_read.get(slot, ())).scalar_tensor_tensor(
                        lb[slot], zt, 0.0, a_, ALU.min, ALU.subtract))
                    s = VE.step(VE.after(s).tensor_tensor(a_, lb[slot], zt, ALU.subtract))
                    score_read[slot] = (s,)
                    for c_ in (0, S):
                        s2 = VE.step(VE.after(s).tensor_tensor(a_[:, c_:c_ + P], a_[:, c_:c_ + P], strict, ALU.mult))
                    return s2

                def stick_turn(slot, s):
                    a_ = soft[:, slot, 0, 0:384]
                    pe_ = PE.after(s, *bank_read[TURNED])
                    pe_.matmul(psum[:, TURNED, 0:384], tri, a_, start=True, stop=False, skip_group_check=True)
                    t = PE.step(pe_.matmul(psum[:, TURNED, P:S], ones, a_[:, S:384], start=False, stop=True,
                                           skip_group_check=True))
                    prob_read[slot] = (t,)
                    w = soft[:, slot, 1, 0:384]
                    s = VE.step(VE.after(t, *pt_read.get(slot, ())).tensor_tensor(w, lb[slot], psum[:, TURNED, 0:384],
                                                                                  ALU.add))
                    bank_read[TURNED] = (s,)
                    s = AC.step(AC.after(s).activation(w, w, ACT.Exp))
                    for c_ in (0, S):
                        s2 = VE.step(VE.after(s).tensor_tensor(w[:, c_:c_ + P], w[:, c_:c_ + P], strict, ALU.mult))
                    return s2

                def out(slot, s, h=h, v=v):
                    col_ = S * (h // 2 % 2)
                    PE.after(s, *(bank_read[OUT] if h % 2 == 0 else ()))
                    t = PE.step(causal_out(slot, s, 64 * (h % 2), v, col_))
                    pt_read[slot] = (t,)
                    if h % 2:
                        kt = (0 if kind == "band" else 5) + h // 2
                        s = split_out(psum[:, OUT, col_:col_ + S], y_hi[:, kt, :], y_lo[:, kt, :], t)
                        bank_read[OUT] = (s,)
                        y_done.append(s)

                if kind == "band":
                    units.append((band_score, lambda slot, s: turn_blocks(slot, s, BLOCKS), out))
                else:
                    units.append((stick_score, stick_turn, out))
            return units

        def heads(col, kind, strips_):
            s = turn_qk(z1, [(col + 128 * i, qT[:, i, :], -0.125 if kind == "band" else 0.125) for i in range(3)]
                        + [(col + 384 + 128 * i, kT[:, i, :], 1.0) for i in range(3)],
                        [done[i] for i in strips_])
            yield
            yield from pipeline(head_units(col, kind, (s, band_ready)))

        work = []

        def between():
            while work:
                try:
                    next(work[0])
                    return
                except StopIteration:
                    work.pop(0)

        c = FFN_PIECES
        for i in range(COLS1 // 512):
            bank = 2 * (i % 2)
            PE.after(*([done[i - 2]] if i > 1 else []))
            end = strip(first, c, h_hi, h_lo, bank, between)
            evacuate(end, i)
            c += 4
            if i == 1:
                work.append(diff())
            if i == 3:
                work.append(heads(QKV_A, "band", (1, 2, 3)))
            if i == 5:
                work.append(heads(QKV_C, "stick", (3, 4, 5)))
            between()
        while work:
            between()
        PE.after(*y_done)
        for i in range(KD):
            end = rows(first, c + i, i, y_hi, y_lo, 0, i == 0, i == KD - 1)
        c += KD
        t = add_norm(1.0, post[1], 0, end)

        t = to_features(x, hn, pre1[:, 2, :], h_hi, h_lo, (0, 1, 2, 3), (), t)
        PE.after(t)
        end = feed_forward(first, c, FFN_STRIPS, True, FFN_STRIPS)
        add_norm(0.5, post[2], 4, end)
        assert c + FFN_PIECES == PIECES1
        end_layer(False)

    masks = special[:, 0:1024].rearrange("p (i q) -> p i q", i=8)
    b_merge = special[:, 1024:4096]
    gain12 = special[:, 4096:4864]
    gla_gain = special[:, 4864:4992]
    w2 = special[:, 4992:5248].rearrange("p (k e d) -> p k e d", k=2, e=2)
    w_gate = special[0:16, 5248:5504]
    pe_rows = special[:, 5504:5536].rearrange("p (k j) -> p k j", k=2)
    pre2 = special[:, 5536:5560].rearrange("p (i k) -> p i k", i=3)
    b_gate = special[:, 5560:5562]
    mem_gain = special[:, 5568:5824].rearrange("p (i d) -> p i d", i=2)
    cmp_gain = special[0:32, 5824:5888]

    znq = big[:, 0:2048].rearrange("p (m c) -> p m c", m=MT)
    z3 = big[:, 2048:2640].rearrange("p (m c) -> p m c", m=MT)
    gqk = big[:, 2640:3664].rearrange("p (m c) -> p m c", m=MT)
    gv = big[:, 3664:4688].rearrange("p (m c) -> p m c", m=MT)
    gr = big[:, 4688:5712].rearrange("p (m c) -> p m c", m=MT)
    mq = big[:, 5712:6736].rearrange("p (m c) -> p m c", m=MT)
    merge = big[:, 6736:12880].rearrange("p (m c) -> p m c", m=MT)
    windows = [big[:, 6736:7248]] + [w[:, 0:2, :].rearrange("p a b -> p (a b)") for w in (y_hi, y_lo)]
    doubled = big[:, 8784:9808]
    merged = big[:, 2640:4688].rearrange("p (m c) -> p m c", m=MT)
    softf = soft[:, :, :, :].rearrange("p a b c -> p (a b c)")

    vb = extra[:, 0:512]
    hid = [extra[:, 512 + 128 * i:640 + 128 * i] for i in range(3)]
    hid_rep = extra[:, 896:1152].rearrange("p (e c) -> p e c", e=2)
    kb = extra[0:32, 1152:1280]
    kbd = extra[:, 1280:1312]
    pc = extra[:, 1312:1568]
    pct = extra[:, 1568:1824]
    att = [pc[:, 0:128], pc[:, 128:256]]
    att_off = pct[:, 0:128]
    gates = extra[:, 1824:1872].rearrange("p (m c) -> p m c", m=MT)
    trig = extra[:, 1872:1920].rearrange("p (f m i) -> p f m i", f=2, m=3)
    glow = extra[0:16, 512:768]
    kcn = extra[0:32, 1920:1984]
    tmp32 = extra[0:32, 1984:2048]
    mn16, sum16, inv16 = cell(16), cell(16), cell(16)
    s24, t24, y24 = cell(24), cell(24), cell(24)
    s8, t8, y8 = cell(8), cell(8), cell(8)
    c1_, c2_, c3_ = cell(1), cell(1), cell(1)

    pos_i = small[:, 500:503].bitcast(I32)
    pos_f = small[:, 504:507]
    assert small_at[0] <= 500
    s_rot = sem("s_rot")
    s = VE.step(dve.memset(small[:, 500:503], 0.0))
    AC.after(s)
    for m in range(MT):
        load(pos_i[:, m:m + 1], T["positions"].rearrange("b (p o) -> p (b o)", o=1)[m * P:m * P + P, :], s_rot)
    ends = T["positions"].rearrange("b (n t) -> (b n) t", t=16)
    for g in range(2):
        load(pos_i[16 * g:16 * g + 15, 2:3], ends[1:16, 15:16], s_rot, allow_slow_non_contiguous=True)
    load(special[:, 0:1024], T["masks"], s_rot)
    dve.wait_ge(s_rot, 80)
    s = VE.step(dve.tensor_copy(pos_f, pos_i))
    ang = hid[0][:, 0:48].rearrange("p (f m i) -> p f m i", f=2, m=3)
    angf, turns, turns_i = hid[0][:, 0:48], hid[1][:, 0:48], hid[2][:, 0:48].bitcast(I32)
    for m in range(3):
        s = VE.step(VE.after(s).tensor_scalar(ang[:, 1, m, :], inv_freq, pos_f[:, m:m + 1], None, ALU.mult))
    s = VE.step(VE.after(s).tensor_copy(ang[:, 0], ang[:, 1]))
    s = VE.step(VE.after(s).tensor_scalar(turns, angf, 1.0 / (2 * math.pi), None, ALU.mult))
    s = VE.step(VE.after(s).tensor_copy(turns_i, turns))
    s = VE.step(VE.after(s).tensor_copy(turns, turns_i))
    rest = 2 * math.pi - 6.28125
    c_mid = float(np.float32(np.round(rest * 2 ** 21) / 2 ** 21))
    for part in (6.28125, c_mid, rest - c_mid):
        s = VE.step(VE.after(s).scalar_tensor_tensor(angf, turns, -part, angf, ALU.mult, ALU.add))
    s = VE.step(VE.after(s).tensor_scalar(angf[:, 0:24], angf[:, 0:24], math.pi / 2, None, ALU.add))
    for _ in range(2):
        s = VE.step(VE.after(s).tensor_scalar(turns, angf, math.pi, -2 * math.pi, ALU.is_gt, ALU.mult))
        s = VE.step(VE.after(s).tensor_tensor(angf, angf, turns, ALU.add))
        s = VE.step(VE.after(s).tensor_scalar(turns, angf, -math.pi, 2 * math.pi, ALU.is_lt, ALU.mult))
        s = VE.step(VE.after(s).tensor_tensor(angf, angf, turns, ALU.add))
    s = VE.step(VE.after(s).tensor_scalar(angf, angf, 3.1415925, -3.1415925, ALU.min, ALU.max))
    s = AC.step(AC.after(s).activation(extra[:, 1872:1920], angf, ACT.Sin))
    end_layer(False)

    def rotate(q4, heads_n, cos, sin, tmps, s):
        x1, x2 = q4[..., 0:8], q4[..., 8:16]
        for tmp, a_, b_ in ((tmps[0], x1, cos), (tmps[1], x2, sin), (tmps[2], x2, cos), (tmps[3], x1, sin)):
            s2 = VE.step(VE.after(s).tensor_tensor(tmp, a_, b_, ALU.mult))
        s = VE.step(VE.after(s2).tensor_tensor(x1, tmps[0], tmps[1], ALU.subtract))
        return VE.step(VE.after(s).tensor_tensor(x2, tmps[2], tmps[3], ALU.add))

    def head_norm(flat, groups, width, scratch, cells, gain, *ready):
        v3 = flat.rearrange("p (g d) -> p g d", d=width)
        sq, t_, y_ = (c_[:, 0:groups] for c_ in cells)
        s = AC.step(AC.after(*ready).activation(scratch, flat, ACT.Square))
        s = VE.step(VE.after(s, *ready).tensor_reduce(sq, scratch.rearrange("p (g d) -> p g d", d=width), AX.X, ALU.add))
        s = VE.step(VE.after(s).tensor_scalar(sq, sq, 1.0 / width, EPS, ALU.mult, ALU.add))
        s = rsqrt(sq, t_, y_, s)
        s = VE.step(VE.after(s).tensor_tensor(v3, v3, y_.unsqueeze(2).broadcast_to((P, groups, width)), ALU.mult))
        if gain is None:
            return s
        return VE.step(VE.after(s).tensor_tensor(v3, v3, gain.unsqueeze(1).broadcast_to((P, groups, width)),
                                                 ALU.mult))

    with nc.Fori(0, L, engines=three) as layer:
        first = layer * PIECES2 + L * PIECES1
        load(memkv[:, :, :], T["mem"].rearrange("b (m p) d -> p (b m) d", p=P))
        for target, name in ((pre2, "pre2"), (w2, "w2"), (w_gate, "w_gate"), (pe_rows, "pe"), (b_gate, "b_gate")):
            load(target, T[name][layer])
        for target, name in ((b_merge, "b_merge"), (gain12, "gain12"), (gla_gain, "gla_gain"),
                             (mem_gain, "mem_gain")):
            load(target, T[name][layer].partition_broadcast(P))
        load(cmp_gain, T["cmp_gain"][layer].partition_broadcast(32))
        for queue in (PE, AC, VE):
            queue.engine.wait_ge(s_par, 16 * loads[0])
        s = VE.step(dve.tensor_scalar(gain12[:, 0:512], gain12[:, 0:512], -0.125, None, ALU.mult))
        gain_ready = VE.step(VE.after(s).tensor_scalar(mem_gain[:, 0, :], mem_gain[:, 0, :], -128.0 ** -0.5, None,
                                                       ALU.mult))

        t = to_features(memkv, memkv, pre2[:, 2, :], y_hi, y_lo, (4, 5, 6, 7), ())
        mem_turned = (PE, PE.n)
        PE.after(t)
        c = 0
        end = strip(first, c, y_hi, y_lo, 0)
        mk = VE.step(VE.after(mem_turned, end).tensor_copy(memkv[:, :, 0:512], psum[:, 0:2, :]))
        t = to_features(x, hn, pre2[:, 0, :], h_hi, h_lo, (4, 5, 6, 7), (), t)
        end = strip(first, c + 4, y_hi, y_lo, 2)
        mv = VE.step(VE.after(end).tensor_copy(memkv[:, :, 512:1024], psum[:, 2:4, :]))
        c += 8
        PE.after(t)

        y_done = []
        got = {}

        def mem_attention():
            s = head_norm(mq.rearrange("p m c -> p (m c)"), 8, P, softf[:, 0:1024], (s8, t8, y8), mem_gain[:, 0, :],
                          got["mq"], gain_ready)
            yield
            kk = memkv[:, :, 0:512]
            for m in range(MT):
                s = head_norm(kk[:, m, :], 4, P, softf[:, 0:512], (s8, t8, y8), mem_gain[:, 1, :], mk, s)
            yield
            s = turn_qk(mq, [(P * h, qT[:, h, :], 1.0) for h in range(4)], (s,))
            yield
            s = turn_qk(memkv, [(P * h, kT[:, h, :], 1.0) for h in range(4)], (s,))
            yield
            segs = [(0, S), (S, S)]
            units = []
            for h in range(4):
                def score(slot, h=h, s=s):
                    prods = [(qT[:, h, m * P:m * P + P], kT[:, h, :], m * S, S) for m in range(MT)]
                    return normalised(slot, softmax_parts(slot, prods, (s,), [None, None], segs), segs, None)

                def turn(slot, s):
                    return turn_blocks(slot, s, [0, S, P, S + P])

                def out(slot, s, h=h):
                    pe_ = PE.after(s, *bank_read[OUT])
                    for k in range(2):
                        t = pe_.matmul(psum[:, OUT, 0:S], memkv[:, k, 512 + P * h:640 + P * h],
                                       soft[:, slot, 1, k * S:k * S + S], start=k == 0, stop=k == 1)
                    t = PE.step(t)
                    pt_read[slot] = (t,)
                    s = split_out(psum[:, OUT, 0:S], y_hi[:, 8 + h, :], y_lo[:, 8 + h, :], t)
                    bank_read[OUT] = (s,)
                    y_done.append(s)

                units.append((score, turn, out))
            PE.after(mv)
            yield from pipeline(units)

        def nsa_prep():
            idle = [r for reads in (prob_read, pt_read) for v_ in reads.values() for r in v_]
            sq = softf[:, 0:1536]
            z4 = znq[:, :, 0:768]
            s = got["nq"]
            ready = (s, got["nk"], gain_ready, *idle)
            for m in range(MT):
                a = AC.step(AC.after(*ready).activation(sq[:, m * 768:m * 768 + 768], z4[:, m, :], ACT.Square))
            s = VE.step(VE.after(a, *ready).tensor_reduce(s24, sq.rearrange("p (g d) -> p g d", d=64), AX.X, ALU.add))
            s = VE.step(VE.after(s).tensor_scalar(s24, s24, 1.0 / 64, EPS, ALU.mult, ALU.add))
            s = rsqrt(s24, t24, y24, s)
            yield
            for m in range(MT):
                v3 = z4[:, m, :].rearrange("p (h d) -> p h d", d=64)
                s2 = VE.step(VE.after(s).tensor_tensor(
                    v3, v3, y24[:, 12 * m:12 * m + 12].unsqueeze(2).broadcast_to((P, 12, 64)), ALU.mult))
            for m in range(MT):
                s = VE.step(VE.after(s2).tensor_tensor(z4[:, m, :], z4[:, m, :], gain12, ALU.mult))
            yield
            for m in range(MT):
                q4 = z4[:, m, :].rearrange("p (h d) -> p h d", d=64)
                cos, sin = (trig[:, f, m, :].unsqueeze(1).broadcast_to((P, 12, 8)) for f in range(2))
                tmps = [softf[:, 96 * i:96 * i + 96].rearrange("p (h d) -> p h d", h=12) for i in range(4)]
                s = rotate(q4, 12, cos, sin, tmps, s)
            got["nsa"] = s
            yield
            d6 = doubled.rearrange("p (m k g r d) -> p m k g r d", m=MT, k=2, g=2, r=2)
            src = znq[:, :, 768:1024].rearrange("p m (k g d) -> p m k g d", k=2, g=2)
            for m in range(MT):
                for k in range(2):
                    for r in range(2):
                        s = VE.step(VE.after(got["nk"]).tensor_copy(d6[:, m, k, :, r, :], src[:, m, k]))
            got["doubled"] = s
            yield

        def windows_of(kv):
            bank = SCORE[kv]
            pe_ = PE.after(got["doubled"], *score_read.get(kv, ()))
            for g in range(2):
                for m in range(MT):
                    col = ((m * 2 + kv) * 2 + g) * 128
                    t = pe_.transpose(psum[:, bank, g * S + m * P:g * S + m * P + P], doubled[:, col:col + 128], ident)
            t = PE.step(t)
            whole = windows[0].rearrange("p (j g n) -> p j g n", j=16, g=2)
            z_ = VE.step(VE.after(t).memset(windows[0], 0.0))
            for g in range(2):
                ps4 = psum[:, bank, g * S:g * S + S].rearrange("p (n j r) -> p r j n", j=8, r=2)
                for par in range(2):
                    for half in range(2):
                        pr = slice(64 * par, 64 * par + 64)
                        src = ps4[pr, par, :, half:half + 15]
                        a = VE.step(VE.after(z_).tensor_tensor(
                            whole[pr, 8 * half:8 * half + 8, g, 0:15], src,
                            pe_rows[pr, kv, 8 * half:8 * half + 8].unsqueeze(2).broadcast_to((64, 8, 15)), ALU.add))
            score_read[kv] = (a,)
            h_ = AC.step(AC.after(a).activation(windows[1], windows[0], ACT.Copy))
            return VE.step(VE.after(h_).tensor_tensor(windows[2], windows[0], f32(windows[1]), ALU.subtract))

        def compress():
            nonlocal c
            for kv in range(2):
                s = windows_of(kv)
                PE.after(s, *(got["cmp_free"]))
                w_hi, w_lo = (w.rearrange("p (j n) -> p j n", j=16) for w in windows[1:])
                for i in range(4):
                    slot = next_piece(first, c)
                    for jj in range(4):
                        j = 4 * i + jj
                        for e in range(2):
                            cols = slice(jj * 256 + e * P, jj * 256 + e * P + P)
                            o = psum[:, got["cmp_bank"], (2 * kv + e) * 32:(2 * kv + e) * 32 + 32]
                            fresh = kv == 0 and j == 0 and e == 0
                            pe.matmul(o, hi[:, slot, cols], w_hi[:, j, :], start=fresh, stop=False,
                                      skip_group_check=True)
                            pe.matmul(o, lo[:, slot, cols], w_hi[:, j, :], start=False, stop=False,
                                      skip_group_check=True)
                            last = pe.matmul(o, hi[:, slot, cols], w_lo[:, j, :], start=False, stop=j == 15,
                                             skip_group_check=True)
                    last.then_inc(s_used, 1)
                    c += 1
                got["windows_read"] = At(s_used, first + (c + 1))
                for q in (AC, VE):
                    q.after(got["windows_read"])
            h_, a_, b_ = hid
            s = VE.step(dve.tensor_copy(h_, psum[:, got["cmp_bank"], 0:128]))
            got["cmp_read"] = s
            s = VE.step(VE.after(s).tensor_tensor(a_, h_, h_, ALU.mult))
            s = VE.step(VE.after(s).tensor_scalar(a_, a_, 0.044715, 1.0, ALU.mult, ALU.add))
            s = VE.step(VE.after(s).tensor_tensor(a_, a_, h_, ALU.mult))
            s = VE.step(VE.after(s).tensor_scalar(a_, a_, -50.0, None, ALU.max))
            s = AC.step(AC.after(s).activation(a_, a_, ACT.Exp, scale=-2.0 * math.sqrt(2.0 / math.pi)))
            s = VE.step(VE.after(s).tensor_scalar(a_, a_, 1.0, None, ALU.add))
            s = VE.step(VE.after(s).reciprocal(b_, a_))
            got["hid"] = VE.step(VE.after(s).tensor_tensor(h_, h_, b_, ALU.mult))

        def nsa():
            h4 = hid[0].rearrange("p (k e n) -> p k e n", k=2, e=2)
            pe_ = PE.after(got["hid"], *bank_read[TURNED])
            for e in range(2):
                t = pe_.matmul(psum[0:32, TURNED, 0:64], h4[:, 0, e, :], w2[:, 0, e, :], start=e == 0, stop=e == 1)
            t = PE.step(t)
            s = VE.step(VE.after(t).tensor_copy(kcn, psum[0:32, TURNED, 0:64]))
            s = VE.step(VE.after(s).tensor_tensor_reduce(tmp32, kcn, kcn, 1.0, 0.0, ALU.mult, ALU.add, c1_[0:32, :]))
            s = VE.step(VE.after(s).tensor_scalar(c1_[0:32, :], c1_[0:32, :], 1.0 / 64, EPS, ALU.mult, ALU.add))
            s = rsqrt(c1_[0:32, :], c2_[0:32, :], c3_[0:32, :], s)
            s = VE.step(VE.after(s).scalar_tensor_tensor(kcn, kcn, c3_[0:32, 0:1], cmp_gain, ALU.mult, ALU.mult))
            s = rotate(kcn, 1, trig[0:32, 0, 2, :], trig[0:32, 1, 2, :], [tmp32[:, 8 * i:8 * i + 8] for i in range(4)],
                       s)
            kbs = VE.step(VE.after(s).tensor_tensor(
                kb.rearrange("p (g d) -> p g d", g=2), kcn.unsqueeze(1).broadcast_to((32, 2, 64)),
                own_keys.unsqueeze(2).broadcast_to((32, 2, 64)), ALU.mult))
            r_ = VE.step(VE.after(got["hid"]).tensor_copy(
                hid_rep.rearrange("p e (j n) -> p e j n", j=4),
                h4[:, 1].unsqueeze(2).broadcast_to((P, 2, 4, 32))))
            yield
            pe_ = PE.after(kbs, r_)
            pe_.transpose(psum[:, TURNED, 64:96], kb, ident[0:32, 0:32])
            for e in range(2):
                t = pe_.matmul(psum[:, SCORE[0], 0:64], hid_rep[:, e, :], w2[:, 1, e, :], start=e == 0, stop=e == 1)
            t = PE.step(t)
            s = VE.step(VE.after(t).tensor_copy(kbd, psum[:, TURNED, 64:96]))
            bank_read[TURNED] = (s,)
            s = VE.step(VE.after(t).tensor_copy(tmp_v, psum[:, SCORE[0], 0:64]))
            score_read[0] = (s,)
            s = VE.step(VE.after(s).tensor_tensor(
                vb.rearrange("p (h d) -> p h d", h=8), tmp_v.unsqueeze(1).broadcast_to((P, 8, 64)),
                own_values.unsqueeze(2).broadcast_to((P, 8, 64)), ALU.mult))
            s = VE.step(VE.after(got["z3"]).tensor_scalar(gates, z3[:, :, 256:280], -80.0, None, ALU.max))
            s = AC.step(AC.after(s).activation(gates, gates, ACT.Exp, scale=-1.0))
            s = VE.step(VE.after(s).tensor_scalar(gates, gates, 1.0, None, ALU.add))
            s = VE.step(VE.after(s).reciprocal(gates, gates))
            gates_ready = s
            yield
            sk = turn_qk(znq, [(512, kT[:, 0, :], 1.0), (640, kT[:, 1, :], 1.0)]
                         + [(P * j, qT[:, j, :], 1.0) for j in range(4)], (got["nsa"],))
            yield
            units = []

            def cmp_score(slot):
                bank = SCORE[slot]
                pe_ = PE.after(sk, s_vb[0], *score_read.get(slot, ()))
                for m in range(MT):
                    for j in range(4):
                        t = pe_.matmul(psum[:, bank, m * P + 32 * j:m * P + 32 * j + 32], qT[:, j, m * P:m * P + P],
                                       kbd, start=True, stop=True, skip_group_check=True)
                t = PE.step(t)
                g3 = lambda a, m: a[:, m * P:m * P + P].rearrange("p (h n) -> p h n", n=16)
                each = lambda a, m: a[:, 8 * m:8 * m + 8].unsqueeze(2).broadcast_to((P, 8, 16))
                tab = lambda a, m: a[:, m, :].unsqueeze(1).broadcast_to((P, 8, 16))
                for m in range(MT):
                    s = VE.step(VE.after(t).tensor_tensor(g3(pc, m), g3(psum[:, bank, :], m), tab(cmp_table, m),
                                                          ALU.add))
                score_read[slot] = (s,)
                all3 = pc.rearrange("p (h n) -> p h n", n=16)
                s = VE.step(VE.after(s).tensor_reduce(mn16, all3, AX.X, ALU.min))
                s = VE.step(VE.after(s).tensor_tensor(all3, all3, mn16.unsqueeze(2).broadcast_to((P, 16, 16)),
                                                      ALU.subtract))
                s = AC.step(AC.after(s).activation(pc, pc, ACT.Exp, scale=-1.0))
                for m in range(MT):
                    s2 = VE.step(VE.after(s).tensor_tensor(g3(pc, m), g3(pc, m), tab(cmp_valid, m), ALU.mult))
                s = VE.step(VE.after(s2).tensor_reduce(sum16, all3, AX.X, ALU.add))
                s = VE.step(VE.after(s).tensor_scalar(sum16, sum16, 1e-30, None, ALU.max))
                s = VE.step(VE.after(s).reciprocal(inv16, sum16))
                s = VE.step(VE.after(s, gates_ready).tensor_tensor(
                    inv16.rearrange("p (m h) -> p m h", m=MT), inv16.rearrange("p (m h) -> p m h", m=MT),
                    gates[:, :, 0:8], ALU.mult))
                return VE.step(VE.after(s).tensor_tensor(all3, all3, inv16.unsqueeze(2).broadcast_to((P, 16, 16)),
                                                         ALU.mult))

            def cmp_turn(slot, s):
                pe_ = PE.after(s, *bank_read[TURNED])
                for m in range(MT):
                    t = pe_.transpose(psum[:, TURNED, m * P:m * P + P], pc[:, m * P:m * P + P], ident)
                t = PE.step(t)
                s = VE.step(VE.after(t).tensor_copy(pct, psum[:, TURNED, 0:S]))
                bank_read[TURNED] = (s,)
                got["pct"] = s
                return s

            s_vb = [(VE, VE.n)]
            units.append((cmp_score, cmp_turn, lambda slot, s: None))
            for j in range(4):
                for b in range(2):
                    for g in range(2):
                        half = slice(64 * g, 64 * g + 64)

                        def score(slot, j=j, b=b, g=g, half=half):
                            q, k = qT[half, j, :], kT[half, b, :]
                            prods = [(q[:, 0:P], k[:, 0:P], 0, P), (q[:, P:S], k, P, S)]
                            s = softmax_parts(slot, prods, (sk,), [causal[:, P:S], causal], SEG)
                            VE.after(gates_ready)
                            at = (1 + b) * 8 + 2 * j + g
                            return normalised(slot, s, SEG, [gates[:, m, at:at + 1] for m in range(MT)])

                        def out(slot, s, j=j, b=b, g=g):
                            col = S * (j % 2)
                            if b == 0 and g == 0:
                                PE.after(got["pct"], *bank_read[OUT]).matmul(
                                    psum[:, OUT, col:col + S], vb[:, j * P:j * P + P], pct, start=True, stop=False,
                                    skip_group_check=True)
                            PE.after(s)
                            v = z3[:, :, b * P + 64 * g:b * P + 64 * g + 64]
                            t = PE.step(causal_out(slot, s, 64 * g, v, col, False, True))
                            pt_read[slot] = (t,)
                            if b == 1 and g == 1:
                                s = split_out(psum[:, OUT, col:col + S], y_hi[:, j, :], y_lo[:, j, :], t)
                                bank_read[OUT] = (s,)
                                y_done.append(s)

                        units.append((score, lambda slot, s: turn_blocks(slot, s, BLOCKS), out))
            yield from pipeline(units)
            got["nsa_done"] = (PE, PE.n)

        tmp_v = hid[1][:, 0:64]

        def gla():
            s = turn_qk(gqk, [(P * i, qT[:, i, :], 0.125) for i in range(2)]
                        + [(256 + P * i, kT[:, i, :], 1.0) for i in range(2)], (got["gqk"],))
            pe_ = PE.after(*bank_read[TURNED])
            for m in range(MT):
                t = pe_.transpose(psum[0:16, TURNED, m * P:m * P + P], z3[:, m, 280:296], ident)
            t = PE.step(t)
            qk = s
            s = VE.step(VE.after(t).tensor_copy(glow, psum[0:16, TURNED, 0:S]))
            bank_read[TURNED] = (s,)
            yield
            pe_ = PE.after(s, *score_read.get(0, ()))
            for i in range(2):
                t = pe_.matmul(psum[:, SCORE[0], i * S:i * S + S], w_gate[:, i * P:i * P + P], glow, start=True,
                               stop=True, skip_group_check=True)
            t = PE.step(t)
            zt, ab, b_sum = qT[:, 2:4, :], kT[:, 2:4, :], softf[:, 0:512].rearrange("p (i t) -> p i t", i=2)
            idle = [r for reads in (prob_read, pt_read) for v_ in reads.values() for r in v_]
            for i in range(2):
                s = VE.step(VE.after(t).tensor_scalar(zt[:, i, :], psum[:, SCORE[0], i * S:i * S + S],
                                                      b_gate[:, i:i + 1], None, ALU.add))
            score_read[0] = (s,)
            s = AC.step(AC.after(s).activation(ab, zt, ACT.Abs))
            s = AC.step(AC.after(s).activation(ab, ab, ACT.Exp, scale=-1.0))
            s = AC.step(AC.after(s).activation(ab, ab, ACT.Ln, bias=1.0))
            s = VE.step(VE.after(s).scalar_tensor_tensor(zt, zt, 0.0, ab, ALU.min, ALU.subtract))
            for i in range(2):
                s2 = VE.step(VE.after(s, *idle).tensor_tensor_scan(ab[:, i, :], consts[:, 256:512], zt[:, i, :], 0.0,
                                                                   ALU.mult, ALU.add))
            csum, s_sum = ab, s2
            yield
            e_buf = big[:, 0:2048].rearrange("p (l t) -> p l t", l=8)
            q_buf = memkv[:, :, :].rearrange("p m c -> p (m c)").rearrange("p (l t) -> p l t", l=8)
            off_read = [None]
            og = gqk.rearrange("p m (h d) -> p m h d", h=4)
            o_last = [qk]
            for hp in range(2):
                for i, half in enumerate(LEVELS):
                    b3 = csum[:, hp, :].rearrange("p (n t) -> p n t", t=2 * half)
                    ref = b3[:, :, half - 1:half].broadcast_to((P, S // (2 * half), 2 * half))
                    s = VE.step(VE.after(s_sum, got["nsa_done"], (PE, PE.n)).tensor_tensor(
                        e_buf[:, i, :].rearrange("p (n t) -> p n t", t=2 * half), b3, ref, ALU.subtract))
                ef = big[:, 0:2048]
                s = VE.step(VE.after(s).scalar_tensor_tensor(ef, ef, -1.0, ef, ALU.mult, ALU.max))
                s = AC.step(AC.after(s).activation(ef, ef, ACT.Exp, scale=-1.0 / 16))
                qb, kb_ = (a[:, hp, :].unsqueeze(1).broadcast_to((P, 8, S)) for a in (qT, kT))
                s = VE.step(VE.after(s, qk).tensor_tensor(q_buf, e_buf, qb, ALU.mult))
                s = VE.step(VE.after(s).tensor_tensor(e_buf, e_buf, kb_, ALU.mult))
                ready = s
                yield
                units = []
                for hh in range(2):
                    for m in range(MT):
                        half_ = slice(64 * hh, 64 * hh + 64)
                        h = 2 * hp + hh

                        def score(slot, m=m, half_=half_, h=h, hp=hp, ready=ready):
                            toks = slice(m * P, m * P + P)
                            pe_ = PE.after(ready, *score_read.get(0, ()), *score_read.get(1, ()))
                            for i in range(8):
                                lhsT, rhs = ((e_buf[half_, i + 1, toks], q_buf[half_, i + 1, toks]) if i < 7
                                             else (kT[half_, hp, toks], qT[half_, hp, toks]))
                                t = pe_.matmul(psum[:, SCORE[i // 4], (i % 4) * P:(i % 4) * P + P], lhsT, rhs,
                                               start=True, stop=True, skip_group_check=True)
                            if m:
                                t = PE.after(*bank_read[TURNED]).matmul(
                                    psum[:, TURNED, 0:P], e_buf[half_, 0, 0:P], q_buf[half_, 0, P:S], start=True,
                                    stop=True)
                            t = PE.step(t)
                            prod = soft[:, slot, :, :].rearrange("p a b -> p (a b)")
                            s = VE.step(VE.after(t).tensor_tensor(
                                prod.rearrange("p (i q) -> p i q", i=8),
                                psum[:, 4:6, :].rearrange("p a (i q) -> p (a i) q", i=4), masks, ALU.mult))
                            score_read[0] = score_read[1] = (s,)
                            s = VE.step(VE.after(s, *prob_read.get(slot, ())).tensor_reduce(
                                att[slot], prod.rearrange("p (i q) -> p q i", i=8), AX.X, ALU.add))
                            if m:
                                s = VE.step(VE.after(s, off_read[0]).tensor_copy(att_off, psum[:, TURNED, 0:P])
                                            if off_read[0] else
                                            VE.after(s).tensor_copy(att_off, psum[:, TURNED, 0:P]))
                                bank_read[TURNED] = (s,)
                            return s

                        def turn(slot, s, m=m, h=h):
                            pe_ = PE.after(s, got["gv"], *bank_read[OUT])
                            o = psum[:, OUT, 0:P]
                            t = pe_.matmul(o, att[slot], gv[:, m, h * P:h * P + P], start=True, stop=not m)
                            if m:
                                t = pe_.matmul(o, att_off, gv[:, 0, h * P:h * P + P], start=False, stop=True)
                            t = PE.step(t)
                            if m:
                                off_read[0] = t
                            prob_read[slot] = (t,)
                            s = VE.step(VE.after(t, qk).tensor_copy(og[:, m, h, :], o))
                            bank_read[OUT] = (s,)
                            o_last[0] = s
                            return s

                        units.append((score, turn, lambda slot, s: None))
                yield from pipeline(units)
            flat = gqk.rearrange("p m c -> p (m c)")
            s = head_norm(flat, 8, P, softf[:, 0:1024], (s8, t8, y8), gla_gain, o_last[0])
            s = VE.step(VE.after(s, got["gr"]).tensor_tensor(flat, flat, gr.rearrange("p m c -> p (m c)"), ALU.mult))
            yield
            for pair in range(2):
                pe_ = PE.after(s, *score_read.get(0, ()), *score_read.get(1, ()))
                for i in range(2):
                    for m in range(MT):
                        col = (2 * pair + i) * P
                        t = pe_.transpose(psum[:, SCORE[pair], i * S + m * P:i * S + m * P + P],
                                          gqk[:, m, col:col + P], ident)
                t = PE.step(t)
                kts = slice(4 + 2 * pair, 6 + 2 * pair)
                e_ = split_out(psum[:, SCORE[pair], :], y_hi[:, kts, :].rearrange("p a b -> p (a b)"),
                               y_lo[:, kts, :].rearrange("p a b -> p (a b)"), t)
                y_done.append(e_)
            yield

        work.clear()
        names = ["gr", "mq", "nq", "nk", "z3", "cmp", "gqk", "gv"] + ["merge"] * 6
        dests = {"gr": gr, "mq": mq, "nq": znq[:, :, 0:512], "nk": znq[:, :, 512:1024], "z3": z3, "gqk": gqk, "gv": gv}
        free = {0: (mk,), 2: (mv,)}
        n_merge = 0
        for i, name in enumerate(names):
            bank = 2 * (i % 2)
            PE.after(*free[bank])
            if name == "cmp":
                while work and not {"doubled"} <= set(got):
                    between()
                got["cmp_free"], got["cmp_bank"] = (), bank
                compress()
                free[bank] = (got["cmp_read"],)
                work.append(nsa())
                continue
            end = strip(first, c, h_hi, h_lo, bank, between)
            c += 4
            out = psum[:, bank:bank + 2, :]
            if name == "merge":
                cols = slice(512 * n_merge, 512 * n_merge + 512)
                s = VE.step(VE.after(end).tensor_tensor(
                    merge[:, :, cols], out, b_merge[:, cols].unsqueeze(1).broadcast_to((P, MT, 512)), ALU.add))
                n_merge += 1
            elif name == "gr":
                s = AC.step(AC.after(end).activation(gr, out, ACT.Silu))
                exp_and_ln()
            elif name == "z3":
                s = VE.step(VE.after(end).tensor_copy(z3, out[:, :, 0:296]))
            elif i % 2:
                s = AC.step(AC.after(end).activation(dests[name], out, ACT.Copy))
            else:
                s = VE.step(VE.after(end).tensor_copy(dests[name], out))
            free[bank] = (s,)
            got[name] = s
            if name == "mq":
                work.append(mem_attention())
            if name == "nk":
                work.append(nsa_prep())
            if name == "gv":
                work.append(gla())
            between()
        merge_ready = s
        while work:
            between()

        for m in range(MT):
            for b in (2, 0, 1):
                w = merge[:, m, b * D:b * D + D]
                s = AC.step(AC.after(merge_ready).activation(w, w, ACT.Sigmoid))
        gate_done = s
        PE.after(*y_done)
        free = {0: (merge_ready,), 4: ()}
        s_prev = None
        for n, b in enumerate((2, 0, 1)):
            bank = 4 * (n % 2)
            PE.after(*free[bank])
            for i in range(4):
                end = rows(first, c + i, 4 * b + i, y_hi, y_lo, bank, i == 0, i == 3)
            c += 4
            for m in range(MT):
                f = psum[:, bank + 2 * m:bank + 2 * m + 2, :].rearrange("p a b -> p (a b)")
                g_ = merge[:, m, b * D:b * D + D]
                s = VE.step(VE.after(end, gate_done).tensor_tensor(merged[:, m, :] if n == 0 else g_, g_, f, ALU.mult))
                if n:
                    s = VE.step(VE.after(s).tensor_tensor(merged[:, m, :], merged[:, m, :], g_, ALU.add))
            free[bank] = (s,)
        for pair in range(KD // 2):
            bank = 4 + pair
            pe_ = PE.after(s)
            for i in range(2):
                for m in range(MT):
                    k = 2 * pair + i
                    t = pe_.transpose(psum[:, bank, i * S + m * P:i * S + m * P + P],
                                      merged[:, m, k * P:k * P + P], ident)
            t = PE.step(t)
            kts = slice(2 * pair, 2 * pair + 2)
            e_ = split_out(psum[:, bank, :], h_hi[:, kts, :].rearrange("p a b -> p (a b)"),
                           h_lo[:, kts, :].rearrange("p a b -> p (a b)"), t)
        PE.after(e_)
        for i in range(KD):
            end = rows(first, c + i, i, h_hi, h_lo, 0, i == 0, i == KD - 1)
        c += KD
        for m in range(MT):
            f = psum[:, 2 * m:2 * m + 2, :].rearrange("p a b -> p (a b)")
            s = VE.step(VE.after(end).tensor_tensor(x[:, m, :], x[:, m, :], f, ALU.add))

        t = to_features(x, hn, pre2[:, 1, :], h_hi, h_lo, (0, 1, 2, 3), (), s)
        PE.after(t)
        end = feed_forward(first, c, MLP_STRIPS, False, 0)
        for m in range(MT):
            f = psum[:, 4 + 2 * m:6 + 2 * m, :].rearrange("p a b -> p (a b)")
            s = VE.step(VE.after(end).tensor_tensor(x[:, m, :], x[:, m, :], f, ALU.add))
        assert c + MLP_STRIPS * 8 == PIECES2
        end_layer(True)

    act.wait_ge(s_used, PIECES)
    round_piece(0, PIECES + AHEAD)
    act.dma_start(T["out"].rearrange("b (m p) d -> p (b m) d", p=P), x[:, :, :]).then_inc(s_out, 16)
    act.wait_ge(s_out, 16)
    act.wait_ge(s_lo, STREAM)


def pieces_of(w, cols):
    K, N = w.shape
    per = PIECE // cols
    a = w.reshape(K // P // per, per, P, N // cols, cols)
    return a.transpose(3, 0, 2, 1, 4).reshape(-1, P, PIECE)


def ffn_pieces(up, down, strips, rows_per):
    u = up.reshape(strips, 4, P, PIECE)
    d = down.reshape(strips, rows_per, P, PIECE)
    out = [u[0]]
    for i in range(1, strips):
        out += [u[i], d[i - 1]]
    return np.concatenate(out + [d[-1]])


def swiglu_pieces(gate, up, down):
    both = np.concatenate([gate.reshape(D, FFN_STRIPS, 256), up.reshape(D, FFN_STRIPS, 256)], 2).reshape(D, -1)
    return ffn_pieces(pieces_of(both, 512), pieces_of(down, 1024), FFN_STRIPS, 2)


def stream_of(a):
    parts = []
    for l in range(L):
        w = a["w_in"][l]
        A, B, C = 384, 256, 384
        qa, ka, va, qb, kb, vb, qc, kc, vc = np.split(w, np.cumsum([A, A, A, B, B, B, C, C]), 1)
        w = np.concatenate([qb, kb, vb, qa, ka, va, qc, kc, vc], 1)
        parts += [swiglu_pieces(a["ffn1_w_gate"][l], a["ffn1_w_up"][l], a["ffn1_w_down"][l]),
                  pieces_of(w, 512), pieces_of(a["w_out"][l], 1024),
                  swiglu_pieces(a["ffn2_w_gate"][l], a["ffn2_w_up"][l], a["ffn2_w_down"][l])]
    sizes = [512, 128, 128, 128, 128, 128, 128, 24, 256, 256, 512, 512, 16, 512, 3072]
    for l in range(L):
        q, kc, vc, ks, vs, kw, vw, g, gq, gk, gv, gr, gl, mq, mg = np.split(a["w_in_2"][l], np.cumsum(sizes)[:-1], 1)
        q = q.reshape(D, 2, 4, 64).transpose(0, 2, 1, 3).reshape(D, 512)
        g = g.reshape(D, 2, 4, 3).transpose(0, 3, 2, 1).reshape(D, 24)
        pad = np.zeros((D, 216), np.float32)
        before = np.concatenate([gr, mq, q, ks, kw, kc, vc, vs, vw, g, gl, pad], 1)
        after = np.concatenate([gq, gk, gv, mg], 1)
        wb = a["w_branch_2"][l]
        nsa_rows = wb[0].reshape(2, 4, 64, D).transpose(1, 0, 2, 3).reshape(512, D)
        parts += [pieces_of(a["mem_w_kv_2"][l], 512), pieces_of(before, 512),
                  pieces_of(a["cmp_w1_2"][l, 0], 256), pieces_of(a["cmp_w1_2"][l, 1], 256),
                  pieces_of(after, 512), pieces_of(wb[2], 1024), pieces_of(nsa_rows, 1024), pieces_of(wb[1], 1024),
                  pieces_of(a["w_out_2"][l], 1024),
                  ffn_pieces(pieces_of(a["w_up_2"][l], 512), pieces_of(a["w_down_2"][l], 1024), MLP_STRIPS, 4)]
    parts.append(np.zeros((STREAM - PIECES, P, PIECE), np.float32))
    out = np.concatenate(parts)
    assert out.shape[0] == STREAM, out.shape
    return out


def shape_constants():
    p, q = np.arange(P)[:, None], np.arange(P)[None, :]
    keys = np.arange(S)[None, :]
    c = np.zeros((P, 1024), np.float32)
    c[:, 0:128] = p == q
    c[:, 128:256] = p > q
    c[:, 256:512] = 1
    c[:, 512:640] = p < q
    c[:, 640:896] = np.where(keys <= P + p, 0, BIG)
    for m in range(MT):
        n = np.arange(16)[None, :]
        seen = (16 * n + 31 <= m * P + p) & (n < N_CMP)
        c[:, 896 + 16 * m:912 + 16 * m] = np.where(seen, 0, BIG)
        c[:, 928 + 16 * m:944 + 16 * m] = seen
    c[:, 960:968] = p // 16 == np.arange(8)[None, :]
    c[:32, 968:970] = p[:32] // 16 == np.arange(2)[None, :]
    c[:, 976:984] = np.power(np.float32(500000.0), -np.arange(8, dtype=np.float32) / 8)
    dist = np.abs(P + p - keys).astype(np.float32)
    late = np.where((keys // 64) > (P + p) // 64, BIG, 0).astype(np.float32)
    slopes = np.exp2(-8.0 * np.arange(1, NB + 1, dtype=np.float32) / NB)
    alibi = np.concatenate([np.float32(s) * dist + late for s in slopes], 1).astype(np.float32)
    masks = np.zeros((P, 8, P), np.float32)
    for i, half in enumerate(LEVELS[1:]):
        masks[:, i] = (p // (2 * half) == q // (2 * half)) & (p % (2 * half) < half) & (q % (2 * half) >= half)
    masks[:, 7] = p == q
    lam = [0.8 - 0.6 * math.exp(-0.3 * l) for l in range(L)]
    lam = np.array([[v, 1.0 - v] for v in lam], np.float32)
    return c, alibi, masks.reshape(P, 1024), lam


def by_tile(g):
    return np.ascontiguousarray(np.swapaxes(g.reshape(g.shape[:-1] + (-1, P)), -1, -2))


def kernel(**inputs):
    import concourse.bacc as bacc
    from concourse.bass_utils import run_bass_kernel_spmd

    a = {k: np.asarray(v) for k, v in inputs.items()}
    consts, alibi, masks, lam = shape_constants()
    rel = np.clip(P - np.arange(-127, 256), -128, 128) + 128
    band = a["rel_bias"][:, :, rel]
    at = np.arange(S)[None, :] - np.arange(P)[:, None] + 127
    arrays = {
        "stream": stream_of(a), "x": a["x"], "mem": a["mem_2"], "positions": a["positions_2"].astype(np.int32),
        "consts": consts, "special1": alibi, "masks": masks, "lam_const": lam,
        "pre1": np.stack([by_tile(a[n]) for n in ("ffn1_pre_g", "mix_pre_g", "ffn2_pre_g")], 2),
        "post1": np.stack([a[n] for n in ("ffn1_post_g", "mix_post_g", "ffn2_post_g")], 1),
        "lams": np.stack([a["diff_lambda_" + n] for n in ("q1", "k1", "q2", "k2")], 1),
        "subln": a["diff_subln_g"],
        "band": np.ascontiguousarray(band[:, :, at].transpose(0, 2, 1, 3)),
        "pre2": np.stack([by_tile(a[n]) for n in ("ln_mix_2", "ln_mlp_2", "mem_norm_2")], 2),
        "w2": np.ascontiguousarray(a["cmp_w2_2"].reshape(L, 2, 2, P, 64).transpose(0, 3, 1, 2, 4)),
        "w_gate": a["gla_w_gate_2"],
        "pe": np.ascontiguousarray(a["cmp_pe_2"].reshape(L, 2, 16, P).transpose(0, 3, 1, 2)),
        "b_gate": by_tile(a["gla_b_gate_2"]),
        "b_merge": a["b_merge_2"].reshape(L, -1),
        "gain12": np.concatenate([np.tile(a["nsa_q_norm_2"], (1, 8)), np.tile(a["nsa_k_norm_2"][:, 1], (1, 2)),
                                  np.tile(a["nsa_k_norm_2"][:, 2], (1, 2))], 1),
        "gla_gain": a["gla_norm_2"],
        "mem_gain": np.stack([a["mem_q_norm_2"], a["mem_k_norm_2"]], 1),
        "cmp_gain": a["nsa_k_norm_2"][:, 0],
    }
    nc = bacc.Bacc("TRN2", target_bir_lowering=False, num_devices=1)
    T, feed = {}, {}
    for name, v in arrays.items():
        feed[f"in_{name}"] = np.ascontiguousarray(v)
        T[name] = nc.dram_tensor(f"in_{name}", v.shape, mybir.dt.from_np(v.dtype), kind="ExternalInput").ap()
    T["out"] = nc.dram_tensor("out", (1, S, D), F32, kind="ExternalOutput").ap()
    build(nc, T)
    return run_bass_kernel_spmd(nc, [feed], core_ids=[0]).results[0]["out"]
```

```python
import math
from contextlib import ExitStack

import numpy as np

import concourse.bass as bass
from concourse import mybir

F32 = mybir.dt.float32
F32R = mybir.dt.float32r
I32 = mybir.dt.int32
ALU = mybir.AluOpType
ACT = mybir.ActivationFunctionType
AX = mybir.AxisListType

P = 128
S = 256
MT = S // P
D = 1024
KD = D // P
L = 2
EPS = 1e-6
BIG = 1e30
HUGE = 3e38

PIECE = 1024
RING = 4
AHEAD = 3

D_FF = 2816
FFN_STRIPS = D_FF // 256
NA, NB, NC_ = 6, 4, 6
COLS1 = 3072
QKV_A, QKV_B, QKV_C = 768, 0, 768 + 1152
FFN_PIECES = FFN_STRIPS * 6
PIECES1 = 2 * FFN_PIECES + COLS1 // 512 * 4 + KD

MLP_STRIPS = 4096 // 512
N_CMP = 15
PIECES2 = 2 * 4 + 13 * 4 + 8 + 12 + KD + MLP_STRIPS * 8
PIECES = L * (PIECES1 + PIECES2)
STREAM = PIECES + RING
assert PIECES1 % RING == 0 and PIECES2 % RING == 0

LEVELS = (128, 64, 32, 16, 8, 4, 2, 1)


class At:

    def __init__(self, sem, value):
        self.sem, self.value = sem, value


class Queue:

    def __init__(self, engine, sem):
        self.engine, self.sem = engine, sem
        self.n, self.seen = 0, {}

    def after(self, *steps):
        for step in steps:
            if isinstance(step, At):
                self.engine.wait_ge(step.sem, step.value)
                continue
            queue, n = step
            if self.seen.get(id(queue), 0) < n:
                self.engine.wait_ge(queue.sem, n)
                self.seen[id(queue)] = n
        return self.engine

    def step(self, instruction):
        instruction.then_inc(self.sem, 1)
        self.n += 1
        return (self, self.n)

    def restart(self):
        self.n, self.seen = 0, {}


def build(nc, T):
    with ExitStack() as stack:
        build_in(nc, T, stack)


def build_in(nc, T, stack):
    def sb(name, shape, dtype=F32):
        return stack.enter_context(nc.sbuf_tensor(name, list(shape), dtype))

    def sem(name):
        return stack.enter_context(nc.semaphore(name))

    pe, dve, act, pool, sp = nc.tensor, nc.vector, nc.scalar, nc.gpsimd, nc.sync
    three = [pe.engine, act.engine, dve.engine]

    raw = sb("raw", [P, RING, PIECE])
    hi = sb("hi", [P, RING, PIECE], F32R)
    lo = sb("lo", [P, RING, PIECE], F32R)
    x = sb("x", [P, MT, D])
    h_hi = sb("h_hi", [P, KD, S], F32R)
    h_lo = sb("h_lo", [P, KD, S], F32R)
    y_hi = sb("y_hi", [P, 12, S], F32R)
    y_lo = sb("y_lo", [P, 12, S], F32R)
    big = sb("big", [P, 12904])
    memkv = sb("memkv", [P, MT, 1024])
    soft = sb("soft", [P, 2, 2, 512])
    qT = sb("qT", [P, 4, S])
    kT = sb("kT", [P, 4, S])
    consts = sb("consts", [P, 1024])
    special = sb("special", [P, 5888])
    extra = sb("extra", [P, 2048])
    small = sb("small", [P, 512])
    psum = stack.enter_context(nc.psum_tensor("psum", [P, 8, 512], F32))

    ident = consts[:, 0:128]
    tri = consts[:, 128:256]
    ones = consts[:, 256:384]
    strict = consts[:, 512:640]
    causal = consts[:, 640:896]
    cmp_table = consts[:, 896:928].rearrange("p (m n) -> p m n", m=MT)
    cmp_valid = consts[:, 928:960].rearrange("p (m n) -> p m n", m=MT)
    own_values = consts[:, 960:968]
    own_keys = consts[0:32, 968:970]
    inv_freq = consts[:, 976:984]
    f32 = lambda a: a.bitcast(F32)

    s_landed = [sem(f"s_landed{i}") for i in range(RING)]
    s_hi = sem("s_hi")
    s_lo = sem("s_lo")
    s_used = sem("s_used")
    PE, AC, VE = (Queue(e, sem(n)) for e, n in ((pe, "s_pe"), (act, "s_act"), (dve, "s_dve")))
    s_pre = sem("s_pre")
    s_par = sem("s_par")
    s_gu = sem("s_gu")
    s_silu = sem("s_silu")
    s_prod = sem("s_prod")
    s_turn = sem("s_turn")
    s_ahi = sem("s_ahi")
    s_alo = sem("s_alo")
    s_down = sem("s_down")
    s_out = sem("s_out")
    ffn_sems = [s_gu, s_silu, s_prod, s_turn, s_ahi, s_alo, s_down]
    layer_sems = [PE.sem, AC.sem, VE.sem, s_pre, s_par] + ffn_sems

    for slot in range(RING):
        sp.dma_start(raw[:, slot, :], T["stream"][slot]).then_inc(s_landed[slot], 16)
    with sp.Fori(0, STREAM // RING - 1) as turn:
        for slot in range(RING):
            sp.wait_ge(s_lo, turn * RING + slot + 1)
            sp.dma_start(raw[:, slot, :], T["stream"][(turn + 1) * RING + slot]).then_inc(s_landed[slot], 16)
    with pool.Fori(0, STREAM // RING) as turn:
        for slot in range(RING):
            pool.wait_ge(s_hi, turn * RING + slot + 1)
            pool.tensor_tensor(lo[:, slot, :], raw[:, slot, :], f32(hi[:, slot, :]),
                               ALU.subtract).then_inc(s_lo, 1)

    def round_piece(first, c):
        slot = c % RING
        act.wait_ge(s_landed[slot], first * (16 // RING) + 16 * (c // RING + 1))
        act.activation(hi[:, slot, :], raw[:, slot, :], ACT.Copy).then_inc(s_hi, 1)

    def next_piece(first, c):
        act.wait_ge(s_used, first + c + 1)
        round_piece(first, c + AHEAD)
        pe.wait_ge(s_lo, first + c + 1)
        return c % RING

    def product(out, lhs_hi, lhs_lo, rhs_hi, rhs_lo, start, stop):
        pe.matmul(out, lhs_hi, rhs_hi, start=start, stop=False)
        pe.matmul(out, lhs_hi, rhs_lo, start=False, stop=False)
        return pe.matmul(out, lhs_lo, rhs_hi, start=False, stop=stop)

    def strip(first, c, a_hi, a_lo, bank, between=None, parts=None):
        for j in range(4):
            slot = next_piece(first, c + j)
            PE.after(*(parts[j:j + 1] if parts else ()))
            for i in range(2):
                k = 2 * j + i
                for m in range(MT):
                    w = slice(i * 512, i * 512 + 512)
                    last = product(psum[:, bank + m, :], a_hi[:, k, m * P:m * P + P], a_lo[:, k, m * P:m * P + P],
                                   hi[:, slot, w], lo[:, slot, w], k == 0, k == KD - 1)
            last.then_inc(s_used, 1)
            if between and j < 3:
                between()
        return At(s_used, first + (c + 4 + 1))

    def rows(first, c, kt, a_hi, a_lo, bank, start, stop):
        slot = next_piece(first, c)
        for m in range(MT):
            for n in range(2):
                w = slice(n * 512, n * 512 + 512)
                last = product(psum[:, bank + 2 * m + n, :], a_hi[:, kt, m * P:m * P + P],
                               a_lo[:, kt, m * P:m * P + P], hi[:, slot, w], lo[:, slot, w], start, stop)
        last.then_inc(s_used, 1)
        return At(s_used, first + (c + 1 + 1))

    def last_rows(first, c, kt, n_kt, a_hi, a_lo, bank, after_first):
        next_piece(first, c)
        for m in range(MT):
            for i in range(n_kt):
                slot = (c + i) % RING
                if m == 0 and i:
                    pe.wait_ge(s_lo, first + c + i + 1)
                for n in range(2):
                    w = slice(n * 512, n * 512 + 512)
                    last = product(psum[:, bank + 2 * m + n, :], a_hi[:, kt + i, m * P:m * P + P],
                                   a_lo[:, kt + i, m * P:m * P + P], hi[:, slot, w], lo[:, slot, w],
                                   False, i == n_kt - 1)
                if m:
                    last.then_inc(s_used, 1)
            if m == 0:
                after_first(PE.step(last))
                for i in range(1, n_kt):
                    act.wait_ge(s_used, first + c + i + 1)
                    round_piece(first, c + i + AHEAD)
        return At(s_used, first + (c + n_kt + 1))

    def exp_and_ln():
        act.preload_act_table_set("natural_log_exp_and_others")

    def rsqrt(v, t, y, *ready):
        s = AC.step(AC.after(*ready).activation(t, v, ACT.Ln))
        s = AC.step(AC.after(s).activation(y, t, ACT.Exp, scale=-0.5))
        s = VE.step(VE.after(s, *ready).tensor_tensor(t, y, y, ALU.mult))
        s = VE.step(VE.after(s).tensor_tensor(t, t, v, ALU.mult))
        s = VE.step(VE.after(s).tensor_scalar(t, t, -0.5, 1.5, ALU.mult, ALU.add))
        return VE.step(VE.after(s).tensor_tensor(y, y, t, ALU.mult))

    small_at = [0]

    def cell(n):
        small_at[0] += n
        assert small_at[0] <= 512, small_at
        return small[:, small_at[0] - n:small_at[0]]

    def row_scale(src, scratch, cells, *ready):
        exp_and_ln()
        ss, t, y = cells
        for m in range(MT):
            s = AC.step(AC.after(*ready).activation(scratch[:, m, :], src[:, m, :], ACT.Square,
                                                    accum_out=ss[:, m:m + 1]))
        s = VE.step(VE.after(s).tensor_scalar(ss, ss, 1.0 / D, EPS, ALU.mult, ALU.add))
        return rsqrt(ss, t, y, s)

    def to_features(src, gain, out_hi, out_lo, banks, done):
        parts, turned = [], {}
        for m in range(MT):
            for pair, bank in enumerate(banks):
                pe_ = PE.after(*done[m])
                for i in range(2):
                    k = 2 * pair + i
                    t = pe_.transpose(psum[:, bank, i * S + m * P:i * S + m * P + P], src[:, m, k * P:k * P + P],
                                      ident)
                turned[pair] = PE.step(t) if m else None
        for pair, bank in enumerate(banks):
            kts = [(2 * pair + i, psum[:, bank, i * S:i * S + S]) for i in range(2)]
            for k, part in kts:
                a = AC.step(AC.after(turned[pair]).activation(out_hi[:, k, :], part, ACT.Copy,
                                                              scale=1.0 if gain is None else gain[:, k:k + 1]))
            for k, part in kts:
                b = VE.step(VE.after(a).scalar_tensor_tensor(out_lo[:, k, :], part,
                                                             1.0 if gain is None else gain[:, k:k + 1],
                                                             f32(out_hi[:, k, :]), ALU.mult, ALU.subtract))
            parts.append(b)
        return parts

    def add_norm(gain, bank, m, *ready):
        f = psum[:, bank + 2 * m:bank + 2 * m + 2, :].rearrange("p a b -> p (a b)")
        ss, v, t, y = (c_[:, m:m + 1] for c_ in f_cells)
        s = AC.step(AC.after(*ready).activation(work_sq[:, m, :], f, ACT.Square, accum_out=ss))
        a = AC.step(AC.after(s).activation(t, ss, ACT.Ln, scale=1.0 / D, bias=eps))
        a = AC.step(AC.after(a).activation(y, t, ACT.Exp, scale=-0.5))
        VE.step(VE.after(s).tensor_scalar(v, ss, 1.0 / D, EPS, ALU.mult, ALU.add))
        b = VE.step(dve.tensor_tensor(work_post[:, m, :], f, gain, ALU.mult))
        s = VE.step(VE.after(a, b).scalar_tensor_tensor(t, v, y, y, ALU.mult, ALU.mult))
        s = VE.step(VE.after(s).scalar_tensor_tensor(y, t, 3.0, y, ALU.subtract, ALU.mult))
        return VE.step(VE.after(s).scalar_tensor_tensor(x[:, m, :], work_post[:, m, :], y, x[:, m, :], ALU.mult,
                                                        ALU.add))

    def add_plain(bank, m, *ready):
        f = psum[:, bank + 2 * m:bank + 2 * m + 2, :].rearrange("p a b -> p (a b)")
        return VE.step(VE.after(*ready).tensor_tensor(x[:, m, :], x[:, m, :], f, ALU.add))

    def feed_forward(first, c, strips, gated, strips_before, parts, scale, finish):
        kts = 2 if gated else 4
        width = kts * P
        pieces = 4 + kts
        per_turn = 2 if gated else 1
        act_s, prod_s = work_act[:, :, 0:width], work_prod[:, :, 0:width]

        def project(base, c, n, parts=None):
            pe.wait_ge(s_prod, n + 1)
            done = strip(base, c, h_hi, h_lo, 0, parts=parts)
            for q in (act, dve):
                q.wait_ge(done.sem, done.value)
            act.wait_ge(s_prod, n + 1)
            for m in range(MT):
                t = act.activation(act_s[:, m, :], psum[:, m, 0:width], ACT.Silu if gated else ACT.Relu,
                                   scale=scale[:, m:m + 1])
            t.then_inc(s_silu, 1)
            dve.wait_ge(s_silu, n + 1)
            dve.wait_ge(s_turn, n + 1)
            if gated:
                for m in range(MT):
                    t = dve.scalar_tensor_tensor(prod_s[:, m, :], psum[:, m, width:2 * width], scale[:, m:m + 1],
                                                 act_s[:, m, :], ALU.mult, ALU.mult)
            else:
                t = dve.tensor_tensor(prod_s, act_s, act_s, ALU.mult)
            t.then_inc(s_prod, 1)

        def down(base, c, n, start):
            pe.wait_ge(s_alo, n)
            for i in range(kts):
                rows(base, c + i, i, y_hi, y_lo, 4, start and i == 0, False)

        def turn(base, c, n):
            pe.wait_ge(s_prod, n + 2)
            for i in range(kts):
                for m in range(MT):
                    t = pe.transpose(psum[:, 2 + i // 2, (i % 2) * S + m * P:(i % 2) * S + m * P + P],
                                     prod_s[:, m, i * P:i * P + P], ident)
            t.then_inc(s_turn, 1)
            src = psum[:, 2:2 + kts // 2, :].rearrange("p a b -> p (a b)")
            high = y_hi[:, 0:kts, :].rearrange("p a b -> p (a b)")
            low = y_lo[:, 0:kts, :].rearrange("p a b -> p (a b)")
            for q in (act, dve):
                q.wait_ge(s_turn, n + 2)
                q.wait_ge(s_used, base + (c + 1))
            act.activation(high, src, ACT.Copy).then_inc(s_ahi, 1)
            dve.wait_ge(s_ahi, n + 1)
            dve.tensor_tensor(low, src, f32(high), ALU.subtract).then_inc(s_alo, 1)

        n0 = strips_before
        project(first, c, n0, parts)
        turn(first, c + 4, n0)
        project(first, c + 4, n0 + 1)
        down(first, c + 8, n0 + 1, True)
        turn(first, c + 8 + kts, n0 + 1)
        left = strips - 2
        c += 8 + kts
        whole = left // per_turn
        if whole:
            with nc.Fori(0, whole, engines=three) as i:
                base = first + i * (pieces * per_turn)
                for j in range(per_turn):
                    n = i * per_turn + (n0 + 2 + j)
                    cj = c + j * pieces
                    project(base, cj, n)
                    down(base, cj + 4, n, False)
                    turn(base, cj + pieces, n)
        c += whole * per_turn * pieces
        for j in range(left - whole * per_turn):
            n = n0 + 2 + whole * per_turn + j
            project(first, c, n)
            down(first, c + 4, n, False)
            turn(first, c + pieces, n)
            c += pieces
        if gated:
            exp_and_ln()
        pe.wait_ge(s_alo, n0 + strips)
        done = []
        end = last_rows(first, c, 0, kts, y_hi, y_lo, 4, lambda end: done.append((finish(0, end),)))
        done.append((finish(1, end),))
        return done

    SCORE, TURNED, OUT = (4, 5), 6, 7
    score_read, prob_read, pt_read = {}, {}, {}
    bank_read = {TURNED: (), OUT: ()}

    def pipeline(units):
        states = [None] * len(units)
        for i in range(len(units) + 2):
            if 0 <= i - 2:
                units[i - 2][2]((i - 2) % 2, states[i - 2])
            if 0 <= i - 1 < len(units):
                states[i - 1] = units[i - 1][1]((i - 1) % 2, states[i - 1])
            if i < len(units):
                states[i] = units[i][0](i % 2)
            yield

    stat = [[cell(8) for _ in range(6)] for _ in range(2)]

    def softmax_parts(slot, products, ready, tables, segments, row_tiles=False):
        bank, prob = SCORE[slot], soft[:, slot, 0, :]
        mn, total, inverse = stat[slot][0:3]
        pe_ = PE.after(*ready, *score_read.get(slot, ()))
        t = None
        for lhsT, rhs, col, width in products:
            if t and row_tiles:
                PE.after(t)
            t = PE.step(pe_.matmul(psum[:, bank, col:col + width], lhsT, rhs, start=True, stop=True))
        for i, ((col, width), table) in enumerate(zip(segments, tables)):
            w = slice(col, col + width)
            a = VE.step(VE.after(t, *prob_read.get(slot, ())).tensor_tensor_reduce(
                prob[:, w], psum[:, bank, w], table, 1.0, HUGE, ALU.add, ALU.min, mn[:, i:i + 1])) \
                if table is not None else VE.step(VE.after(t, *prob_read.get(slot, ())).tensor_scalar(
                    prob[:, w], psum[:, bank, w], 0.0, HUGE, ALU.add, ALU.min, accum_out=mn[:, i:i + 1]))
            s = AC.step(AC.after(a).activation(prob[:, w], prob[:, w], ACT.Exp, scale=-1.0, bias=mn[:, i:i + 1],
                                               accum_out=total[:, i:i + 1]))
        score_read[slot] = (a,)
        return s

    def normalised(slot, s, segments, gates):
        prob = soft[:, slot, 0, :]
        total, inverse = stat[slot][1:3]
        n = len(segments)
        r = VE.step(VE.after(s).reciprocal(inverse[:, 0:n], total[:, 0:n]))
        for i, (col, width) in enumerate(segments):
            w = slice(col, col + width)
            r2 = VE.step(VE.after(r).tensor_scalar(prob[:, w], prob[:, w], inverse[:, i:i + 1],
                                                   gates[i] if gates else None, ALU.mult,
                                                   ALU.mult if gates else ALU.bypass))
        return r2

    def turn_blocks(slot, ready, cols):
        pe_ = PE.after(ready, *bank_read[TURNED])
        for i, col in enumerate(cols):
            t = pe_.transpose(psum[:, TURNED, i * P:i * P + P], soft[:, slot, 0, col:col + P], ident)
        t = PE.step(t)
        prob_read[slot] = (t,)
        n = len(cols) * P
        a = VE.step(VE.after(t, *pt_read.get(slot, ())).tensor_copy(soft[:, slot, 1, 0:n], psum[:, TURNED, 0:n]))
        bank_read[TURNED] = (a,)
        return a

    def split_out(src, high, low, t):
        a = AC.step(AC.after(t).activation(high, src, ACT.Copy))
        b = VE.step(VE.after(t, a).tensor_tensor(low, src, f32(high), ALU.subtract))
        return b

    def causal_out(slot, pt, base, v, col, start=True, stop=True):
        probs = soft[:, slot, 1, :]
        out = psum[base:base + 64, OUT, col:col + S]
        pe.matmul(out[:, 0:P], v[:, 0, :], probs[:, 0:P], start=start, stop=stop, skip_group_check=True)
        pe.matmul(out[:, P:S], v[:, 0, :], probs[:, P:2 * P], start=start, stop=False, skip_group_check=True)
        return pe.matmul(out[:, P:S], v[:, 1, :], probs[:, 2 * P:3 * P], start=False, stop=stop,
                         skip_group_check=True)

    SEG = [(0, P), (P, S)]
    BLOCKS = [0, P, 2 * P]

    def turn_qk(z, jobs, ready):
        for n, (col, target, scale) in enumerate(jobs):
            bank = SCORE[n % 2]
            pe_ = PE.after(*ready, *score_read.get(n % 2, ()))
            for m in range(MT):
                t = pe_.transpose(psum[:, bank, m * P:m * P + P], z[:, m, col:col + P], ident)
            t = PE.step(t)
            a = AC.step(AC.after(t).activation(target, psum[:, bank, 0:S], ACT.Copy, scale=scale))
            score_read[n % 2] = (a,)
        return a

    def take_out(dst, bank, end, by_act, y, *ready):
        for m in range(MT):
            src = psum[:, bank + m, 0:dst.shape[2]]
            if by_act:
                s = AC.step(AC.after(end, *ready).activation(dst[:, m, :], src, ACT.Copy, scale=y[:, m:m + 1]))
            else:
                s = VE.step(VE.after(end, *ready).tensor_scalar(dst[:, m, :], src, y[:, m:m + 1], None, ALU.mult))
        return s

    def load(target, source, s=None, **how):
        act.dma_start(target, source, **how).then_inc(s or s_par, 16)
        loads[0] += not s

    loads = [0]
    x_cells = (cell(2), cell(2), cell(2))
    scale = x_cells[2]
    f_cells = (cell(2), cell(2), cell(2), cell(2))
    eps = cell(1)
    work_sq = big[:, 2048:4096].rearrange("p (m d) -> p m d", m=MT)
    work_act = big[:, 0:1024].rearrange("p (m d) -> p m d", m=MT)
    work_prod = big[:, 1024:2048].rearrange("p (m d) -> p m d", m=MT)
    work_post = big[:, 4096:6144].rearrange("p (m d) -> p m d", m=MT)

    s_const = sem("s_const")
    load(consts[:, :], T["consts"], s_const)
    load(x[:, :, :], T["x"].rearrange("b (m p) d -> p (b m) d", p=P), s_const)
    load(special[:, 0:1024], T["special1"], s_const)
    for c in range(AHEAD):
        round_piece(0, c)
    for queue in (PE, AC, VE):
        queue.engine.wait_ge(s_const, 48)

    def start_counts():
        act.sem_inc(s_prod, 1)
        act.sem_inc(s_turn, 1)

    def end_layer():
        nc.multi_engine_barrier(three)
        for one in layer_sems:
            act.sem_clear(one)
        start_counts()
        nc.multi_engine_barrier(three)
        for queue in (PE, AC, VE):
            queue.restart()
        for reads in (score_read, prob_read, pt_read):
            reads.clear()
        bank_read[TURNED] = bank_read[OUT] = ()
        loads[0] = 0

    dve.memset(eps, EPS)
    loads[0] = 0
    act.sem_inc(s_used, 1)
    start_counts()
    nc.multi_engine_barrier(three)

    z1 = big[:, 0:6144].rearrange("p (m c) -> p m c", m=MT)
    post = [big[:, 6144 + 1024 * i:7168 + 1024 * i] for i in range(3)]
    band = big[:, 9216:10752].rearrange("p (h k) -> p h k", h=NA)
    alibi = special[:, 0:1024].rearrange("p (h k) -> p h k", h=NB)
    pre1 = special[:, 1024:1048].rearrange("p (i k) -> p i k", i=3)
    lam_in = special[:, 1056:1056 + 128].rearrange("p (i k) -> p i k", i=4)
    lam_c = special[:, 1184:1186]
    subln = special[:, 1216:1280]
    lam_t = special[:, 1280:1312]
    ob = special[:, 1536:2048]
    ob2 = special[:, 2048:2560]
    lb = [special[:, 2560 + 384 * i:2944 + 384 * i] for i in range(2)]
    lams = cell(8)
    c_ratio = [cell(2), cell(2)]
    r0 = cell(8)
    ob_s, ob_t, ob_y = cell(8), cell(8), cell(8)

    with nc.Fori(0, L, engines=three) as layer:
        first = layer * PIECES1
        load(pre1, T["pre1"][layer], s_pre)
        load(lam_in, T["lams"][layer].partition_broadcast(P))
        load(lam_c, T["lam_const"][layer].partition_broadcast(P))
        load(subln, T["subln"][layer].partition_broadcast(P))
        for i in range(3):
            load(post[i], T["post1"][layer, i].partition_broadcast(P))
        load(band, T["band"][layer])
        for queue in (AC, VE):
            queue.engine.wait_ge(s_pre, 16)

        parts = to_features(x, pre1[:, 0, :], h_hi, h_lo, (2, 3, 4, 5), ((), ()))
        AC.after(row_scale(x, work_sq, x_cells))
        dve.wait_ge(s_par, 16 * loads[0])
        for i, weight in enumerate((0.5, 1.0, 0.5)):
            post_ready = VE.step(dve.tensor_scalar(post[i], post[i], weight / -2, None, ALU.mult))
        VE.after(post_ready)
        done = feed_forward(first, 0, FFN_STRIPS, True, 0, parts, scale, lambda m, end: add_norm(post[0], 4, m, end))

        parts = to_features(x, pre1[:, 1, :], h_hi, h_lo, (2, 3, 4, 5), done)
        x_scale = row_scale(x, work_sq, x_cells, *done[1])
        s = VE.step(dve.tensor_scalar(band, band, -1.0, None, ALU.mult))
        band_ready = VE.step(VE.after(s).memset(band[0:64, :, 192:256], BIG))
        for i in range(2):
            s = VE.step(VE.after(s).tensor_tensor_reduce(lam_t, lam_in[:, 2 * i, :], lam_in[:, 2 * i + 1, :], 1.0,
                                                 0.0, ALU.mult, ALU.add, lams[:, i:i + 1]))
        s = AC.step(AC.after(s).activation(lams[:, 2:4], lams[:, 0:2], ACT.Exp))
        s = VE.step(VE.after(s).tensor_tensor(lams[:, 4:5], lams[:, 3:4], lams[:, 2:3], ALU.subtract))
        lam_ready = VE.step(VE.after(s).tensor_tensor(lams[:, 5:6], lams[:, 4:5], lam_c[:, 0:1], ALU.subtract))
        minus_lam = lams[:, 5:6]
        gain_ready = VE.step(dve.tensor_scalar(subln, subln, lam_c[:, 1:2], None, ALU.mult))

        done = {}


        def diff_units():
            units = []
            for h in range(NB):
                for m in range(MT):
                    def score(slot, h=h, m=m):
                        keys = (m + 1) * P
                        prods, segs = [], []
                        for j in range(2):
                            rows_ = slice(32 * (2 * (h % 2) + j), 32 * (2 * (h % 2) + j) + 32)
                            prods.append((qT[rows_, h // 2, m * P:m * P + P], kT[rows_, h // 2, 0:keys],
                                          j * S, keys))
                            segs.append((j * S, keys))
                        table = alibi[:, h, (1 - m) * P:(1 - m) * P + keys]
                        s = softmax_parts(slot, prods, (diff_qk[0],), [table] * 2, segs, True)
                        total, inverse = stat[slot][1:3]
                        r = VE.step(VE.after(s).reciprocal(inverse[:, 0:2], total[:, 0:2]))
                        c1 = VE.step(VE.after(r, lam_ready).scalar_tensor_tensor(
                            c_ratio[slot][:, 0:1], total[:, 0:1], inverse[:, 1:2], minus_lam, ALU.mult, ALU.mult))
                        VE.step(VE.after(r).tensor_copy(r0[:, 4 * m + h:4 * m + h + 1], inverse[:, 0:1]))
                        prob = soft[:, slot, 0, :]
                        return VE.step(VE.after(c1).scalar_tensor_tensor(
                            prob[:, 0:keys], prob[:, S:S + keys], c_ratio[slot][:, 0:1], prob[:, 0:keys],
                            ALU.mult, ALU.add))

                    def turn(slot, s, m=m):
                        return turn_blocks(slot, s, [P * i for i in range(m + 1)])

                    def out(slot, s, h=h, m=m):
                        pe_ = PE.after(s, *bank_read[OUT])
                        for i in range(m + 1):
                            t = pe_.matmul(psum[:, OUT, (4 * m + h) * 64:(4 * m + h) * 64 + 64],
                                           soft[:, slot, 1, i * P:i * P + P],
                                           z1[:, i, QKV_B + 512 + 64 * h:QKV_B + 576 + 64 * h],
                                           start=i == 0, stop=i == m, skip_group_check=True)
                        t = PE.step(t)
                        pt_read[slot] = (t,)
                        last_out[0] = t

                    units.append((score, turn, out))
            return units

        last_out, diff_qk, y_done = [None], [None], []

        def diff():
            diff_qk[0] = turn_qk(z1, [(QKV_B + 128 * i, qT[:, i, :], -32.0 ** -0.5) for i in range(2)]
                                 + [(QKV_B + 256 + 128 * i, kT[:, i, :], 1.0) for i in range(2)],
                                 (done[0], done[1]))
            yield
            yield from pipeline(diff_units())
            o3 = ob.rearrange("p (g d) -> p g d", d=64)
            q3 = ob2.rearrange("p (g d) -> p g d", d=64)
            s = VE.step(VE.after(last_out[0]).tensor_tensor(
                o3, psum[:, OUT, :].rearrange("p (g d) -> p g d", d=64), r0.unsqueeze(2).broadcast_to((P, 8, 64)),
                ALU.mult))
            bank_read[OUT] = (s,)
            s = VE.step(VE.after(s).tensor_tensor(q3, o3, o3, ALU.mult))
            s = VE.step(VE.after(s).tensor_reduce(ob_s, q3, AX.X, ALU.add))
            s = VE.step(VE.after(s).tensor_scalar(ob_s, ob_s, 1.0 / 64, EPS, ALU.mult, ALU.add))
            s = rsqrt(ob_s, ob_t, ob_y, s)
            yield
            s = VE.step(VE.after(s).tensor_tensor(o3, o3, ob_y.unsqueeze(2).broadcast_to((P, 8, 64)), ALU.mult))
            s = VE.step(VE.after(s, gain_ready).tensor_tensor(o3, o3, subln.unsqueeze(1).broadcast_to((P, 8, 64)),
                                                              ALU.mult))
            yield
            pe_ = PE.after(s, *bank_read[TURNED])
            for i in range(2):
                for m in range(MT):
                    t = pe_.transpose(psum[:, TURNED, i * S + m * P:i * S + m * P + P],
                                      ob[:, m * S + i * P:m * S + i * P + P], ident)
            t = PE.step(t)
            s = split_out(psum[:, TURNED, :], y_hi[:, 3:5, :].rearrange("p a b -> p (a b)"),
                          y_lo[:, 3:5, :].rearrange("p a b -> p (a b)"), t)
            bank_read[TURNED] = (s,)
            y_done.append(s)
            yield

        def head_units(col, kind, ready):
            units = []
            for h in range(6):
                half = slice(64 * (h % 2), 64 * (h % 2) + 64)
                q, k = qT[half, h // 2, :], kT[half, h // 2, :]
                v = z1[:, :, col + 768 + 64 * h:col + 832 + 64 * h]

                def band_score(slot, h=h, q=q, k=k):
                    prods = [(q[:, 0:P], k[:, 0:P], 0, P), (q[:, P:S], k, P, S)]
                    s = softmax_parts(slot, prods, ready, [band[:, h, P:S], band[:, h, :]], SEG)
                    return normalised(slot, s, SEG, None)

                def stick_score(slot, q=q, k=k):
                    bank = SCORE[slot]
                    zt = psum[:, bank, 0:384]
                    a_ = soft[:, slot, 0, 0:384]
                    pe_ = PE.after(*ready, *score_read.get(slot, ()))
                    pe_.matmul(psum[:, bank, 0:S], k[:, 0:P], q, start=True, stop=True)
                    t = PE.step(pe_.matmul(psum[:, bank, S:384], k[:, P:S], q[:, P:S], start=True, stop=True))
                    s = AC.step(AC.after(t, *prob_read.get(slot, ())).activation(a_, zt, ACT.Abs))
                    s = AC.step(AC.after(s).activation(a_, a_, ACT.Exp, scale=-1.0))
                    s = AC.step(AC.after(s).activation(a_, a_, ACT.Ln, bias=1.0))
                    s = VE.step(VE.after(s, *pt_read.get(slot, ())).scalar_tensor_tensor(
                        lb[slot], zt, 0.0, a_, ALU.min, ALU.subtract))
                    s = VE.step(VE.after(s).tensor_tensor(a_, lb[slot], zt, ALU.subtract))
                    score_read[slot] = (s,)
                    for c_ in (0, S):
                        s2 = VE.step(VE.after(s).tensor_tensor(a_[:, c_:c_ + P], a_[:, c_:c_ + P], strict, ALU.mult))
                    return s2

                def stick_turn(slot, s):
                    a_ = soft[:, slot, 0, 0:384]
                    pe_ = PE.after(s, *bank_read[TURNED])
                    pe_.matmul(psum[:, TURNED, 0:384], tri, a_, start=True, stop=False, skip_group_check=True)
                    t = PE.step(pe_.matmul(psum[:, TURNED, P:S], ones, a_[:, S:384], start=False, stop=True,
                                           skip_group_check=True))
                    prob_read[slot] = (t,)
                    w = soft[:, slot, 1, 0:384]
                    s = VE.step(VE.after(t, *pt_read.get(slot, ())).tensor_tensor(w, lb[slot], psum[:, TURNED, 0:384],
                                                                                  ALU.add))
                    bank_read[TURNED] = (s,)
                    s = AC.step(AC.after(s).activation(w, w, ACT.Exp))
                    for c_ in (0, S):
                        s2 = VE.step(VE.after(s).tensor_tensor(w[:, c_:c_ + P], w[:, c_:c_ + P], strict, ALU.mult))
                    return s2

                def out(slot, s, h=h, v=v):
                    col_ = S * (h // 2 % 2)
                    PE.after(s, *(bank_read[OUT] if h % 2 == 0 else ()))
                    t = PE.step(causal_out(slot, s, 64 * (h % 2), v, col_))
                    pt_read[slot] = (t,)
                    if h % 2:
                        kt = (0 if kind == "band" else 5) + h // 2
                        s = split_out(psum[:, OUT, col_:col_ + S], y_hi[:, kt, :], y_lo[:, kt, :], t)
                        bank_read[OUT] = (s,)
                        y_done.append(s)

                if kind == "band":
                    units.append((band_score, lambda slot, s: turn_blocks(slot, s, BLOCKS), out))
                else:
                    units.append((stick_score, stick_turn, out))
            return units

        def heads(col, kind, strips_):
            s = turn_qk(z1, [(col + 128 * i, qT[:, i, :], -0.125 if kind == "band" else 0.125) for i in range(3)]
                        + [(col + 384 + 128 * i, kT[:, i, :], 1.0) for i in range(3)],
                        [done[i] for i in strips_])
            yield
            yield from pipeline(head_units(col, kind, (s, band_ready)))

        work = []

        def between():
            while work:
                try:
                    next(work[0])
                    return
                except StopIteration:
                    work.pop(0)

        c = FFN_PIECES
        for i in range(COLS1 // 512):
            bank = 2 * (i % 2)
            PE.after(*([done[i - 2]] if i > 1 else []))
            end = strip(first, c, h_hi, h_lo, bank, between, None if i else parts)
            done[i] = take_out(z1[:, :, i * 512:i * 512 + 512], bank, end, i % 2, scale, x_scale)
            c += 4
            if i == 1:
                work.append(diff())
            if i == 3:
                work.append(heads(QKV_A, "band", (1, 2, 3)))
            if i == 5:
                work.append(heads(QKV_C, "stick", (3, 4, 5)))
            between()
        while work:
            between()
        PE.after(*y_done)
        for i in range(KD - 2):
            rows(first, c + i, i, y_hi, y_lo, 0, i == 0, False)
        x_done = []
        end = last_rows(first, c + KD - 2, KD - 2, 2, y_hi, y_lo, 0,
                        lambda end: x_done.append((add_norm(post[1], 0, 0, end),)))
        x_done.append((add_norm(post[1], 0, 1, end),))
        c += KD

        parts = to_features(x, pre1[:, 2, :], h_hi, h_lo, (4, 5, 6, 7), x_done)
        s = row_scale(x, work_sq, x_cells, *x_done[1])
        AC.after(s)
        VE.after(s)
        feed_forward(first, c, FFN_STRIPS, True, FFN_STRIPS, parts, scale, lambda m, end: add_norm(post[2], 4, m, end))
        assert c + FFN_PIECES == PIECES1
        end_layer()

    masks = special[:, 0:1024].rearrange("p (i q) -> p i q", i=8)
    b_merge = special[:, 1024:4096]
    gain12 = special[:, 4096:4864]
    gla_gain = special[:, 4864:4992]
    w2 = special[:, 4992:5248].rearrange("p (k e d) -> p k e d", k=2, e=2)
    w_gate = special[0:16, 5248:5504]
    pe_rows = special[:, 5504:5536].rearrange("p (k j) -> p k j", k=2)
    pre2 = special[:, 5536:5560].rearrange("p (i k) -> p i k", i=3)
    b_gate = special[:, 5560:5562]
    mem_gain = special[:, 5568:5824].rearrange("p (i d) -> p i d", i=2)
    cmp_gain = special[0:32, 5824:5888]

    znq = big[:, 0:2048].rearrange("p (m c) -> p m c", m=MT)
    z3 = big[:, 2048:2640].rearrange("p (m c) -> p m c", m=MT)
    gqk = big[:, 2640:3664].rearrange("p (m c) -> p m c", m=MT)
    gv = big[:, 3664:4688].rearrange("p (m c) -> p m c", m=MT)
    gr = big[:, 4688:5712].rearrange("p (m c) -> p m c", m=MT)
    mq = big[:, 5712:6736].rearrange("p (m c) -> p m c", m=MT)
    merge = big[:, 6736:12880].rearrange("p (m c) -> p m c", m=MT)
    windows = [[big[:, 6736 + 512 * kv:7248 + 512 * kv]]
               + [w[:, 2 * kv:2 * kv + 2, :].rearrange("p a b -> p (a b)") for w in (y_hi, y_lo)] for kv in range(2)]
    doubled = big[:, 8784:9808]
    merged = merge[:, :, 2 * D:3 * D]
    softf = soft[:, :, :, :].rearrange("p a b c -> p (a b c)")

    vb = extra[:, 0:512]
    hid = [extra[:, 512 + 128 * i:640 + 128 * i] for i in range(3)]
    hid_rep = extra[:, 896:1152].rearrange("p (e c) -> p e c", e=2)
    kb = extra[0:32, 1152:1280]
    kbd = extra[:, 1280:1312]
    pc = extra[:, 1312:1568]
    pct = extra[:, 1568:1824]
    hid_rows = extra[0:32, 1312:1824]
    att = [pc[:, 0:128], pc[:, 128:256]]
    att_off = pct[:, 0:128]
    gates = extra[:, 1824:1872].rearrange("p (m c) -> p m c", m=MT)
    trig = extra[:, 1872:1920].rearrange("p (f m i) -> p f m i", f=2, m=3)
    glow = extra[0:16, 512:768]
    kcn = extra[0:32, 1920:1984]
    tmp32 = extra[0:32, 1984:2048]
    mn16, sum16, inv16 = cell(16), cell(16), cell(16)
    s24, t24, y24 = cell(24), cell(24), cell(24)
    s8, t8, y8 = cell(8), cell(8), cell(8)
    m_cells = (cell(2), cell(2), cell(2))
    c1_, c2_, c3_ = cell(1), cell(1), cell(1)

    pos_i = small[:, 500:503].bitcast(I32)
    pos_f = small[:, 504:507]
    assert small_at[0] <= 500
    s_rot = sem("s_rot")
    s = VE.step(dve.memset(small[:, 500:503], 0.0))
    AC.after(s)
    for m in range(MT):
        load(pos_i[:, m:m + 1], T["positions"].rearrange("b (p o) -> p (b o)", o=1)[m * P:m * P + P, :], s_rot)
    ends = T["positions"].rearrange("b (n t) -> (b n) t", t=16)
    for g in range(2):
        load(pos_i[16 * g:16 * g + 15, 2:3], ends[1:16, 15:16], s_rot, allow_slow_non_contiguous=True)
    load(special[:, 0:1024], T["masks"], s_rot)
    dve.wait_ge(s_rot, 80)
    s = VE.step(dve.tensor_copy(pos_f, pos_i))
    ang = hid[0][:, 0:48].rearrange("p (f m i) -> p f m i", f=2, m=3)
    angf, turns, turns_i = hid[0][:, 0:48], hid[1][:, 0:48], hid[2][:, 0:48].bitcast(I32)
    for m in range(3):
        s = VE.step(VE.after(s).tensor_scalar(ang[:, 1, m, :], inv_freq, pos_f[:, m:m + 1], None, ALU.mult))
    s = VE.step(VE.after(s).tensor_copy(ang[:, 0], ang[:, 1]))
    s = VE.step(VE.after(s).tensor_scalar(turns, angf, 1.0 / (2 * math.pi), None, ALU.mult))
    s = VE.step(VE.after(s).tensor_copy(turns_i, turns))
    s = VE.step(VE.after(s).tensor_copy(turns, turns_i))
    rest = 2 * math.pi - 6.28125
    c_mid = float(np.float32(np.round(rest * 2 ** 21) / 2 ** 21))
    for part in (6.28125, c_mid, rest - c_mid):
        s = VE.step(VE.after(s).scalar_tensor_tensor(angf, turns, -part, angf, ALU.mult, ALU.add))
    s = VE.step(VE.after(s).tensor_scalar(angf[:, 0:24], angf[:, 0:24], math.pi / 2, None, ALU.add))
    for _ in range(2):
        s = VE.step(VE.after(s).tensor_scalar(turns, angf, math.pi, -2 * math.pi, ALU.is_gt, ALU.mult))
        s = VE.step(VE.after(s).tensor_tensor(angf, angf, turns, ALU.add))
        s = VE.step(VE.after(s).tensor_scalar(turns, angf, -math.pi, 2 * math.pi, ALU.is_lt, ALU.mult))
        s = VE.step(VE.after(s).tensor_tensor(angf, angf, turns, ALU.add))
    s = VE.step(VE.after(s).tensor_scalar(angf, angf, 3.1415925, -3.1415925, ALU.min, ALU.max))
    s = AC.step(AC.after(s).activation(extra[:, 1872:1920], angf, ACT.Sin))
    end_layer()

    def rotate(q4, heads_n, cos, sin, tmps, s):
        x1, x2 = q4[..., 0:8], q4[..., 8:16]
        for tmp, a_, b_ in ((tmps[0], x1, cos), (tmps[1], x2, sin), (tmps[2], x2, cos), (tmps[3], x1, sin)):
            s2 = VE.step(VE.after(s).tensor_tensor(tmp, a_, b_, ALU.mult))
        s = VE.step(VE.after(s2).tensor_tensor(x1, tmps[0], tmps[1], ALU.subtract))
        return VE.step(VE.after(s).tensor_tensor(x2, tmps[2], tmps[3], ALU.add))

    def head_norm(flat, groups, width, scratch, cells, gain, *ready):
        v3 = flat.rearrange("p (g d) -> p g d", d=width)
        sq, t_, y_ = (c_[:, 0:groups] for c_ in cells)
        s = AC.step(AC.after(*ready).activation(scratch, flat, ACT.Square))
        s = VE.step(VE.after(s, *ready).tensor_reduce(sq, scratch.rearrange("p (g d) -> p g d", d=width), AX.X, ALU.add))
        s = VE.step(VE.after(s).tensor_scalar(sq, sq, 1.0 / width, EPS, ALU.mult, ALU.add))
        s = rsqrt(sq, t_, y_, s)
        s = VE.step(VE.after(s).tensor_tensor(v3, v3, y_.unsqueeze(2).broadcast_to((P, groups, width)), ALU.mult))
        if gain is None:
            return s
        return VE.step(VE.after(s).tensor_tensor(v3, v3, gain.unsqueeze(1).broadcast_to((P, groups, width)),
                                                 ALU.mult))

    with nc.Fori(0, L, engines=three) as layer:
        first = layer * PIECES2 + L * PIECES1
        load(memkv[:, :, :], T["mem"].rearrange("b (m p) d -> p (b m) d", p=P), s_pre)
        load(pre2, T["pre2"][layer], s_pre)
        for target, name in ((w2, "w2"), (w_gate, "w_gate"), (pe_rows, "pe"), (b_gate, "b_gate")):
            load(target, T[name][layer])
        for target, name in ((b_merge, "b_merge"), (gain12, "gain12"), (gla_gain, "gla_gain"),
                             (mem_gain, "mem_gain")):
            load(target, T[name][layer].partition_broadcast(P))
        load(cmp_gain, T["cmp_gain"][layer].partition_broadcast(32))
        for queue in (PE, AC, VE):
            queue.engine.wait_ge(s_pre, 32)

        parts = to_features(memkv, pre2[:, 2, :], y_hi, y_lo, (4, 5, 6, 7), ((), ()))
        m_scale = row_scale(memkv, big[:, 0:2048].rearrange("p (m d) -> p m d", m=MT), m_cells)
        c = 0
        end = strip(first, c, y_hi, y_lo, 0, parts=parts)
        mk = take_out(memkv[:, :, 0:512], 0, end, False, m_cells[2], m_scale)
        parts = to_features(x, pre2[:, 0, :], h_hi, h_lo, (4, 5, 6, 7), ((), ()))
        x_scale = row_scale(x, work_sq, x_cells)
        end = strip(first, c + 4, y_hi, y_lo, 2)
        mv = take_out(memkv[:, :, 512:1024], 2, end, False, m_cells[2], m_scale)
        c += 8
        for queue in (PE, VE):
            queue.engine.wait_ge(s_par, 16 * loads[0])
        s = VE.step(dve.tensor_scalar(gain12[:, 0:512], gain12[:, 0:512], -0.125, None, ALU.mult))
        gain_ready = VE.step(VE.after(s).tensor_scalar(mem_gain[:, 0, :], mem_gain[:, 0, :], -128.0 ** -0.5, None,
                                                       ALU.mult))

        y_done = {b: [] for b in range(3)}
        got = {}

        def mem_attention():
            s = head_norm(mq.rearrange("p m c -> p (m c)"), 8, P, softf[:, 0:1024], (s8, t8, y8), mem_gain[:, 0, :],
                          got["mq"], got["nsa"], gain_ready)
            yield
            kk = memkv[:, :, 0:512]
            for m in range(MT):
                s = head_norm(kk[:, m, :], 4, P, softf[:, 0:512], (s8, t8, y8), mem_gain[:, 1, :], mk, s)
            yield
            s = turn_qk(mq, [(P * h, qT[:, h, :], 1.0) for h in range(4)], (s,))
            yield
            s = turn_qk(memkv, [(P * h, kT[:, h, :], 1.0) for h in range(4)], (s,))
            yield
            segs = [(0, S), (S, S)]
            units = []
            for h in range(4):
                def score(slot, h=h, s=s):
                    prods = [(qT[:, h, m * P:m * P + P], kT[:, h, :], m * S, S) for m in range(MT)]
                    return normalised(slot, softmax_parts(slot, prods, (s,), [None, None], segs), segs, None)

                def turn(slot, s):
                    return turn_blocks(slot, s, [0, S, P, S + P])

                def out(slot, s, h=h):
                    pe_ = PE.after(s, *bank_read[OUT])
                    for k in range(2):
                        t = pe_.matmul(psum[:, OUT, 0:S], memkv[:, k, 512 + P * h:640 + P * h],
                                       soft[:, slot, 1, k * S:k * S + S], start=k == 0, stop=k == 1)
                    t = PE.step(t)
                    pt_read[slot] = (t,)
                    s = split_out(psum[:, OUT, 0:S], y_hi[:, 8 + h, :], y_lo[:, 8 + h, :], t)
                    bank_read[OUT] = (s,)
                    y_done[2].append(s)

                units.append((score, turn, out))
            PE.after(mv)
            yield from pipeline(units)

        def nsa_prep():
            idle = [r for reads in (prob_read, pt_read) for v_ in reads.values() for r in v_]
            sq = softf[:, 0:1536]
            z4 = znq[:, :, 0:768]
            s = got["nq"]
            ready = (s, got["nk"], gain_ready, *idle)
            for m in range(MT):
                a = AC.step(AC.after(*ready).activation(sq[:, m * 768:m * 768 + 768], z4[:, m, :], ACT.Square))
            s = VE.step(VE.after(a, *ready).tensor_reduce(s24, sq.rearrange("p (g d) -> p g d", d=64), AX.X, ALU.add))
            s = VE.step(VE.after(s).tensor_scalar(s24, s24, 1.0 / 64, EPS, ALU.mult, ALU.add))
            s = rsqrt(s24, t24, y24, s)
            yield
            for m in range(MT):
                v3 = z4[:, m, :].rearrange("p (h d) -> p h d", d=64)
                s2 = VE.step(VE.after(s).tensor_tensor(
                    v3, v3, y24[:, 12 * m:12 * m + 12].unsqueeze(2).broadcast_to((P, 12, 64)), ALU.mult))
            for m in range(MT):
                s = VE.step(VE.after(s2).tensor_tensor(z4[:, m, :], z4[:, m, :], gain12, ALU.mult))
            yield
            for m in range(MT):
                q4 = z4[:, m, :].rearrange("p (h d) -> p h d", d=64)
                cos, sin = (trig[:, f, m, :].unsqueeze(1).broadcast_to((P, 12, 8)) for f in range(2))
                tmps = [softf[:, 96 * i:96 * i + 96].rearrange("p (h d) -> p h d", h=12) for i in range(4)]
                s = rotate(q4, 12, cos, sin, tmps, s)
            got["nsa"] = s
            yield
        def make_windows():
            d6 = doubled.rearrange("p (m k g r d) -> p m k g r d", m=MT, k=2, g=2, r=2)
            src = znq[:, :, 768:1024].rearrange("p m (k g d) -> p m k g d", k=2, g=2)
            for m in range(MT):
                for k in range(2):
                    for r in range(2):
                        s = VE.step(VE.after(got["nk"]).tensor_copy(d6[:, m, k, :, r, :], src[:, m, k]))
            got["doubled"] = s
            yield
            for kv in range(2):
                got["windows"] = windows_of(kv)
                yield

        def windows_of(kv):
            bank = SCORE[kv]
            pe_ = PE.after(got["doubled"], *score_read.get(kv, ()))
            for g in range(2):
                for m in range(MT):
                    col = ((m * 2 + kv) * 2 + g) * 128
                    t = pe_.transpose(psum[:, bank, g * S + m * P:g * S + m * P + P], doubled[:, col:col + 128], ident)
            t = PE.step(t)
            rows_, high, low = windows[kv]
            whole = rows_.rearrange("p (j g n) -> p j g n", j=16, g=2)
            z_ = VE.step(VE.after(t).memset(rows_, 0.0))
            for g in range(2):
                ps4 = psum[:, bank, g * S:g * S + S].rearrange("p (n j r) -> p r j n", j=8, r=2)
                for par in range(2):
                    for half in range(2):
                        pr = slice(64 * par, 64 * par + 64)
                        src = ps4[pr, par, :, half:half + 15]
                        a = VE.step(VE.after(z_).tensor_tensor(
                            whole[pr, 8 * half:8 * half + 8, g, 0:15], src,
                            pe_rows[pr, kv, 8 * half:8 * half + 8].unsqueeze(2).broadcast_to((64, 8, 15)), ALU.add))
            score_read[kv] = (a,)
            h_ = AC.step(AC.after(a).activation(high, rows_, ACT.Copy))
            return VE.step(VE.after(h_).tensor_tensor(low, rows_, f32(high), ALU.subtract))

        def compress(bank):
            nonlocal c
            PE.after(got["windows"])
            for kv in range(2):
                w_hi, w_lo = (w.rearrange("p (j n) -> p j n", j=16) for w in windows[kv][1:])
                for i in range(4):
                    slot = next_piece(first, c)
                    for jj in range(4):
                        j, cols = 4 * i + jj, slice(jj * 256, jj * 256 + 256)
                        last = product(psum[0:32, bank, kv * 256:kv * 256 + 256], w_hi[:, j, :], w_lo[:, j, :],
                                       hi[:, slot, cols], lo[:, slot, cols], j == 0, j == 15)
                    last.then_inc(s_used, 1)
                    c += 1
                    between()
            end = At(s_used, first + (c + 1))
            got["hid_rows"] = VE.step(VE.after(end).tensor_copy(hid_rows, psum[0:32, bank, :]))
            return got["hid_rows"]

        def hidden():
            h_, a_, b_ = hid
            pe_ = PE.after(got["hid_rows"], *bank_read[TURNED])
            for i in range(4):
                t = pe_.transpose(psum[:, TURNED, 32 * i:32 * i + 32], hid_rows[:, i * P:i * P + P], ident[0:32, 0:32])
            t = PE.step(t)
            s = VE.step(VE.after(t).tensor_copy(h_, psum[:, TURNED, 0:128]))
            bank_read[TURNED] = (s,)
            s = VE.step(VE.after(s).tensor_tensor(a_, h_, h_, ALU.mult))
            s = VE.step(VE.after(s).tensor_scalar(a_, a_, 0.044715, 1.0, ALU.mult, ALU.add))
            s = VE.step(VE.after(s).tensor_tensor(a_, a_, h_, ALU.mult))
            s = VE.step(VE.after(s).tensor_scalar(a_, a_, -50.0, None, ALU.max))
            s = AC.step(AC.after(s).activation(a_, a_, ACT.Exp, scale=-2.0 * math.sqrt(2.0 / math.pi)))
            s = VE.step(VE.after(s).tensor_scalar(a_, a_, 1.0, None, ALU.add))
            s = VE.step(VE.after(s).reciprocal(b_, a_))
            got["hid"] = VE.step(VE.after(s).tensor_tensor(h_, h_, b_, ALU.mult))

        def nsa():
            hidden()
            yield
            h4 = hid[0].rearrange("p (k e n) -> p k e n", k=2, e=2)
            pe_ = PE.after(got["hid"], *bank_read[TURNED])
            for e in range(2):
                t = pe_.matmul(psum[0:32, TURNED, 0:64], h4[:, 0, e, :], w2[:, 0, e, :], start=e == 0, stop=e == 1)
            t = PE.step(t)
            s = VE.step(VE.after(t).tensor_copy(kcn, psum[0:32, TURNED, 0:64]))
            s = VE.step(VE.after(s).tensor_tensor_reduce(tmp32, kcn, kcn, 1.0, 0.0, ALU.mult, ALU.add, c1_[0:32, :]))
            s = VE.step(VE.after(s).tensor_scalar(c1_[0:32, :], c1_[0:32, :], 1.0 / 64, EPS, ALU.mult, ALU.add))
            s = rsqrt(c1_[0:32, :], c2_[0:32, :], c3_[0:32, :], s)
            s = VE.step(VE.after(s).scalar_tensor_tensor(kcn, kcn, c3_[0:32, 0:1], cmp_gain, ALU.mult, ALU.mult))
            s = rotate(kcn, 1, trig[0:32, 0, 2, :], trig[0:32, 1, 2, :], [tmp32[:, 8 * i:8 * i + 8] for i in range(4)],
                       s)
            kbs = VE.step(VE.after(s).tensor_tensor(
                kb.rearrange("p (g d) -> p g d", g=2), kcn.unsqueeze(1).broadcast_to((32, 2, 64)),
                own_keys.unsqueeze(2).broadcast_to((32, 2, 64)), ALU.mult))
            r_ = VE.step(VE.after(got["hid"]).tensor_copy(
                hid_rep.rearrange("p e (j n) -> p e j n", j=4),
                h4[:, 1].unsqueeze(2).broadcast_to((P, 2, 4, 32))))
            yield
            pe_ = PE.after(kbs, r_)
            pe_.transpose(psum[:, TURNED, 64:96], kb, ident[0:32, 0:32])
            for e in range(2):
                t = pe_.matmul(psum[:, SCORE[0], 0:64], hid_rep[:, e, :], w2[:, 1, e, :], start=e == 0, stop=e == 1)
            t = PE.step(t)
            s = VE.step(VE.after(t).tensor_copy(kbd, psum[:, TURNED, 64:96]))
            bank_read[TURNED] = (s,)
            s = VE.step(VE.after(t).tensor_copy(tmp_v, psum[:, SCORE[0], 0:64]))
            score_read[0] = (s,)
            s = VE.step(VE.after(s).tensor_tensor(
                vb.rearrange("p (h d) -> p h d", h=8), tmp_v.unsqueeze(1).broadcast_to((P, 8, 64)),
                own_values.unsqueeze(2).broadcast_to((P, 8, 64)), ALU.mult))
            s = VE.step(VE.after(got["z3"]).tensor_scalar(gates, z3[:, :, 256:280], -80.0, None, ALU.max))
            s = AC.step(AC.after(s).activation(gates, gates, ACT.Exp, scale=-1.0))
            s = VE.step(VE.after(s).tensor_scalar(gates, gates, 1.0, None, ALU.add))
            s = VE.step(VE.after(s).reciprocal(gates, gates))
            gates_ready = s
            yield
            sk = turn_qk(znq, [(512, kT[:, 0, :], 1.0), (640, kT[:, 1, :], 1.0)]
                         + [(P * j, qT[:, j, :], 1.0) for j in range(4)], (got["nsa"],))
            yield
            units = []

            def cmp_score(slot):
                bank = SCORE[slot]
                pe_ = PE.after(sk, s_vb[0], *score_read.get(slot, ()))
                for m in range(MT):
                    for j in range(4):
                        t = pe_.matmul(psum[:, bank, m * P + 32 * j:m * P + 32 * j + 32], qT[:, j, m * P:m * P + P],
                                       kbd, start=True, stop=True, skip_group_check=True)
                t = PE.step(t)
                g3 = lambda a, m: a[:, m * P:m * P + P].rearrange("p (h n) -> p h n", n=16)
                each = lambda a, m: a[:, 8 * m:8 * m + 8].unsqueeze(2).broadcast_to((P, 8, 16))
                tab = lambda a, m: a[:, m, :].unsqueeze(1).broadcast_to((P, 8, 16))
                for m in range(MT):
                    s = VE.step(VE.after(t).tensor_tensor(g3(pc, m), g3(psum[:, bank, :], m), tab(cmp_table, m),
                                                          ALU.add))
                score_read[slot] = (s,)
                all3 = pc.rearrange("p (h n) -> p h n", n=16)
                s = VE.step(VE.after(s).tensor_reduce(mn16, all3, AX.X, ALU.min))
                s = VE.step(VE.after(s).tensor_tensor(all3, all3, mn16.unsqueeze(2).broadcast_to((P, 16, 16)),
                                                      ALU.subtract))
                s = AC.step(AC.after(s).activation(pc, pc, ACT.Exp, scale=-1.0))
                for m in range(MT):
                    s2 = VE.step(VE.after(s).tensor_tensor(g3(pc, m), g3(pc, m), tab(cmp_valid, m), ALU.mult))
                s = VE.step(VE.after(s2).tensor_reduce(sum16, all3, AX.X, ALU.add))
                s = VE.step(VE.after(s).tensor_scalar(sum16, sum16, 1e-30, None, ALU.max))
                s = VE.step(VE.after(s).reciprocal(inv16, sum16))
                s = VE.step(VE.after(s, gates_ready).tensor_tensor(
                    inv16.rearrange("p (m h) -> p m h", m=MT), inv16.rearrange("p (m h) -> p m h", m=MT),
                    gates[:, :, 0:8], ALU.mult))
                return VE.step(VE.after(s).tensor_tensor(all3, all3, inv16.unsqueeze(2).broadcast_to((P, 16, 16)),
                                                         ALU.mult))

            def cmp_turn(slot, s):
                pe_ = PE.after(s, *bank_read[TURNED])
                for m in range(MT):
                    t = pe_.transpose(psum[:, TURNED, m * P:m * P + P], pc[:, m * P:m * P + P], ident)
                t = PE.step(t)
                s = VE.step(VE.after(t).tensor_copy(pct, psum[:, TURNED, 0:S]))
                bank_read[TURNED] = (s,)
                got["pct"] = s
                return s

            s_vb = [(VE, VE.n)]
            units.append((cmp_score, cmp_turn, lambda slot, s: None))
            for j in range(4):
                for b in range(2):
                    for g in range(2):
                        half = slice(64 * g, 64 * g + 64)

                        def score(slot, j=j, b=b, g=g, half=half):
                            q, k = qT[half, j, :], kT[half, b, :]
                            prods = [(q[:, 0:P], k[:, 0:P], 0, P), (q[:, P:S], k, P, S)]
                            s = softmax_parts(slot, prods, (sk,), [causal[:, P:S], causal], SEG)
                            VE.after(gates_ready)
                            at = (1 + b) * 8 + 2 * j + g
                            return normalised(slot, s, SEG, [gates[:, m, at:at + 1] for m in range(MT)])

                        def out(slot, s, j=j, b=b, g=g):
                            col = S * (j % 2)
                            if b == 0 and g == 0:
                                PE.after(got["pct"], *bank_read[OUT]).matmul(
                                    psum[:, OUT, col:col + S], vb[:, j * P:j * P + P], pct, start=True, stop=False,
                                    skip_group_check=True)
                            PE.after(s)
                            v = z3[:, :, b * P + 64 * g:b * P + 64 * g + 64]
                            t = PE.step(causal_out(slot, s, 64 * g, v, col, False, True))
                            pt_read[slot] = (t,)
                            if b == 1 and g == 1:
                                s = split_out(psum[:, OUT, col:col + S], y_hi[:, j, :], y_lo[:, j, :], t)
                                bank_read[OUT] = (s,)
                                y_done[0].append(s)

                        units.append((score, lambda slot, s: turn_blocks(slot, s, BLOCKS), out))
            yield from pipeline(units)
            got["nsa_done"] = (PE, PE.n)

        tmp_v = hid[1][:, 0:64]

        def gla():
            s = turn_qk(gqk, [(P * i, qT[:, i, :], 0.125) for i in range(2)]
                        + [(256 + P * i, kT[:, i, :], 1.0) for i in range(2)], (got["gqk"],))
            pe_ = PE.after(*bank_read[TURNED])
            for m in range(MT):
                t = pe_.transpose(psum[0:16, TURNED, m * P:m * P + P], z3[:, m, 280:296], ident)
            t = PE.step(t)
            qk = s
            s = VE.step(VE.after(t).tensor_copy(glow, psum[0:16, TURNED, 0:S]))
            bank_read[TURNED] = (s,)
            yield
            pe_ = PE.after(s, *score_read.get(0, ()))
            for i in range(2):
                t = pe_.matmul(psum[:, SCORE[0], i * S:i * S + S], w_gate[:, i * P:i * P + P], glow, start=True,
                               stop=True, skip_group_check=True)
            t = PE.step(t)
            zt, ab, b_sum = qT[:, 2:4, :], kT[:, 2:4, :], softf[:, 0:512].rearrange("p (i t) -> p i t", i=2)
            idle = [r for reads in (prob_read, pt_read) for v_ in reads.values() for r in v_]
            for i in range(2):
                s = VE.step(VE.after(t).tensor_scalar(zt[:, i, :], psum[:, SCORE[0], i * S:i * S + S],
                                                      b_gate[:, i:i + 1], None, ALU.add))
            score_read[0] = (s,)
            s = AC.step(AC.after(s).activation(ab, zt, ACT.Abs))
            s = AC.step(AC.after(s).activation(ab, ab, ACT.Exp, scale=-1.0))
            s = AC.step(AC.after(s).activation(ab, ab, ACT.Ln, bias=1.0))
            s = VE.step(VE.after(s).scalar_tensor_tensor(zt, zt, 0.0, ab, ALU.min, ALU.subtract))
            for i in range(2):
                s2 = VE.step(VE.after(s, *idle).tensor_tensor_scan(ab[:, i, :], consts[:, 256:512], zt[:, i, :], 0.0,
                                                                   ALU.mult, ALU.add))
            csum, s_sum = ab, s2
            yield
            e_buf = big[:, 0:2048].rearrange("p (l t) -> p l t", l=8)
            q_buf = memkv[:, :, :].rearrange("p m c -> p (m c)").rearrange("p (l t) -> p l t", l=8)
            off_read = [None]
            og = gqk.rearrange("p m (h d) -> p m h d", h=4)
            o_last = [qk]
            for hp in range(2):
                for i, half in enumerate(LEVELS):
                    b3 = csum[:, hp, :].rearrange("p (n t) -> p n t", t=2 * half)
                    ref = b3[:, :, half - 1:half].broadcast_to((P, S // (2 * half), 2 * half))
                    s = VE.step(VE.after(s_sum, got["nsa_done"], (PE, PE.n)).tensor_tensor(
                        e_buf[:, i, :].rearrange("p (n t) -> p n t", t=2 * half), b3, ref, ALU.subtract))
                ef = big[:, 0:2048]
                s = VE.step(VE.after(s).scalar_tensor_tensor(ef, ef, -1.0, ef, ALU.mult, ALU.max))
                s = AC.step(AC.after(s).activation(ef, ef, ACT.Exp, scale=-1.0 / 16))
                qb, kb_ = (a[:, hp, :].unsqueeze(1).broadcast_to((P, 8, S)) for a in (qT, kT))
                s = VE.step(VE.after(s, qk).tensor_tensor(q_buf, e_buf, qb, ALU.mult))
                s = VE.step(VE.after(s).tensor_tensor(e_buf, e_buf, kb_, ALU.mult))
                ready = s
                yield
                units = []
                for hh in range(2):
                    for m in range(MT):
                        half_ = slice(64 * hh, 64 * hh + 64)
                        h = 2 * hp + hh

                        def score(slot, m=m, half_=half_, h=h, hp=hp, ready=ready):
                            toks = slice(m * P, m * P + P)
                            pe_ = PE.after(ready, *score_read.get(0, ()), *score_read.get(1, ()))
                            for i in range(8):
                                lhsT, rhs = ((e_buf[half_, i + 1, toks], q_buf[half_, i + 1, toks]) if i < 7
                                             else (kT[half_, hp, toks], qT[half_, hp, toks]))
                                t = pe_.matmul(psum[:, SCORE[i // 4], (i % 4) * P:(i % 4) * P + P], lhsT, rhs,
                                               start=True, stop=True, skip_group_check=True)
                            if m:
                                t = PE.after(*bank_read[TURNED]).matmul(
                                    psum[:, TURNED, 0:P], e_buf[half_, 0, 0:P], q_buf[half_, 0, P:S], start=True,
                                    stop=True)
                            t = PE.step(t)
                            prod = soft[:, slot, :, :].rearrange("p a b -> p (a b)")
                            s = VE.step(VE.after(t).tensor_tensor(
                                prod.rearrange("p (i q) -> p i q", i=8),
                                psum[:, 4:6, :].rearrange("p a (i q) -> p (a i) q", i=4), masks, ALU.mult))
                            score_read[0] = score_read[1] = (s,)
                            s = VE.step(VE.after(s, *prob_read.get(slot, ())).tensor_reduce(
                                att[slot], prod.rearrange("p (i q) -> p q i", i=8), AX.X, ALU.add))
                            if m:
                                s = VE.step(VE.after(s, off_read[0]).tensor_copy(att_off, psum[:, TURNED, 0:P])
                                            if off_read[0] else
                                            VE.after(s).tensor_copy(att_off, psum[:, TURNED, 0:P]))
                                bank_read[TURNED] = (s,)
                            return s

                        def turn(slot, s, m=m, h=h):
                            pe_ = PE.after(s, got["gv"], *bank_read[OUT])
                            o = psum[:, OUT, 0:P]
                            t = pe_.matmul(o, att[slot], gv[:, m, h * P:h * P + P], start=True, stop=not m)
                            if m:
                                t = pe_.matmul(o, att_off, gv[:, 0, h * P:h * P + P], start=False, stop=True)
                            t = PE.step(t)
                            if m:
                                off_read[0] = t
                            prob_read[slot] = (t,)
                            s = VE.step(VE.after(t, qk).tensor_copy(og[:, m, h, :], o))
                            bank_read[OUT] = (s,)
                            o_last[0] = s
                            return s

                        units.append((score, turn, lambda slot, s: None))
                yield from pipeline(units)
            flat = gqk.rearrange("p m c -> p (m c)")
            s = head_norm(flat, 8, P, softf[:, 0:1024], (s8, t8, y8), gla_gain, o_last[0])
            s = VE.step(VE.after(s, got["gr"]).tensor_tensor(flat, flat, gr.rearrange("p m c -> p (m c)"), ALU.mult))
            yield
            for pair in range(2):
                pe_ = PE.after(s, *score_read.get(0, ()), *score_read.get(1, ()))
                for i in range(2):
                    for m in range(MT):
                        col = (2 * pair + i) * P
                        t = pe_.transpose(psum[:, SCORE[pair], i * S + m * P:i * S + m * P + P],
                                          gqk[:, m, col:col + P], ident)
                t = PE.step(t)
                kts = slice(4 + 2 * pair, 6 + 2 * pair)
                e_ = split_out(psum[:, SCORE[pair], :], y_hi[:, kts, :].rearrange("p a b -> p (a b)"),
                               y_lo[:, kts, :].rearrange("p a b -> p (a b)"), t)
                y_done[1].append(e_)
            yield

        work.clear()
        names = ["nk", "nq", "mq", "gr", "z3", "gqk", "gv", "cmp"] + ["merge"] * 6
        dests = {"mq": mq, "nq": znq[:, :, 0:512], "nk": znq[:, :, 512:1024], "z3": z3, "gqk": gqk, "gv": gv}
        free = {0: (mk,), 2: (mv,)}
        n_merge = 0
        for i, name in enumerate(names):
            bank = 2 * (i % 2)
            PE.after(*free[bank])
            if name == "cmp":
                free[bank] = (compress(bank),)
                work += [nsa(), gla()]
                continue
            end = strip(first, c, h_hi, h_lo, bank, between, None if i else parts)
            c += 4
            if name == "merge":
                cols = slice(512 * n_merge, 512 * n_merge + 512)
                for m in range(MT):
                    s = VE.step(VE.after(end, x_scale).scalar_tensor_tensor(
                        merge[:, m, cols], psum[:, bank + m, :], scale[:, m:m + 1], b_merge[:, cols], ALU.mult, ALU.add))
                n_merge += 1
            elif name == "gr":
                for m in range(MT):
                    s = AC.step(AC.after(end, x_scale).activation(gr[:, m, :], psum[:, bank + m, :], ACT.Silu,
                                                                  scale=scale[:, m:m + 1]))
                exp_and_ln()
            else:
                s = take_out(dests[name], bank, end, i % 2, scale, x_scale)
            free[bank] = (s,)
            got[name] = s
            if name == "nk":
                work.append(make_windows())
            if name == "nq":
                work.append(nsa_prep())
            if name == "mq":
                work.append(mem_attention())
            between()

        for m in range(MT):
            for b in (2, 0, 1):
                w = merge[:, m, b * D:b * D + D]
                gate_done = AC.step(AC.after(s).activation(w, w, ACT.Sigmoid))
        exp_and_ln()
        merge_done = []

        def take_branch(b, m, end):
            f = psum[:, 2 * m:2 * m + 2, :].rearrange("p a b -> p (a b)")
            g_ = merge[:, m, b * D:b * D + D]
            s = VE.step(VE.after(end, gate_done).tensor_tensor(g_, g_, f, ALU.mult))
            if b != 2:
                s = VE.step(VE.after(s).tensor_tensor(merged[:, m, :], merged[:, m, :], g_, ALU.add))
            merge_done.append((s,))
            return s

        PE.after(*free[0], *free[2])
        for b in (2, 0):
            while len(y_done[b]) < 4:
                between()
            PE.after(*y_done[b])
            for i in range(4):
                end = rows(first, c + i, 4 * b + i, y_hi, y_lo, 0, i == 0, i == 3)
                if i < 3:
                    between()
            c += 4
            for m in range(MT):
                s = take_branch(b, m, end)
            between()
            PE.after(s)
        while work:
            between()
        PE.after(*y_done[1])
        merge_done.clear()
        for i in range(2):
            rows(first, c + i, 4 + i, y_hi, y_lo, 0, i == 0, False)
        end = last_rows(first, c + 2, 6, 2, y_hi, y_lo, 0, lambda end: take_branch(1, 0, end))
        take_branch(1, 1, end)
        c += 4
        parts = to_features(merged, None, h_hi, h_lo, (4, 5, 6, 7), merge_done)
        for i in range(KD - 2):
            PE.after(parts[i // 2])
            rows(first, c + i, i, h_hi, h_lo, 0, i == 0, False)
        PE.after(parts[-1])
        x_done = []
        end = last_rows(first, c + KD - 2, KD - 2, 2, h_hi, h_lo, 0, lambda end: x_done.append((add_plain(0, 0, end),)))
        x_done.append((add_plain(0, 1, end),))
        c += KD

        parts = to_features(x, pre2[:, 1, :], h_hi, h_lo, (4, 5, 6, 7), x_done)
        s = row_scale(x, work_sq, x_cells, *x_done[1])
        AC.after(s)
        VE.after(s)
        feed_forward(first, c, MLP_STRIPS, False, 0, parts, scale, lambda m, end: add_plain(4, m, end))
        assert c + MLP_STRIPS * 8 == PIECES2
        end_layer()

    act.wait_ge(s_used, PIECES)
    round_piece(0, PIECES + AHEAD)
    act.dma_start(T["out"].rearrange("b (m p) d -> p (b m) d", p=P), x[:, :, :]).then_inc(s_out, 16)
    act.wait_ge(s_out, 16)
    act.wait_ge(s_lo, STREAM)


def pieces_of(w, cols):
    K, N = w.shape
    per = PIECE // cols
    a = w.reshape(K // P // per, per, P, N // cols, cols)
    return a.transpose(3, 0, 2, 1, 4).reshape(-1, P, PIECE)


def ffn_pieces(up, down, strips, rows_per):
    u = up.reshape(strips, 4, P, PIECE)
    d = down.reshape(strips, rows_per, P, PIECE)
    out = [u[0]]
    for i in range(1, strips):
        out += [u[i], d[i - 1]]
    return np.concatenate(out + [d[-1]])


def swiglu_pieces(gate, up, down):
    both = np.concatenate([gate.reshape(D, FFN_STRIPS, 256), up.reshape(D, FFN_STRIPS, 256)], 2).reshape(D, -1)
    return ffn_pieces(pieces_of(both, 512), pieces_of(down, 1024), FFN_STRIPS, 2)


def stream_of(a):
    parts = []
    for l in range(L):
        w = a["w_in"][l]
        A, B, C = 384, 256, 384
        qa, ka, va, qb, kb, vb, qc, kc, vc = np.split(w, np.cumsum([A, A, A, B, B, B, C, C]), 1)
        w = np.concatenate([qb, kb, vb, qa, ka, va, qc, kc, vc], 1)
        parts += [swiglu_pieces(a["ffn1_w_gate"][l], a["ffn1_w_up"][l], a["ffn1_w_down"][l]),
                  pieces_of(w, 512), pieces_of(a["w_out"][l], 1024),
                  swiglu_pieces(a["ffn2_w_gate"][l], a["ffn2_w_up"][l], a["ffn2_w_down"][l])]
    sizes = [512, 128, 128, 128, 128, 128, 128, 24, 256, 256, 512, 512, 16, 512, 3072]
    for l in range(L):
        q, kc, vc, ks, vs, kw, vw, g, gq, gk, gv, gr, gl, mq, mg = np.split(a["w_in_2"][l], np.cumsum(sizes)[:-1], 1)
        q = q.reshape(D, 2, 4, 64).transpose(0, 2, 1, 3).reshape(D, 512)
        g = g.reshape(D, 2, 4, 3).transpose(0, 3, 2, 1).reshape(D, 24)
        pad = np.zeros((D, 216), np.float32)
        before = np.concatenate([ks, kw, kc, vc, q, mq, gr, vs, vw, g, gl, pad, gq, gk, gv], 1)
        wb = a["w_branch_2"][l]
        nsa_rows = wb[0].reshape(2, 4, 64, D).transpose(1, 0, 2, 3).reshape(512, D)
        parts += [pieces_of(a["mem_w_kv_2"][l], 512), pieces_of(before, 512),
                  pieces_of(a["cmp_w1_2"][l, 0], 256), pieces_of(a["cmp_w1_2"][l, 1], 256),
                  pieces_of(mg, 512), pieces_of(wb[2], 1024), pieces_of(nsa_rows, 1024), pieces_of(wb[1], 1024),
                  pieces_of(a["w_out_2"][l], 1024),
                  ffn_pieces(pieces_of(a["w_up_2"][l], 512), pieces_of(a["w_down_2"][l], 1024), MLP_STRIPS, 4)]
    parts.append(np.zeros((STREAM - PIECES, P, PIECE), np.float32))
    out = np.concatenate(parts)
    assert out.shape[0] == STREAM, out.shape
    return out


def shape_constants():
    p, q = np.arange(P)[:, None], np.arange(P)[None, :]
    keys = np.arange(S)[None, :]
    c = np.zeros((P, 1024), np.float32)
    c[:, 0:128] = p == q
    c[:, 128:256] = p > q
    c[:, 256:512] = 1
    c[:, 512:640] = p < q
    c[:, 640:896] = np.where(keys <= P + p, 0, BIG)
    for m in range(MT):
        n = np.arange(16)[None, :]
        seen = (16 * n + 31 <= m * P + p) & (n < N_CMP)
        c[:, 896 + 16 * m:912 + 16 * m] = np.where(seen, 0, BIG)
        c[:, 928 + 16 * m:944 + 16 * m] = seen
    c[:, 960:968] = p // 16 == np.arange(8)[None, :]
    c[:32, 968:970] = p[:32] // 16 == np.arange(2)[None, :]
    c[:, 976:984] = np.power(np.float32(500000.0), -np.arange(8, dtype=np.float32) / 8)
    dist = np.abs(P + p - keys).astype(np.float32)
    late = np.where((keys // 64) > (P + p) // 64, BIG, 0).astype(np.float32)
    slopes = np.exp2(-8.0 * np.arange(1, NB + 1, dtype=np.float32) / NB)
    alibi = np.concatenate([np.float32(s) * dist + late for s in slopes], 1).astype(np.float32)
    masks = np.zeros((P, 8, P), np.float32)
    for i, half in enumerate(LEVELS[1:]):
        masks[:, i] = (p // (2 * half) == q // (2 * half)) & (p % (2 * half) < half) & (q % (2 * half) >= half)
    masks[:, 7] = p == q
    lam = [0.8 - 0.6 * math.exp(-0.3 * l) for l in range(L)]
    lam = np.array([[v, 1.0 - v] for v in lam], np.float32)
    return c, alibi, masks.reshape(P, 1024), lam


def by_tile(g):
    return np.ascontiguousarray(np.swapaxes(g.reshape(g.shape[:-1] + (-1, P)), -1, -2))


def kernel(**inputs):
    import concourse.bacc as bacc
    from concourse.bass_utils import run_bass_kernel_spmd

    a = {k: np.asarray(v) for k, v in inputs.items()}
    consts, alibi, masks, lam = shape_constants()
    rel = np.clip(P - np.arange(-127, 256), -128, 128) + 128
    band = a["rel_bias"][:, :, rel]
    at = np.arange(S)[None, :] - np.arange(P)[:, None] + 127
    arrays = {
        "stream": stream_of(a), "x": a["x"], "mem": a["mem_2"], "positions": a["positions_2"].astype(np.int32),
        "consts": consts, "special1": alibi, "masks": masks, "lam_const": lam,
        "pre1": np.stack([by_tile(a[n]) for n in ("ffn1_pre_g", "mix_pre_g", "ffn2_pre_g")], 2),
        "post1": np.stack([a[n] for n in ("ffn1_post_g", "mix_post_g", "ffn2_post_g")], 1),
        "lams": np.stack([a["diff_lambda_" + n] for n in ("q1", "k1", "q2", "k2")], 1),
        "subln": a["diff_subln_g"],
        "band": np.ascontiguousarray(band[:, :, at].transpose(0, 2, 1, 3)),
        "pre2": np.stack([by_tile(a[n]) for n in ("ln_mix_2", "ln_mlp_2", "mem_norm_2")], 2),
        "w2": np.ascontiguousarray(a["cmp_w2_2"].reshape(L, 2, 2, P, 64).transpose(0, 3, 1, 2, 4)),
        "w_gate": a["gla_w_gate_2"],
        "pe": np.ascontiguousarray(a["cmp_pe_2"].reshape(L, 2, 16, P).transpose(0, 3, 1, 2)),
        "b_gate": by_tile(a["gla_b_gate_2"]),
        "b_merge": a["b_merge_2"].reshape(L, -1),
        "gain12": np.concatenate([np.tile(a["nsa_q_norm_2"], (1, 8)), np.tile(a["nsa_k_norm_2"][:, 1], (1, 2)),
                                  np.tile(a["nsa_k_norm_2"][:, 2], (1, 2))], 1),
        "gla_gain": a["gla_norm_2"],
        "mem_gain": np.stack([a["mem_q_norm_2"], a["mem_k_norm_2"]], 1),
        "cmp_gain": a["nsa_k_norm_2"][:, 0],
    }
    nc = bacc.Bacc("TRN2", target_bir_lowering=False, num_devices=1)
    T, feed = {}, {}
    for name, v in arrays.items():
        feed[f"in_{name}"] = np.ascontiguousarray(v)
        T[name] = nc.dram_tensor(f"in_{name}", v.shape, mybir.dt.from_np(v.dtype), kind="ExternalInput").ap()
    T["out"] = nc.dram_tensor("out", (1, S, D), F32, kind="ExternalOutput").ap()
    build(nc, T)
    return run_bass_kernel_spmd(nc, [feed], core_ids=[0]).results[0]["out"]
```

```python
import math
from contextlib import ExitStack

import numpy as np

import concourse.bass as bass
from concourse import mybir

F32 = mybir.dt.float32
F32R = mybir.dt.float32r
I32 = mybir.dt.int32
ALU = mybir.AluOpType
ACT = mybir.ActivationFunctionType
AX = mybir.AxisListType

P = 128
S = 256
MT = S // P
D = 1024
KD = D // P
L = 2
EPS = 1e-6
BIG = 1e30
HUGE = 3e38

PIECE = 1024
RING = 4
AHEAD = 3

D_FF = 2816
FFN_STRIPS = D_FF // 256
NA, NB = 6, 4
COLS1 = 3072
QKV_A, QKV_B, QKV_C = 768 + 1152, 0, 768
OUT_ORDER = (3, 4, 5, 6, 7, 0, 1, 2)
FFN_PIECES = FFN_STRIPS * 6
PIECES1 = 2 * FFN_PIECES + COLS1 // 512 * 4 + KD

MLP_STRIPS = 4096 // 512
N_CMP = 15
PIECES2 = 2 * 4 + 13 * 4 + 8 + 12 + KD + MLP_STRIPS * 8
PIECES = L * (PIECES1 + PIECES2)
STREAM = PIECES + RING
assert PIECES1 % RING == 0 and PIECES2 % RING == 0

LEVELS = (128, 64, 32, 16, 8, 4, 2, 1)


class At:

    def __init__(self, sem, value):
        self.sem, self.value = sem, value


class Queue:

    def __init__(self, engine, sem):
        self.engine, self.sem = engine, sem
        self.n, self.seen = 0, {}

    def after(self, *steps):
        for step in steps:
            if isinstance(step, At):
                self.engine.wait_ge(step.sem, step.value)
                continue
            queue, n = step
            if self.seen.get(id(queue), 0) < n:
                self.engine.wait_ge(queue.sem, n)
                self.seen[id(queue)] = n
        return self.engine

    def step(self, instruction):
        instruction.then_inc(self.sem, 1)
        self.n += 1
        return (self, self.n)

    def restart(self):
        self.n, self.seen = 0, {}


def build(nc, T):
    with ExitStack() as stack:
        build_in(nc, T, stack)


def build_in(nc, T, stack):
    def sb(name, shape, dtype=F32):
        return stack.enter_context(nc.sbuf_tensor(name, list(shape), dtype))

    def sem(name):
        return stack.enter_context(nc.semaphore(name))

    pe, dve, act, pool, sp = nc.tensor, nc.vector, nc.scalar, nc.gpsimd, nc.sync
    three = [pe.engine, act.engine, dve.engine]

    raw = sb("raw", [P, RING, PIECE])
    hi = sb("hi", [P, RING, PIECE], F32R)
    lo = sb("lo", [P, RING, PIECE], F32R)
    x = sb("x", [P, MT, D])
    h_hi = sb("h_hi", [P, KD, S], F32R)
    h_lo = sb("h_lo", [P, KD, S], F32R)
    y_hi = sb("y_hi", [P, 12, S], F32R)
    y_lo = sb("y_lo", [P, 12, S], F32R)
    big = sb("big", [P, 12904])
    memkv = sb("memkv", [P, MT, 1024])
    soft = sb("soft", [P, 2, 2, 512])
    qT = sb("qT", [P, 4, S])
    kT = sb("kT", [P, 4, S])
    consts = sb("consts", [P, 1024])
    special = sb("special", [P, 5888])
    extra = sb("extra", [P, 2048])
    small = sb("small", [P, 512])
    psum = stack.enter_context(nc.psum_tensor("psum", [P, 8, 512], F32))

    ident = consts[:, 0:128]
    tri = consts[:, 128:256]
    ones = consts[:, 256:384]
    strict = consts[:, 512:640]
    causal = consts[:, 640:896]
    cmp_table = consts[:, 896:928].rearrange("p (m n) -> p m n", m=MT)
    cmp_valid = consts[:, 928:960].rearrange("p (m n) -> p m n", m=MT)
    own_values = consts[:, 960:968]
    own_keys = consts[0:32, 968:970]
    f32 = lambda a: a.bitcast(F32)

    s_landed = [sem(f"s_landed{i}") for i in range(RING)]
    s_hi = sem("s_hi")
    s_lo = sem("s_lo")
    s_used = sem("s_used")
    PE, AC, VE = (Queue(e, sem(n)) for e, n in ((pe, "s_pe"), (act, "s_act"), (dve, "s_dve")))
    s_pre = sem("s_pre")
    s_pre2 = sem("s_pre2")
    s_mem = sem("s_mem")
    s_masks = sem("s_masks")
    s_par = sem("s_par")
    s_gu = sem("s_gu")
    s_silu = sem("s_silu")
    s_prod = sem("s_prod")
    s_turn = sem("s_turn")
    s_ahi = sem("s_ahi")
    s_alo = sem("s_alo")
    s_down = sem("s_down")
    s_out = sem("s_out")
    ffn_sems = [s_gu, s_silu, s_prod, s_turn, s_ahi, s_alo, s_down]
    layer_sems = [PE.sem, AC.sem, VE.sem, s_par] + ffn_sems

    for slot in range(RING):
        sp.dma_start(raw[:, slot, :], T["stream"][slot]).then_inc(s_landed[slot], 16)
    with sp.Fori(0, STREAM // RING - 1) as turn:
        for slot in range(RING):
            sp.wait_ge(s_lo, turn * RING + slot + 1)
            sp.dma_start(raw[:, slot, :], T["stream"][(turn + 1) * RING + slot]).then_inc(s_landed[slot], 16)
    with pool.Fori(0, STREAM // RING) as turn:
        for slot in range(RING):
            pool.wait_ge(s_hi, turn * RING + slot + 1)
            pool.tensor_tensor(lo[:, slot, :], raw[:, slot, :], f32(hi[:, slot, :]),
                               ALU.subtract).then_inc(s_lo, 1)

    def round_piece(first, c):
        slot = c % RING
        act.wait_ge(s_landed[slot], first * (16 // RING) + 16 * (c // RING + 1))
        act.activation(hi[:, slot, :], raw[:, slot, :], ACT.Copy).then_inc(s_hi, 1)

    def next_piece(first, c):
        act.wait_ge(s_used, first + c + 1)
        round_piece(first, c + AHEAD)
        pe.wait_ge(s_lo, first + c + 1)
        return c % RING

    def product(out, lhs_hi, lhs_lo, rhs_hi, rhs_lo, start, stop):
        pe.matmul(out, lhs_hi, rhs_hi, start=start, stop=False)
        pe.matmul(out, lhs_hi, rhs_lo, start=False, stop=False)
        return pe.matmul(out, lhs_lo, rhs_hi, start=False, stop=stop)

    def strip(first, c, a_hi, a_lo, bank, between=None, parts=None):
        for j in range(4):
            slot = next_piece(first, c + j)
            PE.after(*(parts[j:j + 1] if parts else ()))
            for i in range(2):
                k = 2 * j + i
                for m in range(MT):
                    w = slice(i * 512, i * 512 + 512)
                    last = product(psum[:, bank + m, :], a_hi[:, k, m * P:m * P + P], a_lo[:, k, m * P:m * P + P],
                                   hi[:, slot, w], lo[:, slot, w], k == 0, k == KD - 1)
            last.then_inc(s_used, 1)
            if between and j < 3:
                between()
        return At(s_used, first + (c + 4 + 1))

    def rows(first, c, kt, a_hi, a_lo, bank, start, stop):
        slot = next_piece(first, c)
        for m in range(MT):
            for n in range(2):
                w = slice(n * 512, n * 512 + 512)
                last = product(psum[:, bank + 2 * m + n, :], a_hi[:, kt, m * P:m * P + P],
                               a_lo[:, kt, m * P:m * P + P], hi[:, slot, w], lo[:, slot, w], start, stop)
        last.then_inc(s_used, 1)
        return At(s_used, first + (c + 1 + 1))

    def last_rows(first, c, kt, n_kt, a_hi, a_lo, bank, after_first):
        next_piece(first, c)
        for m in range(MT):
            for i in range(n_kt):
                slot = (c + i) % RING
                if m == 0 and i:
                    pe.wait_ge(s_lo, first + c + i + 1)
                for n in range(2):
                    w = slice(n * 512, n * 512 + 512)
                    last = product(psum[:, bank + 2 * m + n, :], a_hi[:, kt + i, m * P:m * P + P],
                                   a_lo[:, kt + i, m * P:m * P + P], hi[:, slot, w], lo[:, slot, w],
                                   False, i == n_kt - 1)
                if m:
                    last.then_inc(s_used, 1)
            if m == 0:
                after_first(PE.step(last))
                for i in range(1, n_kt):
                    act.wait_ge(s_used, first + c + i + 1)
                    round_piece(first, c + i + AHEAD)
        return At(s_used, first + (c + n_kt + 1))

    def exp_and_ln():
        act.preload_act_table_set("natural_log_exp_and_others")

    def rsqrt(v, t, y, *ready):
        s = AC.step(AC.after(*ready).activation(t, v, ACT.Ln))
        s = AC.step(AC.after(s).activation(y, t, ACT.Exp, scale=-0.5))
        s = VE.step(VE.after(s, *ready).tensor_tensor(t, y, y, ALU.mult))
        s = VE.step(VE.after(s).tensor_tensor(t, t, v, ALU.mult))
        s = VE.step(VE.after(s).tensor_scalar(t, t, -0.5, 1.5, ALU.mult, ALU.add))
        return VE.step(VE.after(s).tensor_tensor(y, y, t, ALU.mult))

    small_at = [0]

    def cell(n):
        small_at[0] += n
        assert small_at[0] <= 500, small_at
        return small[:, small_at[0] - n:small_at[0]]

    def row_scale(src, scratch, cells, *ready):
        ss, t, y = cells
        for m in range(MT):
            s = AC.step(AC.after(*ready).activation(scratch[:, m, :], src[:, m, :], ACT.Square,
                                                    accum_out=ss[:, m:m + 1]))
        s = VE.step(VE.after(s).tensor_scalar(ss, ss, 1.0 / D, EPS, ALU.mult, ALU.add))
        return rsqrt(ss, t, y, s)

    def to_features(src, gain, out_hi, out_lo, banks, done):
        parts, turned = [], {}
        for m in range(MT):
            for pair, bank in enumerate(banks):
                pe_ = PE.after(*done[m])
                for i in range(2):
                    k = 2 * pair + i
                    t = pe_.transpose(psum[:, bank, i * S + m * P:i * S + m * P + P], src[:, m, k * P:k * P + P],
                                      ident)
                turned[pair] = PE.step(t) if m else None
        for pair, bank in enumerate(banks):
            kts = [(2 * pair + i, psum[:, bank, i * S:i * S + S]) for i in range(2)]
            for k, part in kts:
                a = AC.step(AC.after(turned[pair]).activation(out_hi[:, k, :], part, ACT.Copy,
                                                              scale=1.0 if gain is None else gain[:, k:k + 1]))
            for k, part in kts:
                b = VE.step(VE.after(a).scalar_tensor_tensor(out_lo[:, k, :], part,
                                                             1.0 if gain is None else gain[:, k:k + 1],
                                                             f32(out_hi[:, k, :]), ALU.mult, ALU.subtract))
            parts.append(b)
        return parts

    def add_norm(gain, bank, m, *ready):
        f = psum[:, bank + 2 * m:bank + 2 * m + 2, :].rearrange("p a b -> p (a b)")
        ss, v, t, y = (c_[:, m:m + 1] for c_ in f_cells)
        s = AC.step(AC.after(*ready).activation(work_sq[:, m, :], f, ACT.Square, accum_out=ss))
        a = AC.step(AC.after(s).activation(t, ss, ACT.Ln, scale=1.0 / D, bias=eps))
        a = AC.step(AC.after(a).activation(y, t, ACT.Exp, scale=-0.5))
        VE.step(VE.after(s).tensor_scalar(v, ss, 1.0 / D, EPS, ALU.mult, ALU.add))
        b = VE.step(dve.tensor_tensor(work_post[:, m, :], f, gain, ALU.mult))
        s = VE.step(VE.after(a, b).scalar_tensor_tensor(t, v, y, y, ALU.mult, ALU.mult))
        s = VE.step(VE.after(s).scalar_tensor_tensor(y, t, 3.0, y, ALU.subtract, ALU.mult))
        return VE.step(VE.after(s).scalar_tensor_tensor(x[:, m, :], work_post[:, m, :], y, x[:, m, :], ALU.mult,
                                                        ALU.add))

    def add_plain(bank, m, *ready):
        f = psum[:, bank + 2 * m:bank + 2 * m + 2, :].rearrange("p a b -> p (a b)")
        return VE.step(VE.after(*ready).tensor_tensor(x[:, m, :], x[:, m, :], f, ALU.add))

    def feed_forward(first, c, strips, gated, strips_before, parts, scale, finish, once=None):
        kts = 2 if gated else 4
        width = kts * P
        pieces = 4 + kts
        per_turn = 2 if gated else 1
        act_s, prod_s = work_act[:, :, 0:width], work_prod[:, :, 0:width]

        def project(base, c, n, parts=None):
            pe.wait_ge(s_prod, n + 1)
            done = strip(base, c, h_hi, h_lo, 0, parts=parts)
            for q in (act, dve):
                q.wait_ge(done.sem, done.value)
            act.wait_ge(s_prod, n + 1)
            for m in range(MT):
                t = act.activation(act_s[:, m, :], psum[:, m, 0:width], ACT.Silu if gated else ACT.Relu,
                                   scale=scale[:, m:m + 1])
            t.then_inc(s_silu, 1)
            dve.wait_ge(s_silu, n + 1)
            dve.wait_ge(s_turn, n + 1)
            if gated:
                for m in range(MT):
                    t = dve.scalar_tensor_tensor(prod_s[:, m, :], psum[:, m, width:2 * width], scale[:, m:m + 1],
                                                 act_s[:, m, :], ALU.mult, ALU.mult)
            else:
                t = dve.tensor_tensor(prod_s, act_s, act_s, ALU.mult)
            t.then_inc(s_prod, 1)

        def down(base, c, n, start):
            pe.wait_ge(s_alo, n)
            for i in range(kts):
                rows(base, c + i, i, y_hi, y_lo, 4, start and i == 0, False)

        def turn(base, c, n):
            pe.wait_ge(s_prod, n + 2)
            for i in range(kts):
                for m in range(MT):
                    t = pe.transpose(psum[:, 2 + i // 2, (i % 2) * S + m * P:(i % 2) * S + m * P + P],
                                     prod_s[:, m, i * P:i * P + P], ident)
            t.then_inc(s_turn, 1)
            src = psum[:, 2:2 + kts // 2, :].rearrange("p a b -> p (a b)")
            high = y_hi[:, 0:kts, :].rearrange("p a b -> p (a b)")
            low = y_lo[:, 0:kts, :].rearrange("p a b -> p (a b)")
            for q in (act, dve):
                q.wait_ge(s_turn, n + 2)
                q.wait_ge(s_used, base + (c + 1))
            act.activation(high, src, ACT.Copy).then_inc(s_ahi, 1)
            dve.wait_ge(s_ahi, n + 1)
            dve.tensor_tensor(low, src, f32(high), ALU.subtract).then_inc(s_alo, 1)

        n0 = strips_before
        project(first, c, n0, parts)
        turn(first, c + 4, n0)
        if once:
            once()
        project(first, c + 4, n0 + 1)
        down(first, c + 8, n0 + 1, True)
        turn(first, c + 8 + kts, n0 + 1)
        left = strips - 2
        c += 8 + kts
        whole = left // per_turn
        if whole:
            with nc.Fori(0, whole, engines=three) as i:
                base = first + i * (pieces * per_turn)
                for j in range(per_turn):
                    n = i * per_turn + (n0 + 2 + j)
                    cj = c + j * pieces
                    project(base, cj, n)
                    down(base, cj + 4, n, False)
                    turn(base, cj + pieces, n)
        c += whole * per_turn * pieces
        for j in range(left - whole * per_turn):
            n = n0 + 2 + whole * per_turn + j
            project(first, c, n)
            down(first, c + 4, n, False)
            turn(first, c + pieces, n)
            c += pieces
        if gated:
            exp_and_ln()
        pe.wait_ge(s_alo, n0 + strips)
        done = []
        end = last_rows(first, c, 0, kts, y_hi, y_lo, 4, lambda end: done.append((finish(0, end),)))
        done.append((finish(1, end),))
        return done

    SCORE, TURNED, OUT = (4, 5), 6, 7
    score_read, prob_read, pt_read = {}, {}, {}
    bank_read = {TURNED: (), OUT: ()}

    def pipeline(units):
        states = [None] * len(units)

        def do(part, i):
            if 0 <= i < len(units) and units[i][part]:
                states[i] = units[i][part](i % 2, states[i])

        for i in range(len(units) + 2):
            do(0, i)
            do(2, i - 1)
            do(4, i - 2)
            do(1, i)
            do(3, i - 1)
            yield

    stat = [[cell(8) for _ in range(6)] for _ in range(2)]

    def softmax_parts(slot, products, ready, tables, segments, row_tiles=False, scales=False):
        bank, prob = SCORE[slot], soft[:, slot, 0, :]
        mn, total, inverse = stat[slot][0:3]
        pe_ = PE.after(*ready, *score_read.get(slot, ()))
        t = None
        for lhsT, rhs, col, width in products:
            if t and row_tiles:
                PE.after(t)
            t = PE.step(pe_.matmul(psum[:, bank, col:col + width], lhsT, rhs, start=True, stop=True))
        for i, ((col, width), table) in enumerate(zip(segments, tables)):
            w = slice(col, col + width)
            VE.after(t, *prob_read.get(slot, ()))
            if scales:
                a = VE.step(dve.tensor_scalar(prob[:, w], psum[:, bank, w], table, HUGE, ALU.mult, ALU.min,
                                              accum_out=mn[:, i:i + 1]))
            else:
                a = VE.step(dve.tensor_tensor_reduce(prob[:, w], psum[:, bank, w], table, 1.0, HUGE, ALU.add, ALU.min,
                                                     mn[:, i:i + 1]))
            s = AC.step(AC.after(a).activation(prob[:, w], prob[:, w], ACT.Exp, scale=-1.0, bias=mn[:, i:i + 1],
                                               accum_out=total[:, i:i + 1]))
        score_read[slot] = (a,)
        return s

    def normalised(slot, s, segments, gates):
        prob = soft[:, slot, 0, :]
        total, inverse = stat[slot][1:3]
        n = len(segments)
        r = VE.step(VE.after(s).reciprocal(inverse[:, 0:n], total[:, 0:n]))
        for i, (col, width) in enumerate(segments):
            w = slice(col, col + width)
            r2 = VE.step(VE.after(r).tensor_scalar(prob[:, w], prob[:, w], inverse[:, i:i + 1],
                                                   gates[i] if gates else None, ALU.mult,
                                                   ALU.mult if gates else ALU.bypass))
        return r2

    def turn_blocks(slot, ready, cols):
        pe_ = PE.after(ready, *bank_read[TURNED])
        for i, col in enumerate(cols):
            t = pe_.transpose(psum[:, TURNED, i * P:i * P + P], soft[:, slot, 0, col:col + P], ident)
        t = PE.step(t)
        prob_read[slot] = (t,)
        n = len(cols) * P
        a = VE.step(VE.after(t, *pt_read.get(slot, ())).tensor_copy(soft[:, slot, 1, 0:n], psum[:, TURNED, 0:n]))
        bank_read[TURNED] = (a,)
        return a

    def split_out(src, high, low, t):
        a = AC.step(AC.after(t).activation(high, src, ACT.Copy))
        b = VE.step(VE.after(t, a).tensor_tensor(low, src, f32(high), ALU.subtract))
        return b

    def causal_out(slot, base, v, col, start=True, stop=True):
        probs = soft[:, slot, 1, :]
        out = psum[base:base + 64, OUT, col:col + S]
        pe.matmul(out[:, 0:P], v[:, 0, :], probs[:, 0:P], start=start, stop=stop, skip_group_check=True)
        pe.matmul(out[:, P:S], v[:, 0, :], probs[:, P:2 * P], start=start, stop=False, skip_group_check=True)
        return pe.matmul(out[:, P:S], v[:, 1, :], probs[:, 2 * P:3 * P], start=False, stop=stop,
                         skip_group_check=True)

    SEG = [(0, P), (P, S)]
    BLOCKS = [0, P, 2 * P]

    def turn_qk(z, jobs, ready):
        for n, (col, target, scale) in enumerate(jobs):
            bank = SCORE[n % 2]
            pe_ = PE.after(*ready, *score_read.get(n % 2, ()))
            for m in range(MT):
                t = pe_.transpose(psum[:, bank, m * P:m * P + P], z[:, m, col:col + P], ident)
            t = PE.step(t)
            a = AC.step(AC.after(t).activation(target, psum[:, bank, 0:S], ACT.Copy, scale=scale))
            score_read[n % 2] = (a,)
        return a

    def take_out(dst, bank, end, by_act, y, *ready):
        for m in range(MT):
            src = psum[:, bank + m, 0:dst.shape[2]]
            if by_act:
                s = AC.step(AC.after(end, *ready).activation(dst[:, m, :], src, ACT.Copy, scale=y[:, m:m + 1]))
            else:
                s = VE.step(VE.after(end, *ready).tensor_scalar(dst[:, m, :], src, y[:, m:m + 1], None, ALU.mult))
        return s

    def load(target, source, s=None, **how):
        act.dma_start(target, source, **how).then_inc(s or s_par, 16)
        loads[0] += not s

    loads = [0]
    x_cells = (cell(2), cell(2), cell(2))
    scale = x_cells[2]
    f_cells = (cell(2), cell(2), cell(2), cell(2))
    eps = cell(1)
    work_sq = big[:, 2048:4096].rearrange("p (m d) -> p m d", m=MT)
    work_act = big[:, 0:1024].rearrange("p (m d) -> p m d", m=MT)
    work_prod = big[:, 1024:2048].rearrange("p (m d) -> p m d", m=MT)
    work_post = big[:, 4096:6144].rearrange("p (m d) -> p m d", m=MT)

    pre1 = special[:, 1024:1048].rearrange("p (i k) -> p i k", i=3)
    pre2 = special[:, 5536:5560].rearrange("p (i k) -> p i k", i=3)
    hid = [extra[:, 512 + 128 * i:640 + 128 * i] for i in range(3)]
    trig = extra[:, 1872:1920].rearrange("p (f m i) -> p f m i", f=2, m=3)
    inv_freq = cell(8)
    s_const, s_rot = sem("s_const"), sem("s_rot")
    pos_i = small[:, 500:503].bitcast(I32)
    pos_f = small[:, 504:507]
    s = VE.step(dve.memset(small[:, 500:503], 0.0))
    AC.after(s)
    for m in range(MT):
        load(pos_i[:, m:m + 1], T["positions"].rearrange("b (p o) -> p (b o)", o=1)[m * P:m * P + P, :], s_rot)
    ends = T["positions"].rearrange("b (n t) -> (b n) t", t=16)
    for g in range(2):
        load(pos_i[16 * g:16 * g + 15, 2:3], ends[1:16, 15:16], s_rot, allow_slow_non_contiguous=True)
    load(inv_freq, T["consts"][:, 976:984], s_rot)
    load(x[:, :, :], T["x"].rearrange("b (m p) d -> p (b m) d", p=P), s_const)
    load(consts[:, :], T["consts"], s_const)
    load(pre1, T["pre1"][0], s_pre)
    load(pre2, T["pre2"][0], s_pre2)
    def start_counts():
        act.sem_inc(s_prod, 1)
        act.sem_inc(s_turn, 1)

    def end_layer():
        nc.multi_engine_barrier(three)
        for one in layer_sems:
            act.sem_clear(one)
        start_counts()
        nc.multi_engine_barrier(three)
        for queue in (PE, AC, VE):
            queue.restart()
        for reads in (score_read, prob_read, pt_read):
            reads.clear()
        bank_read[TURNED] = bank_read[OUT] = ()
        loads[0] = 0

    def load_mem():
        load(memkv[:, :, :], T["mem"].rearrange("b (m p) d -> p (b m) d", p=P), s_mem)

    dve.wait_ge(s_rot, 80)
    s = VE.step(dve.tensor_copy(pos_f, pos_i))
    ang = hid[0][:, 0:48].rearrange("p (f m i) -> p f m i", f=2, m=3)
    angf, turns, turns_i = hid[0][:, 0:48], hid[1][:, 0:48], hid[2][:, 0:48].bitcast(I32)
    for m in range(3):
        s = VE.step(VE.after(s).tensor_scalar(ang[:, 1, m, :], inv_freq, pos_f[:, m:m + 1], None, ALU.mult))
    s = VE.step(VE.after(s).tensor_copy(ang[:, 0], ang[:, 1]))
    s = VE.step(VE.after(s).tensor_scalar(turns, angf, 1.0 / (2 * math.pi), None, ALU.mult))
    s = VE.step(VE.after(s).tensor_copy(turns_i, turns))
    s = VE.step(VE.after(s).tensor_copy(turns, turns_i))
    rest = 2 * math.pi - 6.28125
    c_mid = float(np.float32(np.round(rest * 2 ** 21) / 2 ** 21))
    for part in (6.28125, c_mid, rest - c_mid):
        s = VE.step(VE.after(s).scalar_tensor_tensor(angf, turns, -part, angf, ALU.mult, ALU.add))
    s = VE.step(VE.after(s).tensor_scalar(angf[:, 0:24], angf[:, 0:24], math.pi / 2, None, ALU.add))
    for _ in range(2):
        s = VE.step(VE.after(s).tensor_scalar(turns, angf, math.pi, -2 * math.pi, ALU.is_gt, ALU.mult))
        s = VE.step(VE.after(s).tensor_tensor(angf, angf, turns, ALU.add))
        s = VE.step(VE.after(s).tensor_scalar(turns, angf, -math.pi, 2 * math.pi, ALU.is_lt, ALU.mult))
        s = VE.step(VE.after(s).tensor_tensor(angf, angf, turns, ALU.add))
    s = VE.step(VE.after(s).tensor_scalar(angf, angf, 3.1415925, -3.1415925, ALU.min, ALU.max))
    for c in range(AHEAD):
        round_piece(0, c)
    AC.step(AC.after(s).activation(extra[:, 1872:1920], angf, ACT.Sin))
    dve.memset(eps, EPS)
    for queue in (PE, AC, VE):
        queue.engine.wait_ge(s_const, 32)
    act.sem_inc(s_used, 1)
    end_layer()

    z1 = big[:, 0:6144].rearrange("p (m c) -> p m c", m=MT)
    post = [big[:, 6144 + 1024 * i:7168 + 1024 * i] for i in range(3)]
    band = big[:, 9216:10752].rearrange("p (h k) -> p h k", h=NA)
    alibi = special[:, 0:1024].rearrange("p (h k) -> p h k", h=NB)
    lam_in = special[:, 1056:1056 + 128].rearrange("p (i k) -> p i k", i=4)
    lam_c = special[:, 1184:1186]
    subln = special[:, 1216:1280]
    lam_t = special[:, 1280:1312]
    ob = special[:, 1536:2048]
    ob2 = special[:, 2048:2560]
    lb = [special[:, 2560 + 384 * i:2944 + 384 * i] for i in range(2)]
    lams = cell(8)
    c_ratio = [cell(2), cell(2)]
    r0 = cell(8)
    ob_s, ob_t, ob_y = cell(8), cell(8), cell(8)

    with nc.Fori(0, L, engines=three) as layer:
        first = layer * PIECES1
        exp_and_ln()
        for queue in (AC, VE):
            queue.engine.wait_ge(s_pre, layer * 16 + 16)

        parts = to_features(x, pre1[:, 0, :], h_hi, h_lo, (2, 3, 4, 5), ((), ()))
        AC.after(row_scale(x, work_sq, x_cells))
        load(special[:, 0:1024], T["special1"])
        load(lam_in, T["lams"][layer].partition_broadcast(P))
        load(lam_c, T["lam_const"][layer].partition_broadcast(P))
        load(subln, T["subln"][layer].partition_broadcast(P))
        for i in range(3):
            load(post[i], T["post1"][layer, i].partition_broadcast(P))
        load(band, T["band"][layer])

        def scale_gains():
            dve.wait_ge(s_par, 16 * loads[0])
            for i, weight in enumerate((0.5, 1.0, 0.5)):
                post_ready = VE.step(dve.tensor_scalar(post[i], post[i], weight / -2, None, ALU.mult))
            VE.after(post_ready)

        done = feed_forward(first, 0, FFN_STRIPS, True, 0, parts, scale, lambda m, end: add_norm(post[0], 4, m, end),
                            scale_gains)

        parts = to_features(x, pre1[:, 1, :], h_hi, h_lo, (2, 3, 4, 5), done)
        x_scale = row_scale(x, work_sq, x_cells, *done[1])
        s = VE.step(dve.tensor_scalar(band, band, -1.0, None, ALU.mult))
        band_ready = VE.step(VE.after(s).memset(band[0:64, :, 192:256], BIG))
        for i in range(2):
            s = VE.step(VE.after(s).tensor_tensor_reduce(lam_t, lam_in[:, 2 * i, :], lam_in[:, 2 * i + 1, :], 1.0,
                                                 0.0, ALU.mult, ALU.add, lams[:, i:i + 1]))
        s = AC.step(AC.after(s).activation(lams[:, 2:4], lams[:, 0:2], ACT.Exp))
        s = VE.step(VE.after(s).tensor_tensor(lams[:, 4:5], lams[:, 3:4], lams[:, 2:3], ALU.subtract))
        lam_ready = VE.step(VE.after(s).tensor_tensor(lams[:, 5:6], lams[:, 4:5], lam_c[:, 0:1], ALU.subtract))
        minus_lam = lams[:, 5:6]
        gain_ready = VE.step(dve.tensor_scalar(subln, subln, lam_c[:, 1:2], None, ALU.mult))

        done = {}


        def diff_units():
            units = []
            for h in range(NB):
                for m in range(MT):
                    def score(slot, _, h=h, m=m):
                        keys = (m + 1) * P
                        prods, segs = [], []
                        for j in range(2):
                            rows_ = slice(32 * (2 * (h % 2) + j), 32 * (2 * (h % 2) + j) + 32)
                            prods.append((qT[rows_, h // 2, m * P:m * P + P], kT[rows_, h // 2, 0:keys],
                                          j * S, keys))
                            segs.append((j * S, keys))
                        table = alibi[:, h, (1 - m) * P:(1 - m) * P + keys]
                        return softmax_parts(slot, prods, (diff_qk[0],), [table] * 2, segs, True)

                    def finish(slot, s, h=h, m=m):
                        keys = (m + 1) * P
                        total, inverse = stat[slot][1:3]
                        r = VE.step(VE.after(s).reciprocal(inverse[:, 0:2], total[:, 0:2]))
                        c1 = VE.step(VE.after(r, lam_ready).scalar_tensor_tensor(
                            c_ratio[slot][:, 0:1], total[:, 0:1], inverse[:, 1:2], minus_lam, ALU.mult, ALU.mult))
                        VE.step(VE.after(r).tensor_copy(r0[:, 4 * m + h:4 * m + h + 1], inverse[:, 0:1]))
                        prob = soft[:, slot, 0, :]
                        return VE.step(VE.after(c1).scalar_tensor_tensor(
                            prob[:, 0:keys], prob[:, S:S + keys], c_ratio[slot][:, 0:1], prob[:, 0:keys],
                            ALU.mult, ALU.add))

                    def turn(slot, s, m=m):
                        return turn_blocks(slot, s, [P * i for i in range(m + 1)])

                    def out(slot, s, h=h, m=m):
                        pe_ = PE.after(s, done[1], *bank_read[OUT])
                        for i in range(m + 1):
                            t = pe_.matmul(psum[:, OUT, (4 * m + h) * 64:(4 * m + h) * 64 + 64],
                                           soft[:, slot, 1, i * P:i * P + P],
                                           z1[:, i, QKV_B + 512 + 64 * h:QKV_B + 576 + 64 * h],
                                           start=i == 0, stop=i == m, skip_group_check=True)
                        t = PE.step(t)
                        pt_read[slot] = (t,)
                        last_out[0] = t

                    units.append((score, finish, turn, None, out))
            return units

        last_out, diff_qk, y_done = [None], [None], {}

        def diff():
            diff_qk[0] = turn_qk(z1, [(QKV_B + 128 * i, qT[:, i, :], -32.0 ** -0.5) for i in range(2)]
                                 + [(QKV_B + 256 + 128 * i, kT[:, i, :], 1.0) for i in range(2)],
                                 (done[0],))
            yield
            yield from pipeline(diff_units())
            o3 = ob.rearrange("p (g d) -> p g d", d=64)
            q3 = ob2.rearrange("p (g d) -> p g d", d=64)
            s = VE.step(VE.after(last_out[0]).tensor_tensor(
                o3, psum[:, OUT, :].rearrange("p (g d) -> p g d", d=64), r0.unsqueeze(2).broadcast_to((P, 8, 64)),
                ALU.mult))
            bank_read[OUT] = (s,)
            s = VE.step(VE.after(s).tensor_tensor(q3, o3, o3, ALU.mult))
            s = VE.step(VE.after(s).tensor_reduce(ob_s, q3, AX.X, ALU.add))
            s = VE.step(VE.after(s).tensor_scalar(ob_s, ob_s, 1.0 / 64, EPS, ALU.mult, ALU.add))
            s = rsqrt(ob_s, ob_t, ob_y, s)
            yield
            s = VE.step(VE.after(s).tensor_tensor(o3, o3, ob_y.unsqueeze(2).broadcast_to((P, 8, 64)), ALU.mult))
            s = VE.step(VE.after(s, gain_ready).tensor_tensor(o3, o3, subln.unsqueeze(1).broadcast_to((P, 8, 64)),
                                                              ALU.mult))
            yield
            pe_ = PE.after(s, *bank_read[TURNED])
            for i in range(2):
                for m in range(MT):
                    t = pe_.transpose(psum[:, TURNED, i * S + m * P:i * S + m * P + P],
                                      ob[:, m * S + i * P:m * S + i * P + P], ident)
            t = PE.step(t)
            s = split_out(psum[:, TURNED, :], y_hi[:, 3:5, :].rearrange("p a b -> p (a b)"),
                          y_lo[:, 3:5, :].rearrange("p a b -> p (a b)"), t)
            bank_read[TURNED] = (s,)
            y_done[3] = y_done[4] = s
            yield

        def head_units(col, kind, ready):
            units = []
            for h in range(6):
                half = slice(64 * (h % 2), 64 * (h % 2) + 64)
                q, k = qT[half, h // 2, :], kT[half, h // 2, :]
                v = z1[:, :, col + 768 + 64 * h:col + 832 + 64 * h]

                def band_score(slot, _, h=h, q=q, k=k):
                    prods = [(q[:, 0:P], k[:, 0:P], 0, P), (q[:, P:S], k, P, S)]
                    return softmax_parts(slot, prods, ready, [band[:, h, P:S], band[:, h, :]], SEG)

                def band_finish(slot, s):
                    return normalised(slot, s, SEG, None)

                def band_turn(slot, s):
                    return turn_blocks(slot, s, BLOCKS)

                def stick_score(slot, _, q=q, k=k):
                    bank = SCORE[slot]
                    zt = psum[:, bank, 0:384]
                    a_ = soft[:, slot, 0, 0:384]
                    pe_ = PE.after(*ready, *score_read.get(slot, ()))
                    pe_.matmul(psum[:, bank, 0:S], k[:, 0:P], q, start=True, stop=True)
                    t = PE.step(pe_.matmul(psum[:, bank, S:384], k[:, P:S], q[:, P:S], start=True, stop=True))
                    s = AC.step(AC.after(t, *prob_read.get(slot, ())).activation(a_, zt, ACT.Abs))
                    s = AC.step(AC.after(s).activation(a_, a_, ACT.Exp, scale=-1.0))
                    return AC.step(AC.after(s).activation(a_, a_, ACT.Ln, bias=1.0))

                def stick_finish(slot, s):
                    zt, a_ = psum[:, SCORE[slot], 0:384], soft[:, slot, 0, 0:384]
                    s = VE.step(VE.after(s, *pt_read.get(slot, ())).scalar_tensor_tensor(
                        lb[slot], zt, 0.0, a_, ALU.min, ALU.subtract))
                    s = VE.step(VE.after(s).tensor_tensor(a_, lb[slot], zt, ALU.subtract))
                    score_read[slot] = (s,)
                    for c_ in (0, S):
                        s2 = VE.step(VE.after(s).tensor_tensor(a_[:, c_:c_ + P], a_[:, c_:c_ + P], strict, ALU.mult))
                    return s2

                def stick_turn(slot, s):
                    a_ = soft[:, slot, 0, 0:384]
                    pe_ = PE.after(s, *bank_read[TURNED])
                    pe_.matmul(psum[:, TURNED, 0:384], tri, a_, start=True, stop=False, skip_group_check=True)
                    t = PE.step(pe_.matmul(psum[:, TURNED, P:S], ones, a_[:, S:384], start=False, stop=True,
                                           skip_group_check=True))
                    prob_read[slot] = (t,)
                    w = soft[:, slot, 1, 0:384]
                    s = VE.step(VE.after(t, *pt_read.get(slot, ())).tensor_tensor(w, lb[slot], psum[:, TURNED, 0:384],
                                                                                  ALU.add))
                    bank_read[TURNED] = (s,)
                    return s

                def stick_late(slot, s):
                    w = soft[:, slot, 1, 0:384]
                    s = AC.step(AC.after(s).activation(w, w, ACT.Exp))
                    for c_ in (0, S):
                        s2 = VE.step(VE.after(s).tensor_tensor(w[:, c_:c_ + P], w[:, c_:c_ + P], strict, ALU.mult))
                    return s2

                def out(slot, s, h=h, v=v):
                    col_ = S * (h // 2 % 2)
                    PE.after(s, *(bank_read[OUT] if h % 2 == 0 else ()))
                    t = PE.step(causal_out(slot, 64 * (h % 2), v, col_))
                    pt_read[slot] = (t,)
                    if h % 2:
                        kt = (0 if kind == "band" else 5) + h // 2
                        s = split_out(psum[:, OUT, col_:col_ + S], y_hi[:, kt, :], y_lo[:, kt, :], t)
                        bank_read[OUT] = (s,)
                        y_done[kt] = s

                if kind == "band":
                    units.append((band_score, band_finish, band_turn, None, out))
                else:
                    units.append((stick_score, stick_finish, stick_turn, stick_late, out))
            return units

        def heads(col, kind, strips_):
            s = turn_qk(z1, [(col + 128 * i, qT[:, i, :], -0.125 if kind == "band" else 0.125) for i in range(3)]
                        + [(col + 384 + 128 * i, kT[:, i, :], 1.0) for i in range(3)],
                        [done[i] for i in strips_])
            yield
            yield from pipeline(head_units(col, kind, (s, band_ready)))

        work = []

        def between():
            while work:
                try:
                    next(work[0])
                    return
                except StopIteration:
                    work.pop(0)

        c = FFN_PIECES
        for i in range(COLS1 // 512):
            bank = 2 * (i % 2)
            PE.after(*([done[i - 2]] if i > 1 else []))
            end = strip(first, c, h_hi, h_lo, bank, between, None if i else parts)
            done[i] = take_out(z1[:, :, i * 512:i * 512 + 512], bank, end, i % 2, scale, x_scale)
            c += 4
            if i == 0:
                work.append(diff())
            if i == 3:
                work.append(heads(QKV_C, "stick", (1, 2, 3)))
            if i == 5:
                work.append(heads(QKV_A, "band", (3, 4, 5)))
            for _ in range(min(i, 2)):
                between()
        PE.after(done[4], done[5])
        for i, kt in enumerate(OUT_ORDER[:-2]):
            while kt not in y_done:
                between()
            PE.after(y_done[kt])
            rows(first, c + i, kt, y_hi, y_lo, 0, i == 0, False)
            between()
        while work:
            between()
        PE.after(*(y_done[kt] for kt in OUT_ORDER[-2:]))
        x_done = []
        end = last_rows(first, c + KD - 2, OUT_ORDER[-2], 2, y_hi, y_lo, 0,
                        lambda end: x_done.append((add_norm(post[1], 0, 0, end),)))
        x_done.append((add_norm(post[1], 0, 1, end),))
        c += KD

        parts = to_features(x, pre1[:, 2, :], h_hi, h_lo, (4, 5, 6, 7), x_done)
        s = row_scale(x, work_sq, x_cells, *x_done[1])
        AC.after(s)
        VE.after(s)
        AC.after(parts[-1])
        load(pre1, T["pre1"][layer + 1], s_pre)
        feed_forward(first, c, FFN_STRIPS, True, FFN_STRIPS, parts, scale, lambda m, end: add_norm(post[2], 4, m, end))
        assert c + FFN_PIECES == PIECES1
        end_layer()

    masks = special[:, 0:1024].rearrange("p (i q) -> p i q", i=8)
    b_merge = special[:, 1024:4096]
    gain12 = special[:, 4096:4864]
    gla_gain = special[:, 4864:4865]
    w2 = special[:, 4992:5248].rearrange("p (k e d) -> p k e d", k=2, e=2)
    w_gate = special[0:16, 5248:5504]
    pe_rows = special[:, 5504:5536].rearrange("p (k j) -> p k j", k=2)
    b_gate = special[:, 5560:5562]
    mem_gain = special[:, 5568:5570]
    cmp_gain = special[0:32, 5824:5888]

    znq = big[:, 0:2048].rearrange("p (m c) -> p m c", m=MT)
    z3 = big[:, 2048:2640].rearrange("p (m c) -> p m c", m=MT)
    gqk = big[:, 2640:3664].rearrange("p (m c) -> p m c", m=MT)
    gv = big[:, 3664:4688].rearrange("p (m c) -> p m c", m=MT)
    gr = big[:, 4688:5712].rearrange("p (m c) -> p m c", m=MT)
    mq = big[:, 5712:6736].rearrange("p (m c) -> p m c", m=MT)
    merge = big[:, 6736:12880].rearrange("p (m c) -> p m c", m=MT)
    windows = [[big[:, 6736 + 512 * kv:7248 + 512 * kv]]
               + [w[:, 2 * kv:2 * kv + 2, :].rearrange("p a b -> p (a b)") for w in (y_hi, y_lo)] for kv in range(2)]
    doubled = big[:, 8784:9808]
    decays = merge[:, :, 2 * D:3 * D].rearrange("p m (l t) -> p m l t", l=4)
    merged = merge[:, :, 2 * D:3 * D]
    softf = soft[:, :, :, :].rearrange("p a b c -> p (a b c)")

    vb = extra[:, 0:512]
    hid_rep = extra[:, 896:1152].rearrange("p (e c) -> p e c", e=2)
    kb = extra[0:32, 1152:1280]
    kbd = extra[:, 1280:1312]
    pc = extra[:, 1312:1568]
    pct = extra[:, 1568:1824]
    hid_rows = extra[0:32, 0:512]
    att = [pc[:, 0:128], pc[:, 128:256]]
    att_off = pct[:, 0:128]
    gates = extra[:, 1824:1872].rearrange("p (m c) -> p m c", m=MT)
    glow = extra[0:16, 512:768]
    kcn = extra[0:32, 1920:1984]
    tmp32 = extra[0:32, 1984:2048]
    mn16, sum16, inv16 = cell(16), cell(16), cell(16)
    s24, t24, y24 = cell(24), cell(24), cell(24)
    s8, t8, y8 = cell(8), cell(8), cell(8)
    m_cells = (cell(2), cell(2), cell(2))
    k8, kt8, ky8 = cell(8), cell(8), cell(8)
    c1_, c2_, c3_ = cell(1), cell(1), cell(1)


    def rotate(q4, cos, sin, tmps, s):
        x1, x2 = q4[..., 0:8], q4[..., 8:16]
        for tmp, a_, b_ in ((tmps[0], x1, cos), (tmps[1], x2, sin), (tmps[2], x2, cos), (tmps[3], x1, sin)):
            s2 = VE.step(VE.after(s).tensor_tensor(tmp, a_, b_, ALU.mult))
        s = VE.step(VE.after(s2).tensor_tensor(x1, tmps[0], tmps[1], ALU.subtract))
        return VE.step(VE.after(s).tensor_tensor(x2, tmps[2], tmps[3], ALU.add))

    act.wait_ge(s_pre, 16 * (L + 1))
    load(special[:, 0:1024], T["masks"], s_masks)
    load_mem()
    with nc.Fori(0, L, engines=three) as layer:
        first = layer * PIECES2 + L * PIECES1
        exp_and_ln()
        for queue in (AC, VE):
            queue.engine.wait_ge(s_pre2, layer * 16 + 16)

        c = 0
        parts = to_features(x, pre2[:, 0, :], h_hi, h_lo, (4, 5, 6, 7), ((), ()))
        x_scale = row_scale(x, work_sq, x_cells)
        for target, name in ((w2, "w2"), (w_gate, "w_gate"), (pe_rows, "pe"), (b_gate, "b_gate")):
            load(target, T[name][layer])
        load(gla_gain, T["gla_gain"][layer].rearrange("(p o) -> p o", o=1))
        load(mem_gain, T["mem_gain"][layer])
        for target, name in ((b_merge, "b_merge"), (gain12, "gain12")):
            load(target, T[name][layer].partition_broadcast(P))
        load(cmp_gain, T["cmp_gain"][layer].partition_broadcast(32))
        y_done = {b: [] for b in range(3)}
        got = {}

        def mem_attention():
            for m in range(MT):
                for h in range(4):
                    s = AC.step(AC.after(got["mq"]).activation(
                        merge[:, m, D + P * h:D + P * h + P], mq[:, m, P * h:P * h + P], ACT.Square,
                        accum_out=s8[:, 4 * m + h:4 * m + h + 1]))
            s = VE.step(VE.after(s).tensor_scalar(s8, s8, 1.0 / P, EPS, ALU.mult, ALU.add))
            q_scale = rsqrt(s8, t8, y8, s)
            yield
            for m in range(MT):
                for h in range(4):
                    s = AC.step(AC.after(got["mk"]).activation(
                        merge[:, m, D + 512 + P * h:D + 640 + P * h], memkv[:, m, P * h:P * h + P],
                        ACT.Square, accum_out=k8[:, 4 * m + h:4 * m + h + 1]))
            s = VE.step(VE.after(s).tensor_scalar(k8, k8, 1.0 / P, EPS, ALU.mult, ALU.add))
            s = rsqrt(k8, kt8, ky8, s)
            k3 = memkv[:, :, 0:512].rearrange("p m (h d) -> p m h d", h=4)
            yield
            for m in range(MT):
                k_s = VE.step(VE.after(s).tensor_tensor(k3[:, m], k3[:, m],
                                                        ky8[:, 4 * m:4 * m + 4].unsqueeze(2).broadcast_to((P, 4, P)),
                                                        ALU.mult))
            yield
            s = turn_qk(mq, [(P * h, qT[:, h, :], mem_gain[:, 0:1]) for h in range(4)], (got["mq"], gain_ready))
            yield
            s = turn_qk(memkv, [(P * h, kT[:, h, :], mem_gain[:, 1:2]) for h in range(4)], (k_s,))
            yield
            segs = [(0, S), (S, S)]
            units = []
            for h in range(4):
                def score(slot, _, h=h, s=s):
                    prods = [(qT[:, h, m * P:m * P + P], kT[:, h, n * P:n * P + P], m * S + n * P, P)
                             for m in range(MT) for n in range(2)]
                    return softmax_parts(slot, prods, (s, q_scale), [y8[:, 4 * m + h:4 * m + h + 1] for m in range(MT)],
                                         segs, scales=True)

                def turn(slot, s):
                    return turn_blocks(slot, s, [0, S, P, S + P])

                def out(slot, s, h=h):
                    pe_ = PE.after(s, *bank_read[OUT])
                    for k in range(2):
                        t = pe_.matmul(psum[:, OUT, 0:S], memkv[:, k, 512 + P * h:640 + P * h],
                                       soft[:, slot, 1, k * S:k * S + S], start=k == 0, stop=k == 1)
                    t = PE.step(t)
                    pt_read[slot] = (t,)
                    s = split_out(psum[:, OUT, 0:S], y_hi[:, 8 + h, :], y_lo[:, 8 + h, :], t)
                    bank_read[OUT] = (s,)
                    y_done[2].append(s)

                units.append((score, lambda slot, s: normalised(slot, s, segs, None), turn, None, out))
            PE.after(got["mv"])
            yield from pipeline(units)

        def idle_now():
            return [r for reads in (prob_read, pt_read) for v_ in reads.values() for r in v_]

        def nsa_prep():
            idle = idle_now()
            sq = softf[:, 0:1536]
            z4 = znq[:, :, 0:768]
            s = got["nq"]
            ready = (s, got["nk"], gain_ready, *idle)
            for m in range(MT):
                a = AC.step(AC.after(*ready).activation(sq[:, m * 768:m * 768 + 768], z4[:, m, :], ACT.Square))
            s = VE.step(VE.after(a, *ready).tensor_reduce(s24, sq.rearrange("p (g d) -> p g d", d=64), AX.X, ALU.add))
            s = VE.step(VE.after(s).tensor_scalar(s24, s24, 1.0 / 64, EPS, ALU.mult, ALU.add))
            s = rsqrt(s24, t24, y24, s)
            yield
            for m in range(MT):
                v3 = z4[:, m, :].rearrange("p (h d) -> p h d", d=64)
                s2 = VE.step(VE.after(s).tensor_tensor(
                    v3, v3, y24[:, 12 * m:12 * m + 12].unsqueeze(2).broadcast_to((P, 12, 64)), ALU.mult))
            for m in range(MT):
                s = VE.step(VE.after(s2).tensor_tensor(z4[:, m, :], z4[:, m, :], gain12, ALU.mult))
            yield
            for m in range(MT):
                q4 = z4[:, m, :].rearrange("p (h d) -> p h d", d=64)
                cos, sin = (trig[:, f, m, :].unsqueeze(1).broadcast_to((P, 12, 8)) for f in range(2))
                tmps = [softf[:, 96 * i:96 * i + 96].rearrange("p (h d) -> p h d", h=12) for i in range(4)]
                s = rotate(q4, cos, sin, tmps, s)
            got["nsa"] = s
            yield
        def make_windows():
            d6 = doubled.rearrange("p (m k g r d) -> p m k g r d", m=MT, k=2, g=2, r=2)
            src = znq[:, :, 768:1024].rearrange("p m (k g d) -> p m k g d", k=2, g=2)
            for m in range(MT):
                for k in range(2):
                    for r in range(2):
                        s = VE.step(VE.after(got["nk"]).tensor_copy(d6[:, m, k, :, r, :], src[:, m, k]))
            got["doubled"] = s
            yield
            for kv in range(2):
                got["windows"] = windows_of(kv)
                yield
            windows_made.append(True)

        def windows_of(kv):
            bank = SCORE[kv]
            pe_ = PE.after(got["doubled"], *score_read.get(kv, ()))
            for g in range(2):
                for m in range(MT):
                    col = ((m * 2 + kv) * 2 + g) * 128
                    t = pe_.transpose(psum[:, bank, g * S + m * P:g * S + m * P + P], doubled[:, col:col + 128], ident)
            t = PE.step(t)
            rows_, high, low = windows[kv]
            whole = rows_.rearrange("p (j g n) -> p j g n", j=16, g=2)
            z_ = VE.step(VE.after(t).memset(rows_, 0.0))
            for g in range(2):
                ps4 = psum[:, bank, g * S:g * S + S].rearrange("p (n j r) -> p r j n", j=8, r=2)
                for par in range(2):
                    for half in range(2):
                        pr = slice(64 * par, 64 * par + 64)
                        src = ps4[pr, par, :, half:half + 15]
                        a = VE.step(VE.after(z_).tensor_tensor(
                            whole[pr, 8 * half:8 * half + 8, g, 0:15], src,
                            pe_rows[pr, kv, 8 * half:8 * half + 8].unsqueeze(2).broadcast_to((64, 8, 15)), ALU.add))
            score_read[kv] = (a,)
            h_ = AC.step(AC.after(a).activation(high, rows_, ACT.Copy))
            return VE.step(VE.after(h_).tensor_tensor(low, rows_, f32(high), ALU.subtract))

        def compress(bank):
            nonlocal c
            PE.after(got["windows"])
            for kv in range(2):
                w_hi, w_lo = (w.rearrange("p (j n) -> p j n", j=16) for w in windows[kv][1:])
                for i in range(4):
                    slot = next_piece(first, c)
                    for jj in range(4):
                        j, cols = 4 * i + jj, slice(jj * 256, jj * 256 + 256)
                        last = product(psum[0:32, bank, kv * 256:kv * 256 + 256], w_hi[:, j, :], w_lo[:, j, :],
                                       hi[:, slot, cols], lo[:, slot, cols], j == 0, j == 15)
                    last.then_inc(s_used, 1)
                    c += 1
                    between()
                    if i == 3:
                        between()
            end = At(s_used, first + (c + 1))
            got["hid_rows"] = VE.step(VE.after(end).tensor_copy(hid_rows, psum[0:32, bank, :]))
            return got["hid_rows"]

        def hidden():
            h_, a_, b_ = hid
            pe_ = PE.after(got["hid_rows"], *bank_read[TURNED])
            for i in range(4):
                t = pe_.transpose(psum[:, TURNED, 32 * i:32 * i + 32], hid_rows[:, i * P:i * P + P], ident[0:32, 0:32])
            t = PE.step(t)
            s = VE.step(VE.after(t).tensor_copy(h_, psum[:, TURNED, 0:128]))
            bank_read[TURNED] = (s,)
            s = VE.step(VE.after(s).tensor_tensor(a_, h_, h_, ALU.mult))
            s = VE.step(VE.after(s).tensor_scalar(a_, a_, 0.044715, 1.0, ALU.mult, ALU.add))
            s = VE.step(VE.after(s).tensor_tensor(a_, a_, h_, ALU.mult))
            s = VE.step(VE.after(s).tensor_scalar(a_, a_, -50.0, None, ALU.max))
            s = AC.step(AC.after(s).activation(a_, a_, ACT.Exp, scale=-2.0 * math.sqrt(2.0 / math.pi)))
            s = VE.step(VE.after(s).tensor_scalar(a_, a_, 1.0, None, ALU.add))
            s = VE.step(VE.after(s).reciprocal(b_, a_))
            got["hid"] = VE.step(VE.after(s).tensor_tensor(h_, h_, b_, ALU.mult))

        def nsa():
            hidden()
            yield
            h4 = hid[0].rearrange("p (k e n) -> p k e n", k=2, e=2)
            pe_ = PE.after(got["hid"], *bank_read[TURNED])
            for e in range(2):
                t = pe_.matmul(psum[0:32, TURNED, 0:64], h4[:, 0, e, :], w2[:, 0, e, :], start=e == 0, stop=e == 1)
            t = PE.step(t)
            s = VE.step(VE.after(t).tensor_copy(kcn, psum[0:32, TURNED, 0:64]))
            s = VE.step(VE.after(s).tensor_tensor_reduce(tmp32, kcn, kcn, 1.0, 0.0, ALU.mult, ALU.add, c1_[0:32, :]))
            s = VE.step(VE.after(s).tensor_scalar(c1_[0:32, :], c1_[0:32, :], 1.0 / 64, EPS, ALU.mult, ALU.add))
            s = rsqrt(c1_[0:32, :], c2_[0:32, :], c3_[0:32, :], s)
            s = VE.step(VE.after(s).scalar_tensor_tensor(kcn, kcn, c3_[0:32, 0:1], cmp_gain, ALU.mult, ALU.mult))
            s = rotate(kcn, trig[0:32, 0, 2, :], trig[0:32, 1, 2, :], [tmp32[:, 8 * i:8 * i + 8] for i in range(4)],
                       s)
            kbs = VE.step(VE.after(s).tensor_tensor(
                kb.rearrange("p (g d) -> p g d", g=2), kcn.unsqueeze(1).broadcast_to((32, 2, 64)),
                own_keys.unsqueeze(2).broadcast_to((32, 2, 64)), ALU.mult))
            r_ = VE.step(VE.after(got["hid"]).tensor_copy(
                hid_rep.rearrange("p e (j n) -> p e j n", j=4),
                h4[:, 1].unsqueeze(2).broadcast_to((P, 2, 4, 32))))
            yield
            pe_ = PE.after(kbs, r_)
            pe_.transpose(psum[:, TURNED, 64:96], kb, ident[0:32, 0:32])
            for e in range(2):
                t = pe_.matmul(psum[:, SCORE[0], 0:64], hid_rep[:, e, :], w2[:, 1, e, :], start=e == 0, stop=e == 1)
            t = PE.step(t)
            s = VE.step(VE.after(t).tensor_copy(kbd, psum[:, TURNED, 64:96]))
            bank_read[TURNED] = (s,)
            s = VE.step(VE.after(t).tensor_copy(tmp_v, psum[:, SCORE[0], 0:64]))
            score_read[0] = (s,)
            s = VE.step(VE.after(s).tensor_tensor(
                vb.rearrange("p (h d) -> p h d", h=8), tmp_v.unsqueeze(1).broadcast_to((P, 8, 64)),
                own_values.unsqueeze(2).broadcast_to((P, 8, 64)), ALU.mult))
            s = VE.step(VE.after(got["z3"]).tensor_scalar(gates, z3[:, :, 256:280], -80.0, None, ALU.max))
            s = AC.step(AC.after(s).activation(gates, gates, ACT.Exp, scale=-1.0))
            s = VE.step(VE.after(s).tensor_scalar(gates, gates, 1.0, None, ALU.add))
            s = VE.step(VE.after(s).reciprocal(gates, gates))
            gates_ready = s
            yield
            sk = turn_qk(znq, [(512, kT[:, 0, :], 1.0), (640, kT[:, 1, :], 1.0)]
                         + [(P * j, qT[:, j, :], 1.0) for j in range(4)], (got["nsa"],))
            yield
            units = []

            def cmp_score(slot, _):
                bank = SCORE[slot]
                pe_ = PE.after(sk, s_vb[0], *score_read.get(slot, ()))
                for m in range(MT):
                    for j in range(4):
                        t = pe_.matmul(psum[:, bank, m * P + 32 * j:m * P + 32 * j + 32], qT[:, j, m * P:m * P + P],
                                       kbd, start=True, stop=True, skip_group_check=True)
                t = PE.step(t)
                g3 = lambda a, m: a[:, m * P:m * P + P].rearrange("p (h n) -> p h n", n=16)
                tab = lambda a, m: a[:, m, :].unsqueeze(1).broadcast_to((P, 8, 16))
                for m in range(MT):
                    s = VE.step(VE.after(t).tensor_tensor(g3(pc, m), g3(psum[:, bank, :], m), tab(cmp_table, m),
                                                          ALU.add))
                score_read[slot] = (s,)
                all3 = pc.rearrange("p (h n) -> p h n", n=16)
                s = VE.step(VE.after(s).tensor_reduce(mn16, all3, AX.X, ALU.min))
                s = VE.step(VE.after(s).tensor_tensor(all3, all3, mn16.unsqueeze(2).broadcast_to((P, 16, 16)),
                                                      ALU.subtract))
                s = AC.step(AC.after(s).activation(pc, pc, ACT.Exp, scale=-1.0))
                for m in range(MT):
                    s2 = VE.step(VE.after(s).tensor_tensor(g3(pc, m), g3(pc, m), tab(cmp_valid, m), ALU.mult))
                s = VE.step(VE.after(s2).tensor_reduce(sum16, all3, AX.X, ALU.add))
                s = VE.step(VE.after(s).tensor_scalar(sum16, sum16, 1e-30, None, ALU.max))
                s = VE.step(VE.after(s).reciprocal(inv16, sum16))
                s = VE.step(VE.after(s, gates_ready).tensor_tensor(
                    inv16.rearrange("p (m h) -> p m h", m=MT), inv16.rearrange("p (m h) -> p m h", m=MT),
                    gates[:, :, 0:8], ALU.mult))
                return VE.step(VE.after(s).tensor_tensor(all3, all3, inv16.unsqueeze(2).broadcast_to((P, 16, 16)),
                                                         ALU.mult))

            def cmp_turn(slot, s):
                pe_ = PE.after(s, *bank_read[TURNED])
                for m in range(MT):
                    t = pe_.transpose(psum[:, TURNED, m * P:m * P + P], pc[:, m * P:m * P + P], ident)
                t = PE.step(t)
                s = VE.step(VE.after(t).tensor_copy(pct, psum[:, TURNED, 0:S]))
                bank_read[TURNED] = (s,)
                got["pct"] = s
                return s

            s_vb = [(VE, VE.n)]
            units.append((cmp_score, None, cmp_turn, None, None))
            for j in range(4):
                for b in range(2):
                    for g in range(2):
                        half = slice(64 * g, 64 * g + 64)

                        def score(slot, _, j=j, b=b, g=g, half=half):
                            q, k = qT[half, j, :], kT[half, b, :]
                            prods = [(q[:, 0:P], k[:, 0:P], 0, P), (q[:, P:S], k, P, S)]
                            return softmax_parts(slot, prods, (sk,), [causal[:, P:S], causal], SEG)

                        def finish(slot, s, j=j, b=b, g=g):
                            VE.after(gates_ready)
                            at = (1 + b) * 8 + 2 * j + g
                            return normalised(slot, s, SEG, [gates[:, m, at:at + 1] for m in range(MT)])

                        def out(slot, s, j=j, b=b, g=g):
                            col = S * (j % 2)
                            if b == 0 and g == 0:
                                PE.after(got["pct"], *bank_read[OUT]).matmul(
                                    psum[:, OUT, col:col + S], vb[:, j * P:j * P + P], pct, start=True, stop=False,
                                    skip_group_check=True)
                            PE.after(s)
                            v = z3[:, :, b * P + 64 * g:b * P + 64 * g + 64]
                            t = PE.step(causal_out(slot, 64 * g, v, col, False, True))
                            pt_read[slot] = (t,)
                            if b == 1 and g == 1:
                                s = split_out(psum[:, OUT, col:col + S], y_hi[:, j, :], y_lo[:, j, :], t)
                                bank_read[OUT] = (s,)
                                y_done[0].append(s)

                        units.append((score, finish, lambda slot, s: turn_blocks(slot, s, BLOCKS), None, out))
            yield from pipeline(units)

        tmp_v = hid[1][:, 0:64]

        def gla():
            dve.wait_ge(s_masks, 16)
            s = turn_qk(gqk, [(P * i, qT[:, i, :], 0.125) for i in range(2)]
                        + [(256 + P * i, kT[:, i, :], 1.0) for i in range(2)], (got["gqk"],))
            pe_ = PE.after(*bank_read[TURNED])
            for m in range(MT):
                t = pe_.transpose(psum[0:16, TURNED, m * P:m * P + P], z3[:, m, 280:296], ident)
            t = PE.step(t)
            qk = s
            s = VE.step(VE.after(t).tensor_copy(glow, psum[0:16, TURNED, 0:S]))
            bank_read[TURNED] = (s,)
            yield
            pe_ = PE.after(s, *score_read.get(0, ()))
            for i in range(2):
                t = pe_.matmul(psum[:, SCORE[0], i * S:i * S + S], w_gate[:, i * P:i * P + P], glow, start=True,
                               stop=True, skip_group_check=True)
            t = PE.step(t)
            zt, ab = qT[:, 2:4, :], kT[:, 2:4, :]
            idle = idle_now()
            for i in range(2):
                s = VE.step(VE.after(t).tensor_scalar(zt[:, i, :], psum[:, SCORE[0], i * S:i * S + S],
                                                      b_gate[:, i:i + 1], None, ALU.add))
            score_read[0] = (s,)
            s = AC.step(AC.after(s).activation(ab, zt, ACT.Abs))
            s = AC.step(AC.after(s).activation(ab, ab, ACT.Exp, scale=-1.0))
            s = AC.step(AC.after(s).activation(ab, ab, ACT.Ln, bias=1.0))
            s = VE.step(VE.after(s).scalar_tensor_tensor(zt, zt, 0.0, ab, ALU.min, ALU.subtract))
            for i in range(2):
                s2 = VE.step(VE.after(s, *idle).tensor_tensor_scan(ab[:, i, :], consts[:, 256:512], zt[:, i, :], 0.0,
                                                                   ALU.mult, ALU.add))
            csum, s_sum = ab, s2
            yield
            e_buf = decays
            q_buf = memkv[:, :, :].rearrange("p m c -> p (m c)").rearrange("p (l t) -> p l t", l=8)
            off_read = [None]
            og = gqk.rearrange("p m (h d) -> p m h d", h=4)
            o_last = [qk]
            for hp in range(2):
                read = (PE, PE.n)
                qb, kb_ = (a[:, hp, :].unsqueeze(1).broadcast_to((P, 4, S)) for a in (qT, kT))
                decayed = []
                for part in range(2):
                    for i in range(4):
                        half = LEVELS[4 * part + i]
                        b3 = csum[:, hp, :].rearrange("p (n t) -> p n t", t=2 * half)
                        ref = b3[:, :, half - 1:half].broadcast_to((P, S // (2 * half), 2 * half))
                        s = VE.step(VE.after(s_sum, read).tensor_tensor(
                            e_buf[:, part, i, :].rearrange("p (n t) -> p n t", t=2 * half), b3, ref, ALU.subtract))
                    yield
                    e_ = e_buf[:, part]
                    s = AC.step(AC.after(s).activation(e_, e_, ACT.Abs))
                    decayed.append(AC.step(AC.after(s).activation(e_, e_, ACT.Exp, scale=-1.0 / 16)))
                for part in range(2):
                    e_ = e_buf[:, part]
                    s2 = VE.step(VE.after(decayed[part], qk).tensor_tensor(q_buf[:, 4 * part:4 * part + 4], e_, qb,
                                                                          ALU.mult))
                    ready = VE.step(VE.after(s2).tensor_tensor(e_, e_, kb_, ALU.mult))
                    yield
                units = []
                for hh in range(2):
                    for m in range(MT):
                        half_ = slice(64 * hh, 64 * hh + 64)
                        h = 2 * hp + hh

                        def score(slot, _, m=m, half_=half_, h=h, hp=hp, ready=ready):
                            toks = slice(m * P, m * P + P)
                            pe_ = PE.after(ready, *score_read.get(0, ()), *score_read.get(1, ()))
                            for i in range(8):
                                l = i + 1
                                lhsT, rhs = ((e_buf[half_, l // 4, l % 4, toks], q_buf[half_, l, toks]) if i < 7
                                             else (kT[half_, hp, toks], qT[half_, hp, toks]))
                                t = pe_.matmul(psum[:, SCORE[i // 4], (i % 4) * P:(i % 4) * P + P], lhsT, rhs,
                                               start=True, stop=True, skip_group_check=True)
                            if m:
                                t = PE.after(*bank_read[TURNED]).matmul(
                                    psum[:, TURNED, 0:P], e_buf[half_, 0, 0, 0:P], q_buf[half_, 0, P:S], start=True,
                                    stop=True)
                            t = PE.step(t)
                            prod = soft[:, slot, :, :].rearrange("p a b -> p (a b)")
                            s = VE.step(VE.after(t).tensor_tensor(
                                prod.rearrange("p (i q) -> p i q", i=8),
                                psum[:, 4:6, :].rearrange("p a (i q) -> p (a i) q", i=4), masks, ALU.mult))
                            score_read[0] = score_read[1] = (s,)
                            s = VE.step(VE.after(s, *prob_read.get(slot, ())).tensor_reduce(
                                att[slot], prod.rearrange("p (i q) -> p q i", i=8), AX.X, ALU.add))
                            if m:
                                s = VE.step(VE.after(s, off_read[0]).tensor_copy(att_off, psum[:, TURNED, 0:P])
                                            if off_read[0] else
                                            VE.after(s).tensor_copy(att_off, psum[:, TURNED, 0:P]))
                                bank_read[TURNED] = (s,)
                            return s

                        def turn(slot, s, m=m, h=h):
                            pe_ = PE.after(s, got["gv"], *bank_read[OUT])
                            o = psum[:, OUT, 0:P]
                            t = pe_.matmul(o, att[slot], gv[:, m, h * P:h * P + P], start=True, stop=not m)
                            if m:
                                t = pe_.matmul(o, att_off, gv[:, 0, h * P:h * P + P], start=False, stop=True)
                            t = PE.step(t)
                            if m:
                                off_read[0] = t
                            prob_read[slot] = (t,)
                            s = VE.step(VE.after(t, qk).tensor_copy(og[:, m, h, :], o))
                            bank_read[OUT] = (s,)
                            o_last[0] = s
                            return s

                        units.append((score, None, turn, None, None))
                yield from pipeline(units)
            gla_done.append(True)
            f3, r3 = (a.rearrange("p m (h d) -> p (m h) d", h=4) for a in (gqk, gr))
            for i in range(8):
                s = AC.step(AC.after(o_last[0], *idle_now()).activation(softf[:, P * i:P * i + P], f3[:, i, :],
                                                                        ACT.Square, accum_out=s8[:, i:i + 1]))
            s = VE.step(VE.after(s).tensor_scalar(s8, s8, 1.0 / P, EPS, ALU.mult, ALU.add))
            s = rsqrt(s8, t8, y8, s)
            yield
            for i in range(8):
                s2 = VE.step(VE.after(s, got["gr"]).scalar_tensor_tensor(f3[:, i, :], f3[:, i, :], y8[:, i:i + 1],
                                                                         r3[:, i, :], ALU.mult, ALU.mult))
            yield
            for pair in range(2):
                pe_ = PE.after(s2, *score_read.get(0, ()), *score_read.get(1, ()))
                for i in range(2):
                    for m in range(MT):
                        col = (2 * pair + i) * P
                        t = pe_.transpose(psum[:, SCORE[pair], i * S + m * P:i * S + m * P + P],
                                          gqk[:, m, col:col + P], ident)
                t = PE.step(t)
                kts = slice(4 + 2 * pair, 6 + 2 * pair)
                high, low = (a[:, kts, :].rearrange("p a b -> p (a b)") for a in (y_hi, y_lo))
                src = psum[:, SCORE[pair], :]
                s = AC.step(AC.after(t).activation(high, src, ACT.Copy, scale=gla_gain))
                s = VE.step(VE.after(s).scalar_tensor_tensor(low, src, gla_gain, f32(high), ALU.mult, ALU.subtract))
                score_read[pair] = (s,)
                y_done[1] += [s, s]
                yield

        work.clear()
        windows_made, gla_done = [], []
        mem_sq = merge[:, :, 0:D]
        names = ["nk", "mk", "mv", "nq", "mq", "gr", "z3", "gqk", "gv", "cmp"] + ["merge"] * 6
        dests = {"mq": mq, "nq": znq[:, :, 0:512], "nk": znq[:, :, 512:1024], "z3": z3, "gqk": gqk, "gv": gv,
                 "mk": memkv[:, :, 0:512], "mv": memkv[:, :, 512:1024]}
        free = {0: (), 2: ()}
        calls, memory = [], []

        def turn_memory():
            calls.append(True)
            if len(calls) < 3:
                return
            for queue in (PE, AC, VE):
                queue.engine.wait_ge(s_mem, layer * 16 + 16)
            PE.after(*parts)
            memory.append(to_features(memkv, pre2[:, 2, :], y_hi, y_lo, (4, 5, 6, 7), ((), ())))
            memory.append(row_scale(memkv, mem_sq, m_cells))

        n_merge = 0
        for i, name in enumerate(names):
            bank = 2 * (i % 2)
            PE.after(*free[bank])
            if name == "cmp":
                while not windows_made:
                    between()
                work.append(gla())
                free[bank] = (compress(bank),)
                work.append(nsa())
                continue
            if name == "merge" and n_merge == 4:
                while not gla_done:
                    between()
            if i == 1:
                mem_parts, m_scale = memory
            if name in ("mk", "mv"):
                end = strip(first, c, y_hi, y_lo, bank, between, mem_parts if name == "mk" else None)
            else:
                end = strip(first, c, h_hi, h_lo, bank, between if i else turn_memory, parts if i == 0 else None)
            c += 4
            if name == "merge":
                cols = slice(512 * n_merge, 512 * n_merge + 512)
                for m in range(MT):
                    s = VE.step(VE.after(end, x_scale).scalar_tensor_tensor(
                        merge[:, m, cols], psum[:, bank + m, :], scale[:, m:m + 1], b_merge[:, cols], ALU.mult,
                        ALU.add))
                n_merge += 1
            elif name == "gr":
                for m in range(MT):
                    s = AC.step(AC.after(end, x_scale).activation(gr[:, m, :], psum[:, bank + m, :], ACT.Silu,
                                                                  scale=scale[:, m:m + 1]))
                exp_and_ln()
            elif name in ("mk", "mv"):
                s = take_out(dests[name], bank, end, i % 2, m_cells[2], m_scale, x_scale)
            else:
                s = take_out(dests[name], bank, end, i % 2 or name == "mq", scale, x_scale)
            free[bank] = (s,)
            got[name] = s
            if name == "mk":
                for queue in (PE, VE):
                    queue.engine.wait_ge(s_par, 16 * loads[0])
                s = VE.step(dve.tensor_scalar(gain12[:, 0:512], gain12[:, 0:512], -0.125, None, ALU.mult))
                gain_ready = VE.step(VE.after(s).tensor_scalar(mem_gain[:, 0:1], mem_gain[:, 0:1], -128.0 ** -0.5, None,
                                                               ALU.mult))
            if name == "mv":
                work.append(make_windows())
            if name == "nq":
                work.append(nsa_prep())
            if name == "mq":
                work.append(mem_attention())
            between()

        merge_ready, gate_done = s, {}

        def gate(b, m):
            w = merge[:, m, b * D:b * D + D]
            gate_done[b, m] = AC.step(AC.after(merge_ready).activation(w, w, ACT.Sigmoid))

        merge_done = []

        def take_branch(b, m, end):
            f = psum[:, 2 * m:2 * m + 2, :].rearrange("p a b -> p (a b)")
            g_ = merge[:, m, b * D:b * D + D]
            s = VE.step(VE.after(end, gate_done[b, m]).tensor_tensor(g_, g_, f, ALU.mult))
            if b != 2:
                s = VE.step(VE.after(s).tensor_tensor(merged[:, m, :], merged[:, m, :], g_, ALU.add))
            merge_done.append((s,))
            return s

        PE.after(*free[0], *free[2])
        for b in (2, 1):
            while len(y_done[b]) < 4:
                between()
            PE.after(*y_done[b])
            for i in range(4):
                end = rows(first, c + i, 4 * b + i, y_hi, y_lo, 0, i == 0, i == 3)
                if b == 2 and i < 3:
                    for m in range(MT):
                        gate((2, 1, 0)[i], m)
                elif i < 3:
                    between()
            if b == 2:
                exp_and_ln()
            c += 4
            for m in range(MT):
                s = take_branch(b, m, end)
                between()
            PE.after(s)
        merge_done.clear()
        for i in range(2):
            while len(y_done[0]) <= i:
                between()
            PE.after(y_done[0][i])
            rows(first, c + i, i, y_hi, y_lo, 0, i == 0, False)
            between()
        while work:
            between()
        PE.after(*y_done[0])
        end = last_rows(first, c + 2, 2, 2, y_hi, y_lo, 0, lambda end: take_branch(0, 0, end))
        take_branch(0, 1, end)
        c += 4
        parts = to_features(merged, None, h_hi, h_lo, (4, 5, 6, 7), merge_done)
        for i in range(KD - 2):
            PE.after(parts[i // 2])
            rows(first, c + i, i, h_hi, h_lo, 0, i == 0, False)
        PE.after(parts[-1])
        x_done = []
        end = last_rows(first, c + KD - 2, KD - 2, 2, h_hi, h_lo, 0, lambda end: x_done.append((add_plain(0, 0, end),)))
        x_done.append((add_plain(0, 1, end),))
        c += KD

        parts = to_features(x, pre2[:, 1, :], h_hi, h_lo, (4, 5, 6, 7), x_done)
        s = row_scale(x, work_sq, x_cells, *x_done[1])
        AC.after(s)
        VE.after(s)
        AC.after(parts[-1])
        load(pre2, T["pre2"][layer + 1], s_pre2)
        load_mem()
        feed_forward(first, c, MLP_STRIPS, False, 0, parts, scale, lambda m, end: add_plain(4, m, end))
        assert c + MLP_STRIPS * 8 == PIECES2
        end_layer()

    act.wait_ge(s_used, PIECES)
    round_piece(0, PIECES + AHEAD)
    act.dma_start(T["out"].rearrange("b (m p) d -> p (b m) d", p=P), x[:, :, :]).then_inc(s_out, 16)
    act.wait_ge(s_out, 16)
    act.wait_ge(s_lo, STREAM)


def pieces_of(w, cols):
    K, N = w.shape
    per = PIECE // cols
    a = w.reshape(K // P // per, per, P, N // cols, cols)
    return a.transpose(3, 0, 2, 1, 4).reshape(-1, P, PIECE)


def ffn_pieces(up, down, strips, rows_per):
    u = up.reshape(strips, 4, P, PIECE)
    d = down.reshape(strips, rows_per, P, PIECE)
    out = [u[0]]
    for i in range(1, strips):
        out += [u[i], d[i - 1]]
    return np.concatenate(out + [d[-1]])


def swiglu_pieces(gate, up, down):
    both = np.concatenate([gate.reshape(D, FFN_STRIPS, 256), up.reshape(D, FFN_STRIPS, 256)], 2).reshape(D, -1)
    return ffn_pieces(pieces_of(both, 512), pieces_of(down, 1024), FFN_STRIPS, 2)


def stream_of(a):
    parts = []
    for l in range(L):
        w = a["w_in"][l]
        A, B, C = 384, 256, 384
        qa, ka, va, qb, kb, vb, qc, kc, vc = np.split(w, np.cumsum([A, A, A, B, B, B, C, C]), 1)
        w = np.concatenate([qb, kb, vb, qc, kc, vc, qa, ka, va], 1)
        parts += [swiglu_pieces(a["ffn1_w_gate"][l], a["ffn1_w_up"][l], a["ffn1_w_down"][l]),
                  pieces_of(w, 512), pieces_of(a["w_out"][l], 1024)[list(OUT_ORDER)],
                  swiglu_pieces(a["ffn2_w_gate"][l], a["ffn2_w_up"][l], a["ffn2_w_down"][l])]
    sizes = [512, 128, 128, 128, 128, 128, 128, 24, 256, 256, 512, 512, 16, 512, 3072]
    for l in range(L):
        q, kc, vc, ks, vs, kw, vw, g, gq, gk, gv, gr, gl, mq, mg = np.split(a["w_in_2"][l], np.cumsum(sizes)[:-1], 1)
        q = q.reshape(D, 2, 4, 64).transpose(0, 2, 1, 3).reshape(D, 512)
        g = g.reshape(D, 2, 4, 3).transpose(0, 3, 2, 1).reshape(D, 24)
        pad = np.zeros((D, 216), np.float32)
        before = np.concatenate([ks, kw, kc, vc, q, mq, gr, vs, vw, g, gl, pad, gq, gk, gv], 1)
        wb = a["w_branch_2"][l]
        nsa_rows = wb[0].reshape(2, 4, 64, D).transpose(1, 0, 2, 3).reshape(512, D)
        parts += [pieces_of(before[:, 0:512], 512), pieces_of(a["mem_w_kv_2"][l], 512), pieces_of(before[:, 512:], 512),
                  pieces_of(a["cmp_w1_2"][l, 0], 256), pieces_of(a["cmp_w1_2"][l, 1], 256),
                  pieces_of(mg, 512), pieces_of(wb[2], 1024), pieces_of(wb[1], 1024), pieces_of(nsa_rows, 1024),
                  pieces_of(a["w_out_2"][l], 1024),
                  ffn_pieces(pieces_of(a["w_up_2"][l], 512), pieces_of(a["w_down_2"][l], 1024), MLP_STRIPS, 4)]
    parts.append(np.zeros((STREAM - PIECES, P, PIECE), np.float32))
    out = np.concatenate(parts)
    assert out.shape[0] == STREAM, out.shape
    return out


def shape_constants():
    p, q = np.arange(P)[:, None], np.arange(P)[None, :]
    keys = np.arange(S)[None, :]
    c = np.zeros((P, 1024), np.float32)
    c[:, 0:128] = p == q
    c[:, 128:256] = p > q
    c[:, 256:512] = 1
    c[:, 512:640] = p < q
    c[:, 640:896] = np.where(keys <= P + p, 0, BIG)
    for m in range(MT):
        n = np.arange(16)[None, :]
        seen = (16 * n + 31 <= m * P + p) & (n < N_CMP)
        c[:, 896 + 16 * m:912 + 16 * m] = np.where(seen, 0, BIG)
        c[:, 928 + 16 * m:944 + 16 * m] = seen
    c[:, 960:968] = p // 16 == np.arange(8)[None, :]
    c[:32, 968:970] = p[:32] // 16 == np.arange(2)[None, :]
    c[:, 976:984] = np.power(np.float32(500000.0), -np.arange(8, dtype=np.float32) / 8)
    dist = np.abs(P + p - keys).astype(np.float32)
    late = np.where((keys // 64) > (P + p) // 64, BIG, 0).astype(np.float32)
    slopes = np.exp2(-8.0 * np.arange(1, NB + 1, dtype=np.float32) / NB)
    alibi = np.concatenate([np.float32(s) * dist + late for s in slopes], 1).astype(np.float32)
    masks = np.zeros((P, 8, P), np.float32)
    for i, half in enumerate(LEVELS[1:]):
        masks[:, i] = (p // (2 * half) == q // (2 * half)) & (p % (2 * half) < half) & (q % (2 * half) >= half)
    masks[:, 7] = p == q
    lam = [0.8 - 0.6 * math.exp(-0.3 * l) for l in range(L)]
    lam = np.array([[v, 1.0 - v] for v in lam], np.float32)
    return c, alibi, masks.reshape(P, 1024), lam


def for_next(a):
    return np.concatenate([a, a[-1:]])


def by_tile(g):
    return np.ascontiguousarray(np.swapaxes(g.reshape(g.shape[:-1] + (-1, P)), -1, -2))


def kernel(**inputs):
    import concourse.bacc as bacc
    from concourse.bass_utils import run_bass_kernel_spmd

    a = {k: np.asarray(v) for k, v in inputs.items()}
    consts, alibi, masks, lam = shape_constants()
    rel = np.clip(P - np.arange(-127, 256), -128, 128) + 128
    band = a["rel_bias"][:, :, rel]
    at = np.arange(S)[None, :] - np.arange(P)[:, None] + 127
    arrays = {
        "stream": stream_of(a), "x": a["x"], "mem": a["mem_2"], "positions": a["positions_2"].astype(np.int32),
        "consts": consts, "special1": alibi, "masks": masks, "lam_const": lam,
        "pre1": for_next(np.stack([by_tile(a[n]) for n in ("ffn1_pre_g", "mix_pre_g", "ffn2_pre_g")], 2)),
        "post1": np.stack([a[n] for n in ("ffn1_post_g", "mix_post_g", "ffn2_post_g")], 1),
        "lams": np.stack([a["diff_lambda_" + n] for n in ("q1", "k1", "q2", "k2")], 1),
        "subln": a["diff_subln_g"],
        "band": np.ascontiguousarray(band[:, :, at].transpose(0, 2, 1, 3)),
        "pre2": for_next(np.stack([by_tile(a[n]) for n in ("ln_mix_2", "ln_mlp_2", "mem_norm_2")], 2)),
        "w2": np.ascontiguousarray(a["cmp_w2_2"].reshape(L, 2, 2, P, 64).transpose(0, 3, 1, 2, 4)),
        "w_gate": a["gla_w_gate_2"],
        "pe": np.ascontiguousarray(a["cmp_pe_2"].reshape(L, 2, 16, P).transpose(0, 3, 1, 2)),
        "b_gate": by_tile(a["gla_b_gate_2"]),
        "b_merge": a["b_merge_2"].reshape(L, -1),
        "gain12": np.concatenate([np.tile(a["nsa_q_norm_2"], (1, 8)), np.tile(a["nsa_k_norm_2"][:, 1], (1, 2)),
                                  np.tile(a["nsa_k_norm_2"][:, 2], (1, 2))], 1),
        "gla_gain": a["gla_norm_2"],
        "mem_gain": np.stack([a["mem_q_norm_2"], a["mem_k_norm_2"]], 2),
        "cmp_gain": a["nsa_k_norm_2"][:, 0],
    }
    nc = bacc.Bacc("TRN2", target_bir_lowering=False, num_devices=1)
    T, feed = {}, {}
    for name, v in arrays.items():
        feed[f"in_{name}"] = np.ascontiguousarray(v)
        T[name] = nc.dram_tensor(f"in_{name}", v.shape, mybir.dt.from_np(v.dtype), kind="ExternalInput").ap()
    T["out"] = nc.dram_tensor("out", (1, S, D), F32, kind="ExternalOutput").ap()
    build(nc, T)
    return run_bass_kernel_spmd(nc, [feed], core_ids=[0]).results[0]["out"]
```
